# Optimizing a Trainium2 kernel written in Bass

```python
import jax, jax.numpy as jnp
from jax import lax
import numpy as np
import jax
import jax.numpy as jnp

D_MODEL = 1024
BATCH = 1
SEQ = 512
DEPTH = 1

CONV_WIDTH = D_MODEL
CONV_KERNEL = 31
N_RET_HEADS = 8
RET_QK_DIM = D_MODEL // N_RET_HEADS
RET_V_DIM = 2 * RET_QK_DIM
RET_QK_WIDTH = N_RET_HEADS * RET_QK_DIM
RET_V_WIDTH = N_RET_HEADS * RET_V_DIM
RET_CHUNK = 128
ROPE_BASE = 10000.0
D_FF = 2816
FFN_CONV_KERNEL = 3
LN_EPS = 1e-5
DEEPNORM_ALPHA = (2.0 * DEPTH) ** 0.25
DEEPNORM_BETA = (8.0 * DEPTH) ** -0.25
N_MOD = 6
IN_SIZES = (RET_QK_WIDTH, RET_QK_WIDTH, RET_V_WIDTH, RET_V_WIDTH,
            CONV_WIDTH, CONV_WIDTH, D_MODEL, D_MODEL)
IN_WIDTH = sum(IN_SIZES)
IN_SPLITS = tuple(int(s) for s in np.cumsum(IN_SIZES)[:-1])


def layer_norm(x, g=None, b=None):
    xf = x.astype(jnp.float32)
    mu = jnp.mean(xf, axis=-1, keepdims=True)
    var = jnp.mean(jnp.square(xf - mu), axis=-1, keepdims=True)
    y = ((xf - mu) * lax.rsqrt(var + LN_EPS)).astype(x.dtype)
    if g is not None:
        y = y * g + b
    return y

def causal_depthwise_conv(x, w, b):
    k_width, ch = w.shape
    y = lax.conv_general_dilated(
        x, w[:, None, :].astype(x.dtype), window_strides=(1,),
        padding=[(k_width - 1, 0)], dimension_numbers=("NWC", "WIO", "NWC"),
        feature_group_count=ch)
    return y + b

def rotary(x, positions):
    half = x.shape[-1] // 2
    inv_freq = ROPE_BASE ** (-jnp.arange(half, dtype=jnp.float32) / half)
    ang = positions.astype(jnp.float32)[..., None] * inv_freq
    cos = jnp.cos(ang)[:, :, None, :]
    sin = jnp.sin(ang)[:, :, None, :]
    x1, x2 = x[..., :half], x[..., half:]
    return jnp.concatenate([x1 * cos - x2 * sin, x2 * cos + x1 * sin], axis=-1)

def chunkwise_retention(q, k, v):
    bsz, seq, heads, dk = q.shape
    dv = v.shape[-1]
    n_chunks = seq // RET_CHUNK
    log_gamma = jnp.log(1.0 - 2.0 ** (-5.0 - jnp.arange(heads, dtype=jnp.float32)))
    q = q.reshape(bsz, n_chunks, RET_CHUNK, heads, dk)
    k = k.reshape(bsz, n_chunks, RET_CHUNK, heads, dk)
    v = v.reshape(bsz, n_chunks, RET_CHUNK, heads, dv)
    idx = jnp.arange(RET_CHUNK, dtype=jnp.float32)
    rel = idx[:, None] - idx[None, :]
    decay = jnp.where(rel[None] >= 0,
                      jnp.exp(log_gamma[:, None, None] * jnp.maximum(rel, 0.0)[None]),
                      0.0)
    scores = jnp.einsum("bnihd,bnjhd->bnhij", q, k) * decay
    inner = jnp.einsum("bnhij,bnjhe->bnihe", scores, v)
    zeta = jnp.exp(log_gamma[:, None] * (RET_CHUNK - 1.0 - idx)[None])
    kv = jnp.einsum("bnjhd,bnjhe->bnhde", k * zeta.T[None, None, :, :, None], v)
    chunk_decay = jnp.exp(log_gamma * RET_CHUNK)[None, :, None, None]

    def step(state, kv_c):
        return state * chunk_decay + kv_c, state

    _, r_prev = lax.scan(step, jnp.zeros((bsz, heads, dk, dv), jnp.float32),
                         jnp.moveaxis(kv, 1, 0))
    r_prev = jnp.moveaxis(r_prev, 0, 1)
    xi = jnp.exp(log_gamma[:, None] * (idx + 1.0)[None])
    cross = jnp.einsum("bnihd,bnhde->bnihe", q * xi.T[None, None, :, :, None], r_prev)
    return (inner + cross).reshape(bsz, seq, heads, dv)

def token_mixer(h, positions, w_in, b_in, conv_dw_w, conv_dw_b, conv_ln_g, conv_ln_b,
                w_conv_out, ret_gn_g, ret_gn_b, w_ret_out, w_out):
    bsz, seq, _ = h.shape
    proj = jnp.einsum("bsd,de->bse", h, w_in) + b_in
    q, k, v, g_ret, c_val, c_gate, gate_a, gate_b = jnp.split(proj, IN_SPLITS, axis=-1)

    a = c_val * jax.nn.sigmoid(c_gate)
    a = causal_depthwise_conv(a, conv_dw_w, conv_dw_b)
    a = jax.nn.silu(layer_norm(a, conv_ln_g, conv_ln_b))
    y_a = jnp.einsum("bsc,cd->bsd", a, w_conv_out)

    qf = rotary(q.reshape(bsz, seq, N_RET_HEADS, RET_QK_DIM).astype(jnp.float32), positions)
    kf = rotary(k.reshape(bsz, seq, N_RET_HEADS, RET_QK_DIM).astype(jnp.float32), positions)
    kf = kf * (RET_QK_DIM ** -0.5)
    vf = v.reshape(bsz, seq, N_RET_HEADS, RET_V_DIM).astype(jnp.float32)
    r = chunkwise_retention(qf, kf, vf)
    mu = jnp.mean(r, axis=-1, keepdims=True)
    var = jnp.mean(jnp.square(r - mu), axis=-1, keepdims=True)
    r = ((r - mu) * lax.rsqrt(var + LN_EPS)).reshape(bsz, seq, RET_V_WIDTH).astype(h.dtype)
    r = (r * ret_gn_g + ret_gn_b) * jax.nn.silu(g_ret)
    y_b = jnp.einsum("bse,ed->bsd", r, w_ret_out)

    m = jax.nn.sigmoid(gate_a) * y_a + jax.nn.sigmoid(gate_b) * y_b
    return jnp.einsum("bsd,de->bse", m, w_out)

def channel_mixer(h, w_up, ffn_dw_w, ffn_dw_b, w_down):
    u = jnp.einsum("bsd,df->bsf", h, w_up)
    u = causal_depthwise_conv(u, ffn_dw_w, ffn_dw_b)
    val, gate = jnp.split(u, 2, axis=-1)
    return jnp.einsum("bsf,fd->bsd", val * jax.nn.silu(gate), w_down)

def first_inputs(seed: int = 0) -> dict:
    key = jax.random.key(seed)
    ks = jax.random.split(key, 32)
    f32 = jnp.float32

    def nrm(k, shape, scale):
        return jax.random.normal(k, shape, f32) * scale

    L, D = DEPTH, D_MODEL
    x = jax.random.normal(ks[0], (BATCH, SEQ, D), f32)
    c = jax.random.normal(ks[1], (BATCH, D), f32)
    offset = jax.random.randint(ks[2], (BATCH, 1), 0, 1024, dtype=jnp.int32)
    positions = offset + jnp.arange(SEQ, dtype=jnp.int32)[None, :]
    return {
        "x": x,
        "c": c,
        "positions": positions,
        "w_ada": nrm(ks[3], (L, D, N_MOD * D), 0.5 * D ** -0.5),
        "b_ada": nrm(ks[4], (L, N_MOD * D), 0.02),
        "w_in": nrm(ks[5], (L, D, IN_WIDTH), D ** -0.5),
        "b_in": nrm(ks[6], (L, IN_WIDTH), 0.02),
        "conv_dw_w": nrm(ks[7], (L, CONV_KERNEL, CONV_WIDTH), CONV_KERNEL ** -0.5),
        "conv_dw_b": nrm(ks[8], (L, CONV_WIDTH), 0.02),
        "conv_ln_g": 1.0 + nrm(ks[9], (L, CONV_WIDTH), 0.02),
        "conv_ln_b": nrm(ks[10], (L, CONV_WIDTH), 0.02),
        "w_conv_out": nrm(ks[11], (L, CONV_WIDTH, D), CONV_WIDTH ** -0.5),
        "ret_gn_g": 1.0 + nrm(ks[12], (L, RET_V_WIDTH), 0.02),
        "ret_gn_b": nrm(ks[13], (L, RET_V_WIDTH), 0.02),
        "w_ret_out": nrm(ks[14], (L, RET_V_WIDTH, D), RET_V_WIDTH ** -0.5),
        "w_out": nrm(ks[15], (L, D, D), DEEPNORM_BETA * D ** -0.5),
        "ln1_g": 1.0 + nrm(ks[16], (L, D), 0.02),
        "ln1_b": nrm(ks[17], (L, D), 0.02),
        "w_up": nrm(ks[18], (L, D, 2 * D_FF), D ** -0.5),
        "ffn_dw_w": nrm(ks[19], (L, FFN_CONV_KERNEL, 2 * D_FF), FFN_CONV_KERNEL ** -0.5),
        "ffn_dw_b": nrm(ks[20], (L, 2 * D_FF), 0.02),
        "w_down": nrm(ks[21], (L, D_FF, D), DEEPNORM_BETA * D_FF ** -0.5),
        "ln2_g": 1.0 + nrm(ks[22], (L, D), 0.02),
        "ln2_b": nrm(ks[23], (L, D), 0.02),
    }

def first_block(x, c, positions, w_ada, b_ada, w_in, b_in, conv_dw_w, conv_dw_b, conv_ln_g,
              conv_ln_b, w_conv_out, ret_gn_g, ret_gn_b, w_ret_out, w_out, ln1_g, ln1_b,
              w_up, ffn_dw_w, ffn_dw_b, w_down, ln2_g, ln2_b):
    for l in range(DEPTH):
        mod = jnp.einsum("bd,de->be", jax.nn.silu(c), w_ada[l]) + b_ada[l]
        shift1, scale1, gate1, shift2, scale2, gate2 = jnp.split(mod[:, None, :], N_MOD, axis=-1)

        h = layer_norm(x) * (1.0 + scale1) + shift1
        t = token_mixer(h, positions, w_in[l], b_in[l], conv_dw_w[l], conv_dw_b[l],
                        conv_ln_g[l], conv_ln_b[l], w_conv_out[l], ret_gn_g[l], ret_gn_b[l],
                        w_ret_out[l], w_out[l])
        x = layer_norm(DEEPNORM_ALPHA * x + gate1 * t, ln1_g[l], ln1_b[l])

        h = layer_norm(x) * (1.0 + scale2) + shift2
        f = channel_mixer(h, w_up[l], ffn_dw_w[l], ffn_dw_b[l], w_down[l])
        x = layer_norm(DEEPNORM_ALPHA * x + gate2 * f, ln2_g[l], ln2_b[l])
    return x


_first_inputs = first_inputs


def first_inputs(seed=0):
    import zlib

    import numpy as np

    out = dict(_first_inputs(seed))
    spreads = {}
    factors = {'b_ada': 5.451,
     'b_in': 8.0,
     'conv_dw_b': 8.0,
     'conv_ln_g': 54.652,
     'conv_ln_b': 56.603,
     'ret_gn_g': 58.576,
     'ret_gn_b': 56.657,
     'ln1_g': 8.111,
     'ln1_b': 8.185,
     'ffn_dw_b': 51.154,
     'ln2_g': 8.039,
     'ln2_b': 8.225}
    for name, (base, spread) in spreads.items():
        noise = np.random.default_rng([zlib.crc32(name.encode()), seed]).standard_normal(out[name].shape)
        drawn = base * np.exp(spread * noise) if base else spread * noise
        out[name] = __import__('jax').numpy.asarray(drawn.astype(out[name].dtype))
    for name, factor in factors.items():
        out[name] = (out[name] * factor).astype(out[name].dtype)
    return out


_narrow_inputs = first_inputs


def first_inputs(seed=0):

    out = dict(_narrow_inputs(seed))
    wider = {'conv_ln_g': 4.66,
     'conv_ln_b': 4.67,
     'ret_gn_g': 4.65,
     'ret_gn_b': 4.64,
     'ln1_g': 3.18,
     'ln1_b': 3.21,
     'ln2_g': 3.23,
     'ln2_b': 3.2}
    for name, times in wider.items():
        mean = out[name].mean()
        out[name] = (mean + times * (out[name] - mean)).astype(out[name].dtype)
    return out


GRID_W = 64
CTX_LEN = 256
D_MIX = D_MODEL
HG_WIDTH = D_MIX // 2
HG_HEAD_DIM = 128
HG_HEADS = HG_WIDTH // HG_HEAD_DIM
ML_WIDTH = D_MIX - HG_WIDTH
ML_HEADS = 4
ML_V_DIM = ML_WIDTH // ML_HEADS
ML_QK_DIM = ML_V_DIM // 2
ML_QK_WIDTH = ML_HEADS * ML_QK_DIM
N_ML_GATES = 4 * ML_HEADS
IN_SIZES_2 = (HG_WIDTH, HG_WIDTH, HG_WIDTH, HG_WIDTH, HG_WIDTH, ML_QK_WIDTH, ML_QK_WIDTH, ML_WIDTH, ML_WIDTH, N_ML_GATES)
D_IN = 5 * HG_WIDTH + 2 * ML_QK_WIDTH + 2 * ML_WIDTH + N_ML_GATES
CONV_K = 3
CHUNK = 64
N_MOD_2 = 9
EPS = 1e-6


def rmsnorm(x, w):
    xf = x.astype(jnp.float32)
    y = xf * lax.rsqrt(jnp.mean(xf * xf, axis=-1, keepdims=True) + EPS)
    return (y * w.astype(jnp.float32)).astype(x.dtype)

def head_rmsnorm(x, w, n_heads):
    shp = x.shape
    xf = x.astype(jnp.float32).reshape(shp[:-1] + (n_heads, shp[-1] // n_heads))
    y = xf * lax.rsqrt(jnp.mean(xf * xf, axis=-1, keepdims=True) + EPS)
    return y.reshape(shp) * w.astype(jnp.float32)

def modulate(xn, shift, scale):
    return xn * (1 + scale) + shift

def swiglu(h, w1, w2):
    g, u = jnp.split(h @ w1, 2, axis=-1)
    return (jax.nn.silu(g) * u) @ w2

def split_heads(a, n_heads):
    return a.reshape(a.shape[:-1] + (n_heads, a.shape[-1] // n_heads))

def seg_reverse(a, n_ctx):
    return jnp.concatenate([jnp.flip(a[:, :n_ctx], axis=1), jnp.flip(a[:, n_ctx:], axis=1)], axis=1)

def to_chunks(a):
    bp, t, h, d = a.shape
    return a.reshape(bp, t // CHUNK, CHUNK, h, d).transpose(1, 0, 3, 2, 4)

def gates_to_chunks(g):
    bp, t, h = g.shape
    return g.reshape(bp, t // CHUNK, CHUNK, h).transpose(1, 0, 3, 2)

def from_chunks(a):
    n, bp, h, l, d = a.shape
    return a.transpose(1, 0, 3, 2, 4).reshape(bp, n * l, h, d)

def hgrn2_chunk_scan(q, k, v, log_f):
    bp, _, h, dk = q.shape
    dv = v.shape[-1]
    scan_order = jnp.tril(jnp.ones((CHUNK, CHUNK), dtype=bool))

    def step(state, inp):
        qb, kb, vb, fb = inp
        b = jnp.cumsum(fb, axis=2)
        diff = b[:, :, :, None, :] - b[:, :, None, :, :]
        decay = jnp.exp(jnp.where(scan_order[:, :, None], diff, -jnp.inf))
        scores = jnp.einsum('bhtd,bhtsd,bhsd->bhts', qb, decay, kb)
        o = jnp.einsum('bhts,bhse->bhte', scores, vb) + jnp.einsum('bhtd,bhde->bhte', qb * jnp.exp(b), state)
        b_last = b[:, :, -1:, :]
        state = jnp.exp(b_last[:, :, 0, :, None]) * state + jnp.einsum('bhsd,bhse->bhde', kb * jnp.exp(b_last - b), vb)
        return state, o

    s0 = jnp.zeros((bp, h, dk, dv), jnp.float32)
    _, out = lax.scan(step, s0, (to_chunks(q), to_chunks(k), to_chunks(v), to_chunks(log_f)))
    return from_chunks(out)

def mlstm_chunk_scan(q, k, v, i_pre, log_f):
    bp, _, h, dqk = q.shape
    dv = v.shape[-1]
    scan_order = jnp.tril(jnp.ones((CHUNK, CHUNK), dtype=bool))

    def step(carry, inp):
        c_mem, n_mem, m = carry
        qb, kb, vb, ib, fb = inp
        b = jnp.cumsum(fb, axis=-1)
        d_log = jnp.where(scan_order, b[..., :, None] - b[..., None, :] + ib[..., None, :], -jnp.inf)
        inter_log = b + m[..., None]
        m_t = jnp.maximum(jnp.max(d_log, axis=-1), inter_log)
        w = jnp.exp(d_log - m_t[..., None])
        inter_w = jnp.exp(inter_log - m_t)
        qk = jnp.einsum('bhtd,bhsd->bhts', qb, kb) * w
        num = jnp.einsum('bhts,bhse->bhte', qk, vb) + inter_w[..., None] * jnp.einsum('bhtd,bhde->bhte', qb, c_mem)
        den = jnp.sum(qk, axis=-1) + inter_w * jnp.einsum('bhtd,bhd->bht', qb, n_mem)
        h_out = num / jnp.maximum(jnp.abs(den), jnp.exp(-m_t))[..., None]
        b_last = b[..., -1]
        state_log = b_last[..., None] - b + ib
        m_new = jnp.maximum(b_last + m, jnp.max(state_log, axis=-1))
        carry_w = jnp.exp(b_last + m - m_new)
        s_w = jnp.exp(state_log - m_new[..., None])
        c_mem = carry_w[..., None, None] * c_mem + jnp.einsum('bhs,bhsd,bhse->bhde', s_w, kb, vb)
        n_mem = carry_w[..., None] * n_mem + jnp.einsum('bhs,bhsd->bhd', s_w, kb)
        return (c_mem, n_mem, m_new), h_out

    init = (jnp.zeros((bp, h, dqk, dv), jnp.float32), jnp.zeros((bp, h, dqk), jnp.float32), jnp.zeros((bp, h), jnp.float32))
    _, out = lax.scan(step, init, (to_chunks(q), to_chunks(k), to_chunks(v), gates_to_chunks(i_pre), gates_to_chunks(log_f)))
    return from_chunks(out)

def short_conv(a, w, b, n_ctx):
    w = w.astype(a.dtype)
    a_ctx, a_lat = a[:, :n_ctx], a[:, n_ctx:]
    bsz, s_lat, ch = a_lat.shape
    rows = s_lat // GRID_W
    lat = lax.conv_general_dilated(a_lat.reshape(bsz, rows, GRID_W, ch), w[:, :, None, :], (1, 1), 'SAME',
                                   dimension_numbers=('NHWC', 'HWIO', 'NHWC'), feature_group_count=ch)
    ctx = lax.conv_general_dilated(a_ctx, w[CONV_K // 2][:, None, :], (1,), 'SAME',
                                   dimension_numbers=('NWC', 'WIO', 'NWC'), feature_group_count=ch)
    return jnp.concatenate([ctx, lat.reshape(bsz, s_lat, ch)], axis=1) + b

def parallel_mixer(h_ctx, h_lat, w_in, ml_gate_b, conv_w, conv_b, lb, hg_norm_w, ml_norm_w, w_out, lat_only):
    f32 = jnp.float32
    n_ctx = h_ctx.shape[1]
    bsz = h_lat.shape[0]
    out_dtype = h_lat.dtype
    h_all = jnp.concatenate([h_ctx, h_lat], axis=1)
    proj = h_all @ w_in
    splits = [int(s) for s in np.cumsum(IN_SIZES_2)[:-1]]
    hg_q, hg_i, hg_g, hg_f_fwd, hg_f_bwd, ml_q, ml_k, ml_v, ml_o, ml_gates = jnp.split(proj, splits, axis=-1)

    def both_dirs(a):
        return jnp.concatenate([a, seg_reverse(a, n_ctx)], axis=0)

    def merge_dirs(o):
        return o[:bsz] + seg_reverse(o[bsz:], n_ctx)

    q = split_heads(jax.nn.silu(hg_q.astype(f32)) * HG_HEAD_DIM ** -0.5, HG_HEADS)
    v = split_heads(hg_i.astype(f32), HG_HEADS)
    lb_dir = jnp.repeat(lb, bsz, axis=0)[:, None, :]
    f_pre = jnp.concatenate([hg_f_fwd, seg_reverse(hg_f_bwd, n_ctx)], axis=0).astype(f32)
    log_f = jnp.log(lb_dir + (1 - lb_dir) * jax.nn.sigmoid(f_pre))
    k_in = (1 - lb_dir) * jax.nn.sigmoid(-f_pre)
    hg_o = hgrn2_chunk_scan(both_dirs(q), split_heads(k_in, HG_HEADS), both_dirs(v), split_heads(log_f, HG_HEADS))
    hg_o = merge_dirs(hg_o).reshape(bsz, -1, HG_WIDTH)
    hg_out = head_rmsnorm(hg_o, hg_norm_w, HG_HEADS) * jax.nn.silu(hg_g.astype(f32))

    qk = jax.nn.silu(short_conv(jnp.concatenate([ml_q, ml_k], axis=-1), conv_w, conv_b, n_ctx)).astype(f32)
    mq, mk = jnp.split(qk, 2, axis=-1)
    mq = split_heads(mq * ML_QK_DIM ** -0.5, ML_HEADS)
    mk = split_heads(mk, ML_HEADS)
    mv = split_heads(ml_v.astype(f32), ML_HEADS)
    gates = ml_gates.astype(f32) + ml_gate_b.astype(f32)
    i_fwd, f_fwd, i_bwd, f_bwd = jnp.split(gates, 4, axis=-1)
    i_dir = jnp.concatenate([i_fwd, seg_reverse(i_bwd, n_ctx)], axis=0)
    logf_dir = jax.nn.log_sigmoid(jnp.concatenate([f_fwd, seg_reverse(f_bwd, n_ctx)], axis=0))
    ml_h = mlstm_chunk_scan(both_dirs(mq), both_dirs(mk), both_dirs(mv), i_dir, logf_dir)
    ml_h = merge_dirs(ml_h).reshape(bsz, -1, ML_WIDTH)
    ml_out = jax.nn.sigmoid(ml_o.astype(f32)) * head_rmsnorm(ml_h, ml_norm_w, ML_HEADS)

    merged = jnp.concatenate([hg_out, ml_out], axis=-1).astype(out_dtype)
    lat_out = merged[:, n_ctx:] @ w_out
    ctx_out = None if lat_only else merged[:, :n_ctx] @ w_out
    return ctx_out, lat_out

def second_inputs(seed: int = 0) -> dict:
    key = jax.random.key(seed)
    ks = jax.random.split(key, 26)
    nrm = jax.random.normal
    f32 = jnp.float32

    def gain(k, shape):
        return 1.0 + 0.01 * nrm(k, shape, f32)

    def fbias(k):
        return 3.0 + 3.0 * jax.random.uniform(k, (DEPTH, ML_HEADS), f32)

    ml_gate_b = jnp.concatenate([0.1 * nrm(ks[10], (DEPTH, ML_HEADS), f32), fbias(ks[11]),
                                 0.1 * nrm(ks[12], (DEPTH, ML_HEADS), f32), fbias(ks[13])], axis=-1)
    return {
        'x': nrm(ks[0], (BATCH, SEQ, D_MODEL), f32),
        'c': nrm(ks[1], (BATCH, D_MODEL), f32),
        'ctx': nrm(ks[2], (BATCH, CTX_LEN, D_MODEL), f32),
        'c_ctx': nrm(ks[3], (D_MODEL,), f32),
        'w_mod': nrm(ks[4], (DEPTH, D_MODEL, N_MOD_2 * D_MODEL), f32) * D_MODEL ** -0.5,
        'b_mod': 0.01 * nrm(ks[5], (DEPTH, N_MOD_2 * D_MODEL), f32),
        'norm1_w': gain(ks[6], (DEPTH, D_MODEL)),
        'ffn1_w1': nrm(ks[7], (DEPTH, D_MODEL, 2 * D_FF), f32) * D_MODEL ** -0.5,
        'ffn1_w2': nrm(ks[8], (DEPTH, D_FF, D_MODEL), f32) * D_FF ** -0.5,
        'norm2_w': gain(ks[9], (DEPTH, D_MODEL)),
        'w_in': nrm(ks[14], (DEPTH, D_MODEL, D_IN), f32) * D_MODEL ** -0.5,
        'ml_gate_b': ml_gate_b,
        'ml_conv_w': nrm(ks[15], (DEPTH, CONV_K, CONV_K, 2 * ML_QK_WIDTH), f32) / CONV_K,
        'ml_conv_b': 0.01 * nrm(ks[16], (DEPTH, 2 * ML_QK_WIDTH), f32),
        'hg_lb_logits': 0.5 * nrm(ks[17], (DEPTH + 1, 2, HG_WIDTH), f32),
        'hg_norm_w': gain(ks[18], (DEPTH, HG_WIDTH)),
        'ml_norm_w': gain(ks[19], (DEPTH, ML_WIDTH)),
        'w_out': nrm(ks[20], (DEPTH, D_MIX, D_MODEL), f32) * D_MIX ** -0.5,
        'norm3_w': gain(ks[21], (DEPTH, D_MODEL)),
        'ffn2_w1': nrm(ks[22], (DEPTH, D_MODEL, 2 * D_FF), f32) * D_MODEL ** -0.5,
        'ffn2_w2': nrm(ks[23], (DEPTH, D_FF, D_MODEL), f32) * D_FF ** -0.5,
        'final_norm_w': gain(ks[24], (D_MODEL,)),
    }

def second_block(x, c, ctx, c_ctx, w_mod, b_mod, norm1_w, ffn1_w1, ffn1_w2, norm2_w, w_in, ml_gate_b,
              ml_conv_w, ml_conv_b, hg_lb_logits, hg_norm_w, ml_norm_w, w_out, norm3_w, ffn2_w1, ffn2_w2,
              final_norm_w):
    lb_all = jnp.cumsum(jax.nn.softmax(hg_lb_logits.astype(jnp.float32), axis=0), axis=0)
    s_ctx = ctx

    def ffn_sub(s, mods, nw, w1, w2):
        shift, scale, gate = mods
        return s + 0.5 * gate * swiglu(modulate(rmsnorm(s, nw), shift, scale), w1, w2)

    for l in range(DEPTH):
        last = l == DEPTH - 1
        mod_lat = jnp.split((jax.nn.silu(c) @ w_mod[l] + b_mod[l])[:, None, :], N_MOD_2, axis=-1)
        mod_ctx = jnp.split(jax.nn.silu(c_ctx) @ w_mod[l] + b_mod[l], N_MOD_2, axis=-1)

        x = ffn_sub(x, mod_lat[0:3], norm1_w[l], ffn1_w1[l], ffn1_w2[l])
        s_ctx = ffn_sub(s_ctx, mod_ctx[0:3], norm1_w[l], ffn1_w1[l], ffn1_w2[l])

        h_lat = modulate(rmsnorm(x, norm2_w[l]), mod_lat[3], mod_lat[4])
        h_ctx = modulate(rmsnorm(s_ctx, norm2_w[l]), mod_ctx[3], mod_ctx[4])
        ctx_mix, lat_mix = parallel_mixer(h_ctx, h_lat, w_in[l], ml_gate_b[l], ml_conv_w[l], ml_conv_b[l],
                                          lb_all[l], hg_norm_w[l], ml_norm_w[l], w_out[l], last)
        x = x + mod_lat[5] * lat_mix

        x = ffn_sub(x, mod_lat[6:9], norm3_w[l], ffn2_w1[l], ffn2_w2[l])
        if not last:
            s_ctx = s_ctx + mod_ctx[5] * ctx_mix
            s_ctx = ffn_sub(s_ctx, mod_ctx[6:9], norm3_w[l], ffn2_w1[l], ffn2_w2[l])

    return rmsnorm(x, final_norm_w)


_first_inputs_2 = second_inputs


def second_inputs(seed=0):
    import zlib

    import numpy as np

    out = dict(_first_inputs_2(seed))
    spreads = {}
    factors = {'b_mod': 4.134,
     'norm1_w': 8.0,
     'norm2_w': 8.0,
     'ml_conv_b': 8.0,
     'hg_lb_logits': 6.554,
     'hg_norm_w': 8.0,
     'ml_norm_w': 8.0,
     'norm3_w': 8.0,
     'final_norm_w': 5.702}
    for name, (base, spread) in spreads.items():
        noise = np.random.default_rng([zlib.crc32(name.encode()), seed]).standard_normal(out[name].shape)
        drawn = base * np.exp(spread * noise) if base else spread * noise
        out[name] = jnp.asarray(drawn.astype(out[name].dtype))
    for name, factor in factors.items():
        out[name] = (out[name] * factor).astype(out[name].dtype)
    return out


_narrow_inputs_2 = second_inputs


def second_inputs(seed=0):

    out = dict(_narrow_inputs_2(seed))
    wider = {'norm2_w': 4.89,
     'ml_conv_w': 7.61,
     'ml_conv_b': 12.0,
     'hg_norm_w': 7.61,
     'ml_norm_w': 12.0,
     'norm3_w': 8.53,
     'final_norm_w': 6.36}
    for name, times in wider.items():
        mean = out[name].mean()
        out[name] = (mean + times * (out[name] - mean)).astype(out[name].dtype)
    return out


N_META = 16
ROPE_THETA = 10000.0
BLOCK_Q = 128
MLA_HEADS = 8
MLA_Q_RANK = 256
MLA_KV_RANK = 128
MLA_NOPE_DIM = 64
MLA_ROPE_DIM = 32
MLA_QK_DIM = MLA_NOPE_DIM + MLA_ROPE_DIM
MLA_V_DIM = 64
DSA_HEADS = 8
DSA_HEAD_DIM = 64
IDX_HEADS = 8
IDX_DIM = 64
TOPK_MAX = 256
MIX_WIDTH = MLA_HEADS * MLA_V_DIM + DSA_HEADS * DSA_HEAD_DIM
IN_SIZES_3 = (MLA_Q_RANK, MLA_KV_RANK, MLA_ROPE_DIM,
            DSA_HEADS * DSA_HEAD_DIM, DSA_HEADS * DSA_HEAD_DIM, DSA_HEADS * DSA_HEAD_DIM,
            IDX_HEADS * IDX_DIM, IDX_DIM, IDX_HEADS)
C_IN = sum(IN_SIZES_3)
D_FF_RAW = -(-8 * D_MODEL // 3)
D_FF_3 = -(-D_FF_RAW // 256) * 256


def rmsnorm_3(x, g):
    x32 = x.astype(jnp.float32)
    y = x32 * lax.rsqrt(jnp.mean(x32 * x32, axis=-1, keepdims=True) + EPS)
    return (y * g.astype(jnp.float32)).astype(x.dtype)

def rope(x, pos):
    half = x.shape[-1] // 2
    inv = jnp.power(ROPE_THETA, -jnp.arange(half, dtype=jnp.float32) / half)
    ang = pos.astype(jnp.float32)[:, None] * inv[None, :]
    cos = jnp.cos(ang)[:, None, :]
    sin = jnp.sin(ang)[:, None, :]
    x32 = x.astype(jnp.float32)
    x1, x2 = x32[..., :half], x32[..., half:]
    return jnp.concatenate([x1 * cos - x2 * sin, x2 * cos + x1 * sin], axis=-1).astype(x.dtype)

def to_blocks(a):
    b, tp = a.shape[0], a.shape[1]
    return a.reshape((b, tp // BLOCK_Q, BLOCK_Q) + a.shape[2:]).swapaxes(0, 1)

def from_blocks(a):
    a = a.swapaxes(0, 1)
    return a.reshape((a.shape[0], a.shape[1] * a.shape[2]) + a.shape[3:])

def causal_block_attention(q, k, v):
    tp = q.shape[1]
    scale = q.shape[-1] ** -0.5
    kpos = jnp.arange(tp)

    def one_block(args):
        qb, blk = args
        qpos = blk * BLOCK_Q + jnp.arange(BLOCK_Q)
        s = jnp.einsum('bqhd,bkhd->bhqk', qb, k, preferred_element_type=jnp.float32) * scale
        s = jnp.where((kpos[None, :] <= qpos[:, None])[None, None], s, -jnp.inf)
        p = jax.nn.softmax(s, axis=-1).astype(v.dtype)
        return jnp.einsum('bhqk,bkhd->bqhd', p, v)

    out = lax.map(one_block, (to_blocks(q), jnp.arange(tp // BLOCK_Q)))
    return from_blocks(out)

def indexed_sparse_attention(q, k, v, q_idx, k_idx, w_idx, topk):
    tp = q.shape[1]
    scale = q.shape[-1] ** -0.5
    idx_scale = IDX_DIM ** -0.5
    kpos = jnp.arange(tp)

    def one_block(args):
        qb, qib, wib, blk = args
        qpos = blk * BLOCK_Q + jnp.arange(BLOCK_Q)
        causal = kpos[None, :] <= qpos[:, None]
        logits = jnp.einsum('bqhd,bkd->bqhk', qib, k_idx, preferred_element_type=jnp.float32) * idx_scale
        score = jnp.einsum('bqh,bqhk->bqk', wib.astype(jnp.float32), jax.nn.relu(logits))
        score = jnp.where(causal[None], score, -jnp.inf)
        _, sel = lax.top_k(score, topk)
        valid = sel <= qpos[None, :, None]
        k_sel = jax.vmap(lambda kb, ib: kb[ib])(k, sel)
        v_sel = jax.vmap(lambda vb, ib: vb[ib])(v, sel)
        s = jnp.einsum('bqhd,bqkhd->bhqk', qb, k_sel, preferred_element_type=jnp.float32) * scale
        s = jnp.where(valid[:, None], s, -jnp.inf)
        p = jax.nn.softmax(s, axis=-1).astype(v.dtype)
        return jnp.einsum('bhqk,bqkhd->bqhd', p, v_sel)

    out = lax.map(one_block, (to_blocks(q), to_blocks(q_idx), to_blocks(w_idx), jnp.arange(tp // BLOCK_Q)))
    return from_blocks(out)

def hybrid_mixer(u, pos, topk, w_in, q_norm_g, w_uq, kv_norm_g, w_ukv, w_o):
    b, tp, _ = u.shape
    proj = u @ w_in
    splits = [int(v) for v in np.cumsum(IN_SIZES_3)[:-1]]
    c_q, c_kv, k_r, q_s, k_s, v_s, q_i, k_i, w_i = jnp.split(proj, splits, axis=-1)

    q = (rmsnorm_3(c_q, q_norm_g) @ w_uq).reshape(b, tp, MLA_HEADS, MLA_QK_DIM)
    q_mla = jnp.concatenate([q[..., :MLA_NOPE_DIM], rope(q[..., MLA_NOPE_DIM:], pos)], axis=-1)
    kv = (rmsnorm_3(c_kv, kv_norm_g) @ w_ukv).reshape(b, tp, MLA_HEADS, MLA_NOPE_DIM + MLA_V_DIM)
    k_rope = rope(k_r[:, :, None, :], pos)
    k_mla = jnp.concatenate([kv[..., :MLA_NOPE_DIM],
                             jnp.broadcast_to(k_rope, (b, tp, MLA_HEADS, MLA_ROPE_DIM))], axis=-1)
    v_mla = kv[..., MLA_NOPE_DIM:]
    o_mla = causal_block_attention(q_mla, k_mla, v_mla)

    q_s = rope(q_s.reshape(b, tp, DSA_HEADS, DSA_HEAD_DIM), pos)
    k_s = rope(k_s.reshape(b, tp, DSA_HEADS, DSA_HEAD_DIM), pos)
    v_s = v_s.reshape(b, tp, DSA_HEADS, DSA_HEAD_DIM)
    q_i = rope(q_i.reshape(b, tp, IDX_HEADS, IDX_DIM), pos)
    k_i = rope(k_i[:, :, None, :], pos)[:, :, 0, :]
    w_i = w_i * (IDX_HEADS ** -0.5)
    o_dsa = indexed_sparse_attention(q_s, k_s, v_s, q_i, k_i, w_i, topk)

    o = jnp.concatenate([o_mla.reshape(b, tp, MLA_HEADS * MLA_V_DIM),
                         o_dsa.reshape(b, tp, DSA_HEADS * DSA_HEAD_DIM)], axis=-1)
    return o @ w_o

def swiglu_3(u, w_gate, w_up, w_down):
    return (jax.nn.silu(u @ w_gate) * (u @ w_up)) @ w_down

def third_inputs(seed: int = 0) -> dict:
    key = jax.random.key(seed)
    ks = jax.random.split(key, 16)
    f32 = jnp.float32

    def w(k, shape, fan_in):
        return jax.random.normal(k, shape, f32) * (fan_in ** -0.5)

    def g(k, shape):
        return 1.0 + 0.02 * jax.random.normal(k, shape, f32)

    return {
        'x': jax.random.normal(ks[0], (BATCH, SEQ, D_MODEL), f32),
        'meta_tokens': jax.random.normal(ks[1], (N_META, D_MODEL), f32),
        'attn_norm_g': g(ks[2], (DEPTH, D_MODEL)),
        'w_in': w(ks[3], (DEPTH, D_MODEL, C_IN), D_MODEL),
        'mla_q_norm_g': g(ks[4], (DEPTH, MLA_Q_RANK)),
        'w_uq': w(ks[5], (DEPTH, MLA_Q_RANK, MLA_HEADS * MLA_QK_DIM), MLA_Q_RANK),
        'mla_kv_norm_g': g(ks[6], (DEPTH, MLA_KV_RANK)),
        'w_ukv': w(ks[7], (DEPTH, MLA_KV_RANK, MLA_HEADS * (MLA_NOPE_DIM + MLA_V_DIM)), MLA_KV_RANK),
        'w_o': w(ks[8], (DEPTH, MIX_WIDTH, D_MODEL), MIX_WIDTH),
        'ffn_norm_g': g(ks[9], (DEPTH, D_MODEL)),
        'w_gate': w(ks[10], (DEPTH, D_MODEL, D_FF_3), D_MODEL),
        'w_up': w(ks[11], (DEPTH, D_MODEL, D_FF_3), D_MODEL),
        'w_down': w(ks[12], (DEPTH, D_FF_3, D_MODEL), D_FF_3),
        'final_norm_g': g(ks[13], (D_MODEL,)),
    }

def third_block(x, meta_tokens, attn_norm_g, w_in, mla_q_norm_g, w_uq, mla_kv_norm_g, w_ukv, w_o,
              ffn_norm_g, w_gate, w_up, w_down, final_norm_g):
    b, seq, _ = x.shape
    topk = min(TOPK_MAX, seq // 4)
    meta = jnp.broadcast_to(meta_tokens[None].astype(x.dtype), (b, N_META, D_MODEL))
    h = jnp.concatenate([meta, x], axis=1)
    t = h.shape[1]
    tp = -(-t // BLOCK_Q) * BLOCK_Q
    h = jnp.pad(h, ((0, 0), (0, tp - t), (0, 0)))
    pos = jnp.arange(tp, dtype=jnp.int32)
    for l in range(DEPTH):
        h = h + hybrid_mixer(rmsnorm_3(h, attn_norm_g[l]), pos, topk, w_in[l], mla_q_norm_g[l], w_uq[l],
                             mla_kv_norm_g[l], w_ukv[l], w_o[l])
        h = h + swiglu_3(rmsnorm_3(h, ffn_norm_g[l]), w_gate[l], w_up[l], w_down[l])
    h = rmsnorm_3(h, final_norm_g)
    return h[:, N_META:t]


def setup_inputs(seed=0):
    out = dict(first_inputs(seed))
    for name, value in second_inputs(seed + 1).items():
        if name != "x":
            out[name + "_2"] = value
    for name, value in third_inputs(seed + 2).items():
        if name != "x":
            out[name + "_3"] = value
    return out


def reference(
    x, c, positions, w_ada, b_ada, w_in, b_in, conv_dw_w, conv_dw_b, conv_ln_g, conv_ln_b,
    w_conv_out, ret_gn_g, ret_gn_b, w_ret_out, w_out, ln1_g, ln1_b, w_up, ffn_dw_w, ffn_dw_b,
    w_down, ln2_g, ln2_b, c_2, ctx_2, c_ctx_2, w_mod_2, b_mod_2, norm1_w_2, ffn1_w1_2,
    ffn1_w2_2, norm2_w_2, w_in_2, ml_gate_b_2, ml_conv_w_2, ml_conv_b_2, hg_lb_logits_2,
    hg_norm_w_2, ml_norm_w_2, w_out_2, norm3_w_2, ffn2_w1_2, ffn2_w2_2, final_norm_w_2,
    meta_tokens_3, attn_norm_g_3, w_in_3, mla_q_norm_g_3, w_uq_3, mla_kv_norm_g_3, w_ukv_3,
    w_o_3, ffn_norm_g_3, w_gate_3, w_up_3, w_down_3, final_norm_g_3,
):
    x = first_block(
        x, c, positions, w_ada, b_ada, w_in, b_in, conv_dw_w, conv_dw_b, conv_ln_g, conv_ln_b,
        w_conv_out, ret_gn_g, ret_gn_b, w_ret_out, w_out, ln1_g, ln1_b, w_up, ffn_dw_w,
        ffn_dw_b, w_down, ln2_g, ln2_b,
    )
    x = second_block(
        x, c_2, ctx_2, c_ctx_2, w_mod_2, b_mod_2, norm1_w_2, ffn1_w1_2, ffn1_w2_2, norm2_w_2,
        w_in_2, ml_gate_b_2, ml_conv_w_2, ml_conv_b_2, hg_lb_logits_2, hg_norm_w_2, ml_norm_w_2,
        w_out_2, norm3_w_2, ffn2_w1_2, ffn2_w2_2, final_norm_w_2,
    )
    return third_block(
        x, meta_tokens_3, attn_norm_g_3, w_in_3, mla_q_norm_g_3, w_uq_3, mla_kv_norm_g_3,
        w_ukv_3, w_o_3, ffn_norm_g_3, w_gate_3, w_up_3, w_down_3, final_norm_g_3,
    )


_drawn_inputs = setup_inputs


def setup_inputs(seed=0):
    import zlib

    import numpy as np

    out = dict(_drawn_inputs(seed))
    spreads = {}
    factors = {'norm1_w_2': 3.003,
     'ml_conv_w_2': 7.916,
     'ml_conv_b_2': 115.197,
     'ml_norm_w_2': 5.507,
     'meta_tokens_3': 4.549,
     'attn_norm_g_3': 8.0,
     'mla_q_norm_g_3': 8.0,
     'w_uq_3': 3.714,
     'mla_kv_norm_g_3': 8.0,
     'ffn_norm_g_3': 8.0,
     'final_norm_g_3': 27.053}
    for name, (base, spread) in spreads.items():
        noise = np.random.default_rng([zlib.crc32(name.encode()), seed]).standard_normal(out[name].shape)
        drawn = base * np.exp(spread * noise) if base else spread * noise
        out[name] = jnp.asarray(drawn.astype(out[name].dtype))
    for name, factor in factors.items():
        out[name] = (out[name] * factor).astype(out[name].dtype)
    return out
```

```python
from contextlib import ExitStack

import numpy as np

import concourse.bass as bass
from concourse import mybir

F32 = mybir.dt.float32
U8 = mybir.dt.uint8
I32 = mybir.dt.int32
ALU = mybir.AluOpType
ACT = mybir.ActivationFunctionType
AX = mybir.AxisListType

P = 128
D = 1024
DT = D // P
SEQ, CTX, META = 512, 256, 16
TOK = CTX + SEQ
LAT = CTX
FF = 2816
FT = FF // P
CONV_K = 31
RET_HEADS = 8
ALPHA = float(2.0 ** 0.25)
LN_EPS, RMS_EPS = 1e-5, 1e-6
SLOT = 4096

VEC_SIZES = dict(
    c=8, b_ada=48, b_cval=8, b_cgate=8, b_qk=16, b_g=16, b_ga=8, b_gb=8, conv_w=8 * CONV_K, conv_b=8,
    cln_g=8, cln_b=8, gn_g=16, gn_b=16, ln1_g=8, ln1_b=8, ffn_w=2 * FT * 3, ffn_b=2 * FT, ln2_g=8, ln2_b=8,
    inv_freq=1,
    cc2=16, b_mod=144, norm1=8, norm2=8, norm3=8, fnorm2=8, mconv_w=36, mconv_b=4, lb0=8, lb1=8,
    hg_norm=4, ml_norm=4, ml_gb=1,
    attn_norm=8, q_norm=2, kv_norm=1, ffn_norm=8, fnorm3=8,
)
VEC_AT = {}
_at = 0
for _name, _n in VEC_SIZES.items():
    VEC_AT[_name] = _at
    _at += _n
NVEC = _at


class Signal:

    def __init__(self, handle):
        self.sem, self.base = handle, 0

    def __call__(self, n):
        return self.sem, n + self.base

    def counted(self, n):
        self.base += n


class Core:

    def __init__(self, nc, ctx, ap):
        self.nc, self.ap = nc, ap

        def sb(name, shape, dt=F32):
            return ctx.enter_context(nc.sbuf_tensor(name, shape, dt))

        def sig(name):
            return Signal(ctx.enter_context(nc.semaphore(name)))

        self.X = sb("X", [P, DT, TOK])
        self.H = sb("H", [P, DT, TOK])
        self.W = [sb(f"W{u}", [P, SLOT]) for u in range(2)]
        self.vec = sb("vec", [P, NVEC])
        self.mod1 = sb("mod1", [P, 48])
        self.mod2 = sb("mod2", [P, 72, 2])
        self.gain = sb("gain", [P, 2, DT])
        self.ident = sb("ident", [P, P])
        self.rot = sb("rot", [P, P])
        self.masks = sb("masks", [P, 16, P], U8)
        self.tri = sb("tri", [P, 2, P])
        self.rot32, self.rot96 = self.tri[:, 0, :], self.tri[:, 1, :]
        self.neg = sb("neg", [P, P])
        self.sel = sb("sel", [4, 4, P])
        self.mean = sb("mean", [P, 4, P])
        self.sq = sb("sq", [P, 3, 512])
        self.rstd = sb("rstd", [P, 512])
        self.stage = sb("stage", [P, 2, 2, 516])
        self.arena = sb("arena", [P, ARENA])
        self.bank = [ctx.enter_context(nc.psum_tensor(f"bank{i}", [P, 512], F32)) for i in range(8)]

        self.loaded = sig("loaded")
        self.weights_in = [sig(f"weights_in{u}") for u in range(2)]
        self.group_done = sig("group_done")
        self.evicted = sig("evicted")
        self.act_turn = sig("act_turn")
        self.dve_turn = sig("dve_turn")
        self.act_done = sig("act_done")
        self.dve_done = sig("dve_done")
        self.pe_done = sig("pe_done")
        self.pool_done = sig("pool_done")
        self.stored = sig("stored")
        self.more = [sig(f"more{i}") for i in range(12)]

    def v(self, name, j=0, n=1):
        at = VEC_AT[name]
        return self.vec[:, bass.ds(at + j, n)] if not isinstance(j, int) else self.vec[:, at + j:at + j + n]


def flat(ap):
    return ap.rearrange("p a t -> p (a t)")


def linear(k, w, groups, kt, cols, src, chunks, act_evict=None, dve_evict=None, products=None,
           dve_other=None, counts=None):
    nc = k.nc
    tiles = cols // P
    half = groups // 2
    assert groups % 2 == 0 and kt * cols <= SLOT
    with nc.Block() as block:
        @block.sync
        def _(sp):
            for u in range(2):
                sp.dma_start(k.W[u][:, :kt * cols], w[u]).then_inc(k.weights_in[u].sem, 16)
            if half > 1:
                with sp.Fori(1, half) as i:
                    for u in range(2):
                        sp.wait_ge(*k.group_done(2 * i + (u - 1)))
                        sp.dma_start(k.W[u][:, :kt * cols],
                                     w[bass.ds(2 * i + u, 1)].rearrange("a p n -> (a p) n")
                                     ).then_inc(k.weights_in[u].sem, 16)

        @block.tensor
        def _(pe):
            with pe.Fori(0, half) as i:
                for u in range(2):
                    pe.wait_ge(*k.weights_in[u](16 * i + 16))
                    pe.wait_ge(*k.evicted(2 * i + (u - 1)))
                    if products:
                        products(pe, i, u).then_inc(k.group_done.sem, 1)
                        continue
                    for g in range(tiles):
                        for c, (a, b) in enumerate(chunks):
                            for kk in range(kt):
                                mm = pe.matmul(k.bank[4 * u + len(chunks) * g + c][:, :b - a],
                                               k.W[u][:, kk * cols + g * P:kk * cols + (g + 1) * P],
                                               src(kk, c), start=kk == 0, stop=kk == kt - 1)
                    mm.then_inc(k.group_done.sem, 1)

        @block.scalar
        def _(act):
            if act_evict:
                with act.Fori(0, half) as i:
                    for u in range(2):
                        act.wait_ge(*k.group_done(2 * i + (u + 1)))
                        act.sem_inc(k.act_turn.sem, 1)
                        act_evict(act, i, u)

        @block.vector
        def _(dve):
            if dve_other:
                dve_other(dve)
            if dve_evict:
                with dve.Fori(0, half) as i:
                    for u in range(2):
                        dve.wait_ge(*k.group_done(2 * i + (u + 1)))
                        dve.sem_inc(k.dve_turn.sem, 1)
                        dve_evict(dve, i, u)

    for u in range(2):
        k.weights_in[u].counted(16 * half)
    k.group_done.counted(groups)
    k.evicted.counted(groups)
    for s, n in (counts or {}).items():
        s.counted(n)


def norm(k, src, dst, nt, a, b, mean, eps, center, gain=None, post=None, shift=None):
    nc, n = k.nc, b - a
    pe_done, act_done, dve_done = k.pe_done, k.act_done, k.dve_done
    steps = nt if center else 0
    with nc.Block() as block:
        @block.tensor
        def _(pe):
            if center:
                for j in range(nt):
                    mm = pe.matmul(k.bank[0][:, :n], k.mean[:, mean, :], src(j), start=j == 0, stop=j == nt - 1)
                mm.then_inc(pe_done.sem, 1)
            for j in range(nt):
                pe.wait_ge(*act_done(j + 1))
                pe.matmul(k.bank[1][:, :n], k.mean[:, mean, :], k.sq[:, j % 3, :n],
                          start=j == 0, stop=j == nt - 1).then_inc(pe_done.sem, 1)

        @block.scalar
        def _(act):
            for j in range(nt):
                if center:
                    act.wait_ge(*dve_done(j + 1))
                if j >= 3:
                    act.wait_ge(*pe_done((1 if center else 0) + j - 2))
                act.activation(k.sq[:, j % 3, :n], dst(j) if center else src(j), ACT.Square
                               ).then_inc(act_done.sem, 1)
            act.wait_ge(*dve_done(steps + 2))
            act.activation(k.rstd[:, :n], k.rstd[:, :n], ACT.Sqrt).then_inc(act_done.sem, 1)
            if post or shift:
                for j in range(nt):
                    act.wait_ge(*dve_done(steps + 3 + j))
                    act.activation(dst(j), dst(j), post or ACT.Identity,
                                   bias=shift(j) if shift else 0.0).then_inc(act_done.sem, 1)

        @block.vector
        def _(dve):
            if center:
                dve.wait_ge(*pe_done(1))
                for j in range(nt):
                    dve.tensor_tensor(dst(j), src(j), k.bank[0][:, :n], ALU.subtract).then_inc(dve_done.sem, 1)
            dve.wait_ge(*pe_done((1 if center else 0) + nt))
            dve.tensor_scalar(k.rstd[:, :n], k.bank[1][:, :n], eps, None, ALU.add).then_inc(dve_done.sem, 1)
            dve.wait_ge(*dve_done(steps + 1))
            dve.reciprocal(k.rstd[:, :n], k.rstd[:, :n]).then_inc(dve_done.sem, 1)
            dve.wait_ge(*act_done(nt + 1))
            for j in range(nt):
                x = dst(j) if center else src(j)
                if gain:
                    dve.scalar_tensor_tensor(dst(j), x, gain(j), k.rstd[:, :n], ALU.mult, ALU.mult
                                             ).then_inc(dve_done.sem, 1)
                else:
                    dve.tensor_tensor(dst(j), x, k.rstd[:, :n], ALU.mult).then_inc(dve_done.sem, 1)
    pe_done.counted((1 if center else 0) + nt)
    act_done.counted(nt * (2 if post or shift else 1) + 1)
    dve_done.counted(steps + 2 + nt)


A_QK = 0
A_V = A_QK + 16 * 512
A_PAD = A_V + 4 * 2048
A_CONV = A_PAD + 8 * 542
A_COS = A_CONV
A_SIN = A_COS + 512
A_TMP = A_SIN + 512
A_DECAY = A_TMP + 2 * 512
A_P = A_DECAY + 2 * 512
ARENA = A_P + 1280


def view(k, at, a, b):
    return k.arena[:, at:at + a * b].rearrange("p (a b) -> p a b", b=b)


def stage_load(k):
    nc, ap = k.nc, k.ap
    wide = k.arena[:, :16 * P].bitcast(I32)
    with nc.Block() as block:
        @block.sync
        def _(sp):
            sp.dma_start(k.vec[:, :], ap["vecs"]).then_inc(k.loaded.sem, 16)
            sp.dma_start(k.X[:, :, LAT:], ap["x_t"].rearrange("(k p) t -> p k t", p=P)).then_inc(k.loaded.sem, 16)
            sp.dma_start(k.X[:, :, :CTX], ap["ctx_t"].rearrange("(k p) t -> p k t", p=P)).then_inc(k.loaded.sem, 16)
            sp.dma_start(k.ident[:, :], ap["ident"]).then_inc(k.loaded.sem, 16)
            sp.dma_start(k.rot[:, :], ap["rot64"]).then_inc(k.loaded.sem, 16)
            sp.dma_start(wide, ap["masks"]).then_inc(k.loaded.sem, 16)
            sp.dma_start(k.tri[:, :, :], ap["tri"]).then_inc(k.loaded.sem, 16)
            sp.dma_start(k.sel[:, :, :], ap["sel"]).then_inc(k.loaded.sem, 16)
            sp.dma_start(k.neg[:, :], ap["neg"]).then_inc(k.loaded.sem, 16)
            sp.wait_ge(*k.loaded(144))

        @block.scalar
        def _(act):
            act.sem_inc(k.evicted.sem, 2)
            act.sem_inc(k.group_done.sem, 2)

        @block.vector
        def _(dve):
            for j, n in enumerate((1024, 256, 128, 1)):
                dve.memset(k.mean[:, j, :], 1.0 / n)
    k.loaded.counted(144)
    k.evicted.counted(2)
    k.group_done.counted(2)
    with nc.Block() as block:
        @block.vector
        def _(dve):
            dve.tensor_copy(k.masks[:, :, :].rearrange("p a b -> p (a b)"), wide)

        @block.scalar
        def _(act):
            act.activation(k.v("c", 0, 8), k.v("c", 0, 8), ACT.Silu)
            act.activation(k.v("cc2", 0, 16), k.v("cc2", 0, 16), ACT.Silu)


def stage_modulation(k, w, groups, n, src, dst, bias):
    def products(pe, i, u):
        for g in range(4):
            for kk in range(DT):
                mm = pe.matmul(k.bank[4 * u][:, g * n:(g + 1) * n], k.W[u][:, kk * 512 + g * P:kk * 512 + (g + 1) * P],
                               src(kk), start=kk == 0, stop=kk == DT - 1)
        return mm

    def evict(dve, i, u):
        at = (2 * i + u) * (4 * n)
        dve.tensor_tensor(dst[:, bass.ds(at, 4 * n)], k.bank[4 * u][:, :4 * n], k.v(bias, at, 4 * n), ALU.add
                          ).then_inc(k.evicted.sem, 1)
    linear(k, w, groups, DT, 512, None, None, dve_evict=evict, products=products)


def stage_gains(k, weight, scale):
    nc = k.nc
    n = len(scale)
    with nc.Block() as block:
        @block.vector
        def _(dve):
            for c, s in enumerate(scale):
                ins = dve.tensor_scalar(k.gain[:, c, :], s, 1.0, None, ALU.add)
                ins.then_inc(k.dve_done.sem, 1)
            if weight is not None:
                for c in range(n):
                    dve.wait_ge(*k.dve_done(c + 1))
                    dve.tensor_tensor(k.gain[:, c, :], k.gain[:, c, :], weight, ALU.mult).then_inc(k.dve_done.sem, 1)
    k.dve_done.counted(n * (2 if weight is not None else 1))


def stage_conv_input(k):
    pad = view(k, A_PAD, DT, 542)

    def act_evict(act, i, u):
        n = 2 * i + u
        act.wait_ge(*k.evicted(2 * i + (u - 1)))
        act.activation(k.stage[:, u, 0, :512], k.bank[4 * u + 1][:, :], ACT.Sigmoid,
                       bias=k.v("b_cgate", n)).then_inc(k.act_done.sem, 1)

    def dve_evict(dve, i, u):
        n = 2 * i + u
        dve.wait_ge(*k.act_done(2 * i + (u + 1)))
        dve.scalar_tensor_tensor(pad[:, bass.ds(n, 1), 30:542].rearrange("p a t -> p (a t)"), k.bank[4 * u][:, :],
                                 k.v("b_cval", n), k.stage[:, u, 0, :512], ALU.add, ALU.mult
                                 ).then_inc(k.evicted.sem, 1)

    def zeros(dve):
        dve.memset(pad[:, :, 0:30], 0.0)
    linear(k, k.ap["w_cpair"], 8, DT, 256, lambda kk, c: k.H[:, kk, LAT:], [(0, 512)],
           act_evict, dve_evict, dve_other=zeros, counts={k.act_done: 8})


def stage_queries_and_conv(k):
    qk = view(k, A_QK, 16, 512)
    pad = view(k, A_PAD, DT, 542)
    conv = view(k, A_CONV, DT, 512)

    def act_evict(act, i, u):
        for g in range(2):
            n = 4 * i + (2 * u + g)
            ins = act.activation(flat(qk[:, bass.ds(n, 1), :]), k.bank[4 * u + g][:, :], ACT.Identity,
                                 bias=k.v("b_qk", n))
        ins.then_inc(k.evicted.sem, 1)

    def dve_conv(dve):
        with dve.Fori(0, DT // 2) as i:
            for tap in range(CONV_K):
                for h in range(2):
                    j = 2 * i + h
                    y, x = flat(conv[:, bass.ds(j, 1), :]), flat(pad[:, bass.ds(j, 1), tap:tap + 512])
                    wt = k.v("conv_w", j * CONV_K + tap)
                    if tap:
                        dve.wait_ge(*k.dve_done(2 * CONV_K * i + (2 * tap + h - 1)))
                        dve.sem_inc(k.dve_turn.sem, 1)
                        dve.scalar_tensor_tensor(y, x, wt, y, ALU.mult, ALU.add).then_inc(k.dve_done.sem, 1)
                    else:
                        dve.tensor_scalar(y, x, wt, k.v("conv_b", j), ALU.mult, ALU.add).then_inc(k.dve_done.sem, 1)
    linear(k, k.ap["w_qk"], 8, DT, 256, lambda kk, c: k.H[:, kk, LAT:], [(0, 512)], act_evict,
           dve_other=dve_conv, counts={k.dve_done: DT * CONV_K})


def stage_values(k):
    v = view(k, A_V, 4, 2048)
    bias = k.stage[0:1, :, :, :].rearrange("p a b c -> p (a b c)")[:, :2048]
    with k.nc.Block() as block:
        @block.sync
        def _(sp):
            sp.dma_start(bias, k.ap["b_v"]).then_inc(k.loaded.sem, 16)
            sp.wait_ge(*k.loaded(16))
    k.loaded.counted(16)

    def products(pe, i, u):
        for t in range(4):
            for kk in range(DT):
                pe.matmul(k.bank[4 * u + t][:, :], k.H[:, kk, LAT + t * P:LAT + (t + 1) * P],
                          k.W[u][:, kk * 512:(kk + 1) * 512], start=kk == 0, stop=False)
            mm = pe.matmul(k.bank[4 * u + t][:, :], k.mean[0:1, 3, :], bias[:, bass.ds((2 * i + u) * 512, 512)],
                           start=False, stop=True)
        return mm

    def act_evict(act, i, u):
        for t in range(4):
            ins = act.activation(v[:, t, bass.ds((2 * i + u) * 512, 512)], k.bank[4 * u + t][:, :], ACT.Copy)
        ins.then_inc(k.evicted.sem, 1)
    linear(k, k.ap["w_v"], 4, DT, 512, None, None, act_evict, products=products)


def stage_rope_tables(k):
    pos = k.arena[:, A_P:A_P + 512]
    posi = k.arena[:, A_P + 512:A_P + 1024].bitcast(I32)
    ang, turns = k.arena[:, A_TMP:A_TMP + 512], k.arena[:, A_TMP + 512:A_TMP + 1024]
    cos, sin = k.arena[:, A_COS:A_COS + 512], k.arena[:, A_SIN:A_SIN + 512]
    TWO_PI = 2 * np.pi
    c1 = 6.28125
    c2 = 0.0019350051879882812
    c3 = float(TWO_PI - c1 - c2)
    magic = float(1.5 * 2 ** 23)
    pi_in = float(np.nextafter(np.float32(np.pi), np.float32(0)))
    d = k.dve_done
    with k.nc.Block() as block:
        @block.sync
        def _(sp):
            sp.dma_start(posi, k.ap["positions_b"]).then_inc(k.loaded.sem, 16)

        @block.vector
        def _(dve):
            def step(ins, n):
                ins.then_inc(d.sem, 1)
                dve.wait_ge(*d(n))
            dve.wait_ge(*k.loaded(16))
            step(dve.tensor_copy(pos, posi), 1)
            step(dve.tensor_scalar(ang, pos, k.v("inv_freq"), None, ALU.mult), 2)
            step(dve.tensor_scalar(turns, ang, float(1 / TWO_PI), None, ALU.mult), 3)
            step(dve.tensor_scalar(turns, turns, magic, None, ALU.add), 4)
            step(dve.tensor_scalar(turns, turns, -magic, None, ALU.add), 5)
            step(dve.scalar_tensor_tensor(ang, turns, -c1, ang, ALU.mult, ALU.add), 6)
            step(dve.scalar_tensor_tensor(ang, turns, -c2, ang, ALU.mult, ALU.add), 7)
            step(dve.scalar_tensor_tensor(ang, turns, -c3, ang, ALU.mult, ALU.add), 8)
            step(dve.tensor_scalar(sin, ang, pi_in, -pi_in, ALU.min, ALU.max), 9)
            step(dve.tensor_scalar(ang, ang, float(np.pi / 2), None, ALU.add), 10)
            step(dve.tensor_scalar(turns, ang, float(np.pi), -float(TWO_PI), ALU.is_gt, ALU.mult), 11)
            step(dve.tensor_tensor(ang, ang, turns, ALU.add), 12)
            step(dve.tensor_scalar(cos, ang, pi_in, -pi_in, ALU.min, ALU.max), 13)

        @block.scalar
        def _(act):
            act.wait_ge(*d(13))
            act.activation(sin, sin, ACT.Sin)
            act.activation(cos, cos, ACT.Sin)
    k.loaded.counted(16)
    d.counted(13)


def stage_retention(k):
    qk = view(k, A_QK, 16, 512)
    v = view(k, A_V, 4, 2048)
    cos, sin = k.arena[:, A_COS:A_COS + 512], k.arena[:, A_SIN:A_SIN + 512]
    tmp = view(k, A_TMP, 2, 512)
    decay = view(k, A_DECAY, 2, 512)
    probs = k.arena[:, A_P:A_P + 1280]
    at = [0, 512, 896, 1152]
    scale = float(P ** -0.5)
    rotated, scored, summed, stats = k.more[0:4]
    roped, weighted, centred, normed = k.more[4:8]
    copied, squared, tabled = k.more[8:11]
    B = k.bank
    with k.nc.Block() as block:
        @block.sync
        def _(sp):
            for h in range(RET_HEADS):
                if h >= 2:
                    sp.wait_ge(*weighted(4 * (h - 1)))
                sp.dma_start(decay[:, h % 2, :], k.ap["decay"][h]).then_inc(tabled.sem, 16)
                sp.wait_ge(*tabled(16 * (h + 1)))

        @block.tensor
        def _(pe):
            for h in range(RET_HEADS):
                if h:
                    pe.wait_ge(*normed(h))
                for s in range(2):
                    mm = pe.matmul(B[s][:, :], k.rot[:, :], qk[:, 2 * h + s, :], start=True, stop=True)
                mm.then_inc(rotated.sem, 1)
                pe.wait_ge(*roped(2 * (h + 1)))
                for j in range(4):
                    pe.matmul(B[2 + j][:, :512 - j * P], qk[:, 2 * h + 1, j * P:(j + 1) * P],
                              qk[:, 2 * h, j * P:], start=True, stop=True).then_inc(scored.sem, 1)
                if h:
                    pe.wait_ge(*copied(2 * h))
                for j in range(4):
                    pe.wait_ge(*weighted(4 * h + j + 1))
                    for e in range(2):
                        mm = pe.matmul(B[6 + e][:, j * P:], v[:, j, h * 256 + e * P:h * 256 + (e + 1) * P],
                                       probs[:, at[j]:at[j] + 512 - j * P], start=j == 0, stop=j == 3)
                mm.then_inc(summed.sem, 1)
                pe.wait_ge(*copied(2 * h + 2))
                for e in range(2):
                    mm = pe.matmul(B[0][:, :], k.mean[:, 1, :], qk[:, 2 * h + e, :], start=e == 0, stop=e == 1)
                mm.then_inc(stats.sem, 1)
                for e in range(2):
                    pe.wait_ge(*squared(2 * h + e + 1))
                    mm = pe.matmul(B[1][:, :], k.mean[:, 1, :], k.sq[:, e, :], start=e == 0, stop=e == 1)
                mm.then_inc(stats.sem, 1)

        @block.scalar
        def _(act):
            for h in range(RET_HEADS):
                act.wait_ge(*summed(h + 1))
                for e in range(2):
                    act.activation(qk[:, 2 * h + e, :], B[6 + e][:, :], ACT.Copy).then_inc(copied.sem, 1)
                for e in range(2):
                    act.wait_ge(*centred(2 * h + e + 1))
                    if h:
                        act.wait_ge(*stats(2 * h))
                    act.activation(k.sq[:, e, :], qk[:, 2 * h + e, :], ACT.Square).then_inc(squared.sem, 1)
                act.wait_ge(*k.dve_done(6 * h + 6))
                act.activation(k.rstd[:, :], k.rstd[:, :], ACT.Sqrt).then_inc(k.act_done.sem, 1)
                act.wait_ge(*normed(h + 1))
                for e in range(2):
                    act.activation(qk[:, 2 * h + e, :], qk[:, 2 * h + e, :], ACT.Identity,
                                   bias=k.v("gn_b", 2 * h + e), scale=k.v("gn_g", 2 * h + e))

        @block.vector
        def _(dve):
            d = k.dve_done
            for h in range(RET_HEADS):
                dve.wait_ge(*rotated(h + 1))
                for s in range(2):
                    x = qk[:, 2 * h + s, :]
                    dve.tensor_tensor(tmp[:, s, :], B[s][:, :], sin, ALU.mult).then_inc(d.sem, 1)
                    dve.tensor_tensor(x, x, cos, ALU.mult).then_inc(d.sem, 1)
                for s in range(2):
                    x = qk[:, 2 * h + s, :]
                    dve.wait_ge(*d(6 * h + 2 * s + 2))
                    dve.tensor_tensor(x, x, tmp[:, s, :], ALU.add).then_inc(roped.sem, 1)
                if h:
                    dve.wait_ge(*summed(h))
                dve.wait_ge(*tabled(16 * (h + 1)))
                for j in range(4):
                    dve.wait_ge(*scored(4 * h + j + 1))
                    dve.scalar_tensor_tensor(probs[:, at[j]:at[j] + 512 - j * P], B[2 + j][:, :512 - j * P], scale,
                                             decay[:, h % 2, :512 - j * P], ALU.mult, ALU.mult
                                             ).then_inc(weighted.sem, 1)
                dve.wait_ge(*stats(2 * h + 1))
                for e in range(2):
                    x = qk[:, 2 * h + e, :]
                    dve.tensor_tensor(x, x, B[0][:, :], ALU.subtract).then_inc(centred.sem, 1)
                dve.wait_ge(*stats(2 * h + 2))
                dve.tensor_scalar(k.rstd[:, :], B[1][:, :], LN_EPS, None, ALU.add).then_inc(d.sem, 1)
                dve.wait_ge(*d(6 * h + 5))
                dve.reciprocal(k.rstd[:, :], k.rstd[:, :]).then_inc(d.sem, 1)
                dve.wait_ge(*k.act_done(h + 1))
                for e in range(2):
                    x = qk[:, 2 * h + e, :]
                    ins = dve.tensor_tensor(x, x, k.rstd[:, :], ALU.mult)
                ins.then_inc(normed.sem, 1)
    n = RET_HEADS
    for s, m in ((k.act_done, n), (rotated, n), (scored, 4 * n), (summed, n), (stats, 2 * n), (roped, 2 * n), (weighted, 4 * n),
                 (centred, 2 * n), (normed, n), (copied, 2 * n), (squared, 2 * n), (tabled, 16 * n), (k.dve_done, 6 * n)):
        s.counted(m)


def stage_gate(k, w, groups, func, bias, dst_at, times):
    dst = view(k, dst_at, 2 * groups, 512)

    def act_evict(act, i, u):
        act.wait_ge(*k.evicted(2 * i + (u - 1)))
        for g in range(2):
            n = 4 * i + (2 * u + g)
            out = k.stage[:, u, g, :512] if times else flat(dst[:, bass.ds(n, 1), :])
            ins = act.activation(out, k.bank[4 * u + g][:, :], func, bias=k.v(bias, n))
        ins.then_inc((k.act_done if times else k.evicted).sem, 1)

    def dve_evict(dve, i, u):
        dve.wait_ge(*k.act_done(2 * i + (u + 1)))
        for g in range(2):
            x = flat(dst[:, bass.ds(4 * i + (2 * u + g), 1), :])
            ins = dve.tensor_tensor(x, x, k.stage[:, u, g, :512], ALU.mult)
        ins.then_inc(k.evicted.sem, 1)
    linear(k, w, groups, DT, 256, lambda kk, c: k.H[:, kk, LAT:], [(0, 512)], act_evict,
           dve_evict if times else None, counts={k.act_done: groups} if times else None)


def stage_conv_out(k):
    m, conv = view(k, A_PAD, DT, 512), view(k, A_CONV, DT, 512)

    def dve_evict(dve, i, u):
        for g in range(2):
            x = flat(m[:, bass.ds(4 * i + (2 * u + g), 1), :])
            ins = dve.tensor_tensor(x, x, k.bank[4 * u + g][:, :], ALU.mult)
        ins.then_inc(k.evicted.sem, 1)
    linear(k, k.ap["w_conv_out"], 4, DT, 256, lambda kk, c: conv[:, kk, :], [(0, 512)], dve_evict=dve_evict)


def stage_retention_out(k):
    m, gate, r = view(k, A_PAD, DT, 512), view(k, A_CONV, DT, 512), view(k, A_QK, 16, 512)

    def dve_evict(dve, i, u):
        for g in range(2):
            n = 4 * i + (2 * u + g)
            x = flat(gate[:, bass.ds(n, 1), :])
            dve.tensor_tensor(x, x, k.bank[4 * u + g][:, :], ALU.mult).then_inc(k.dve_done.sem, 1)
        for g in range(2):
            n = 4 * i + (2 * u + g)
            dve.wait_ge(*k.dve_done(4 * i + (2 * u + g + 1)))
            dve.sem_inc(k.dve_turn.sem, 1)
            ins = dve.tensor_tensor(flat(m[:, bass.ds(n, 1), :]), flat(m[:, bass.ds(n, 1), :]),
                                    flat(gate[:, bass.ds(n, 1), :]), ALU.add)
        ins.then_inc(k.evicted.sem, 1)
    linear(k, k.ap["w_ret_out"], 4, 16, 256, lambda kk, c: r[:, kk, :], [(0, 512)], dve_evict=dve_evict,
           counts={k.dve_done: 8})


def stage_residual(k, w, groups, kt, cols, src, chunks, gate, alpha):
    tiles = cols // P
    nch = len(chunks)

    def tile(n, c):
        a, b = chunks[c]
        return k.X[:, bass.ds(n, 1), a:b].rearrange("p a t -> p (a t)")

    def act_evict(act, i, u):
        for g in range(tiles):
            for c in range(nch):
                n = tiles * (2 * i + u) + g
                ins = act.activation(tile(n, c), tile(n, c), ACT.Copy, scale=alpha)
        ins.then_inc(k.act_done.sem, 1)

    def dve_evict(dve, i, u):
        if alpha != 1.0:
            dve.wait_ge(*k.act_done(2 * i + (u + 1)))
            dve.sem_inc(k.dve_turn.sem, 1)
        for g in range(tiles):
            for c in range(nch):
                n = tiles * (2 * i + u) + g
                a, b = chunks[c]
                ins = dve.scalar_tensor_tensor(tile(n, c), k.bank[4 * u + nch * g + c][:, :b - a],
                                               gate(n, c) if gate else 1.0,
                                               tile(n, c), ALU.mult, ALU.add)
        ins.then_inc(k.evicted.sem, 1)
    linear(k, w, groups, kt, cols, src, chunks, act_evict if alpha != 1.0 else None, dve_evict,
           counts={k.act_done: groups} if alpha != 1.0 else None)


def stage_ffn1_up(k):
    hidden = view(k, 0, FT, 512)
    with k.nc.Block() as block:
        @block.vector
        def _(dve):
            for u in range(2):
                dve.memset(k.stage[:, u, :, 0:2], 0.0)
    taps = view(k, FT * 512, 4, 512)

    def act_evict(act, i, u):
        act.wait_ge(*k.evicted(2 * i + (u - 1)))
        for g in range(2):
            act.activation(k.stage[:, u, g, 2:514], k.bank[4 * u + g][:, :], ACT.Copy).then_inc(k.act_done.sem, 1)
        act.wait_ge(*k.dve_done(12 * i + (6 * u + 6)))
        act.sem_inc(k.act_turn.sem, 1)
        act.activation(k.stage[:, u, 1, 2:514], taps[:, 2 * u + 1, :], ACT.Silu).then_inc(k.act_done.sem, 1)

    def dve_evict(dve, i, u):
        n = 2 * i + u
        dve.wait_ge(*k.act_done(6 * i + (3 * u + 2)))
        dve.sem_inc(k.dve_turn.sem, 1)
        for tap in range(3):
            for g in range(2):
                y, x, wt = taps[:, 2 * u + g, :], k.stage[:, u, g, tap:tap + 512], k.v("ffn_w", n * 6 + (3 * g + tap))
                if tap:
                    dve.wait_ge(*k.dve_done(12 * i + (6 * u + 2 * tap + g - 1)))
                    dve.sem_inc(k.dve_turn.sem, 1)
                    dve.scalar_tensor_tensor(y, x, wt, y, ALU.mult, ALU.add).then_inc(k.dve_done.sem, 1)
                else:
                    dve.tensor_scalar(y, x, wt, k.v("ffn_b", n * 2 + g), ALU.mult, ALU.add
                                      ).then_inc(k.dve_done.sem, 1)
        dve.wait_ge(*k.act_done(6 * i + (3 * u + 3)))
        dve.sem_inc(k.dve_turn.sem, 1)
        dve.tensor_tensor(flat(hidden[:, bass.ds(n, 1), :]), taps[:, 2 * u, :], k.stage[:, u, 1, 2:514], ALU.mult
                          ).then_inc(k.evicted.sem, 1)
    linear(k, k.ap["w_up"], FT, DT, 256, lambda kk, c: k.H[:, kk, LAT:], [(0, 512)], act_evict, dve_evict,
           counts={k.act_done: 3 * FT, k.dve_done: 6 * FT})


def x_lat(k):
    return lambda j: k.X[:, j, LAT:]


def block_one(k):
    ap = k.ap
    h = lambda j: k.H[:, j, LAT:]
    stage_modulation(k, ap["w_ada"], 12, 1, lambda kk: k.v("c", kk), k.mod1, "b_ada")
    stage_gains(k, None, [k.mod1[:, 8:16]])
    norm(k, x_lat(k), h, DT, LAT, TOK, 0, LN_EPS, True, lambda j: k.gain[:, 0, j:j + 1],
         shift=lambda j: k.mod1[:, j:j + 1])
    stage_conv_input(k)
    stage_queries_and_conv(k)
    stage_values(k)
    conv = view(k, A_CONV, DT, 512)
    norm(k, lambda j: conv[:, j, :], lambda j: conv[:, j, :], DT, 0, 512, 0, LN_EPS, True,
         lambda j: k.v("cln_g", j), post=ACT.Silu, shift=lambda j: k.v("cln_b", j))
    stage_gate(k, ap["w_ga"], 4, ACT.Sigmoid, "b_ga", A_PAD, False)
    stage_conv_out(k)
    stage_rope_tables(k)
    stage_retention(k)
    stage_gate(k, ap["w_g"], 8, ACT.Silu, "b_g", A_QK, True)
    stage_gate(k, ap["w_gb"], 4, ACT.Sigmoid, "b_gb", A_CONV, False)
    stage_retention_out(k)
    m = view(k, A_PAD, DT, 512)
    stage_residual(k, ap["w_out"], 4, DT, 256, lambda kk, c: m[:, kk, :], [(LAT, TOK)],
                   lambda n, c: k.mod1[:, bass.ds(16 + n, 1)], ALPHA)
    norm(k, x_lat(k), x_lat(k), DT, LAT, TOK, 0, LN_EPS, True, lambda j: k.v("ln1_g", j),
         shift=lambda j: k.v("ln1_b", j))
    stage_gains(k, None, [k.mod1[:, 32:40]])
    norm(k, x_lat(k), h, DT, LAT, TOK, 0, LN_EPS, True, lambda j: k.gain[:, 0, j:j + 1],
         shift=lambda j: k.mod1[:, 24 + j:25 + j])
    stage_ffn1_up(k)
    hidden = view(k, 0, FT, 512)
    stage_residual(k, ap["w_down"], 8, FT, P, lambda kk, c: hidden[:, kk, :], [(LAT, TOK)],
                   lambda n, c: k.mod1[:, bass.ds(40 + n, 1)], ALPHA)
    norm(k, x_lat(k), x_lat(k), DT, LAT, TOK, 0, LN_EPS, True, lambda j: k.v("ln2_g", j),
         shift=lambda j: k.v("ln2_b", j))


HEADS2 = 4
CH = 2 * 64
NCH = TOK // CH
M2_QG = 0
M2_F = M2_QG + 8 * 512
M2_V = M2_F + 8 * TOK
M2_OUT = M2_V + 2 * NCH * 512
M2_WORK = M2_OUT + 8 * 512
ML_QP = 0
ML_KC = ML_QP + 4 * 660
ML_Q = ML_KC + 2 * 258
ML_K = ML_Q + 2 * 512
ML_O = ML_K + 2 * TOK
ML_RAW = M2_WORK
ML_ROWS = ML_O + 4 * 512


def chunks_both():
    return [(0, CTX), (LAT, TOK)]


def stage_swiglu(k, w, src, chunks, hidden, func=None):
    widths = [b - a for a, b in chunks]
    at = [0, widths[0]]
    nch = len(chunks)

    def act_evict(act, i, u):
        act.wait_ge(*k.evicted(2 * i + (u - 1)))
        s = flat(k.stage[:, u, :, :])
        for c in range(nch):
            ins = act.activation(s[:, at[c]:at[c] + widths[c]], k.bank[4 * u + c][:, :widths[c]], ACT.Silu)
        ins.then_inc(k.act_done.sem, 1)

    def dve_evict(dve, i, u):
        dve.wait_ge(*k.act_done(2 * i + (u + 1)))
        s = flat(k.stage[:, u, :, :])
        for c in range(nch):
            h = flat(hidden[:, bass.ds(2 * i + u, 1), at[c]:at[c] + widths[c]])
            ins = dve.tensor_tensor(h, s[:, at[c]:at[c] + widths[c]], k.bank[4 * u + nch + c][:, :widths[c]], ALU.mult)
        ins.then_inc(k.evicted.sem, 1)
    linear(k, w, FT, DT, 256, src, chunks, act_evict, dve_evict, counts={k.act_done: FT})


def stage_half_gates(k, gates):
    with k.nc.Block() as block:
        @block.vector
        def _(dve):
            for c, g in enumerate(gates):
                dve.tensor_scalar(k.gain[:, c, :], g, 0.5, None, ALU.mult)


def stage_token_values(k, w, sets, tiles, first, dst, last_rows=P):
    nc = k.nc
    n = sets * tiles
    with nc.Block() as block:
        @block.sync
        def _(sp):
            for s in range(sets):
                sp.dma_start(k.W[s][:, :SLOT], w[s]).then_inc(k.weights_in[s].sem, 16)

        @block.tensor
        def _(pe):
            for m in range(n):
                s, t = divmod(m, tiles)
                rows = last_rows if t == tiles - 1 else P
                if t == 0:
                    pe.wait_ge(*k.weights_in[s](16))
                if m >= 8:
                    pe.wait_ge(*k.act_done(m - 7))
                for kk in range(DT):
                    mm = pe.matmul(k.bank[m % 8][:rows, :], k.H[:, kk, first + t * P:first + t * P + rows],
                                   k.W[s][:, kk * 512:(kk + 1) * 512], start=kk == 0, stop=kk == DT - 1)
                mm.then_inc(k.pe_done.sem, 1)

        @block.scalar
        def _(act):
            for m in range(n):
                s, t = divmod(m, tiles)
                rows = last_rows if t == tiles - 1 else P
                act.wait_ge(*k.pe_done(m + 1))
                act.activation(dst(s, t)[:rows], k.bank[m % 8][:rows, :], ACT.Copy).then_inc(k.act_done.sem, 1)
    for s in range(sets):
        k.weights_in[s].counted(16)
    k.pe_done.counted(n)
    k.act_done.counted(n)


def stage_hgrn(k):
    qg = view(k, M2_QG, 8, 512)
    fpre = view(k, M2_F, 8, TOK)
    val = k.arena[:, M2_V:M2_V + 2 * NCH * 512].rearrange("p (s t e) -> p s t e", s=2, t=NCH)
    out = view(k, M2_OUT, 8, 512)
    pre = k.arena[:, M2_WORK:M2_WORK + TOK]
    key = k.arena[:, M2_WORK + TOK:M2_WORK + 2 * TOK]
    suf = k.arena[:, M2_WORK + 2 * TOK:M2_WORK + 3 * TOK]
    both = view(k, M2_WORK + 3 * TOK, 2, 512)
    score = k.sq
    spare = k.stage[:, :, :, :].rearrange("p a b c -> p (a b c)")
    key_t = spare[:, 0:TOK].rearrange("p (c d) -> p c d", d=P)
    state = spare[:, TOK:2 * TOK].rearrange("p (c d) -> p c d", d=P)
    gated, ready, scored, merged, turned, turn_copied, kv_done, states, summed, taken = k.more[0:10]
    B = k.bank
    units = [(h, d) for h in range(HEADS2) for d in range(2)]
    order = [[0, 1, 2, 3, 4, 5], [1, 0, 5, 4, 3, 2]]
    levels = 7
    with k.nc.Block() as block:
        @block.vector
        def _(dve):
            for d in range(2):
                dve.memset(score[:, d, :], 0.0)
            dve.tensor_tensor(k.v("lb1", 0, 8), k.v("lb0", 0, 8), k.v("lb1", 0, 8), ALU.subtract
                              ).then_inc(k.dve_done.sem, 1)
            dve.wait_ge(*k.act_done(1))
            dve.tensor_scalar(k.v("lb1", 0, 8), k.v("lb0", 0, 8), -1.0, 1.0, ALU.mult, ALU.add)

        @block.scalar
        def _(act):
            act.wait_ge(*k.dve_done(1))
            act.activation(k.v("lb0", 0, 8), k.v("lb1", 0, 8), ACT.Sigmoid).then_inc(k.act_done.sem, 1)
    k.dve_done.counted(1)
    k.act_done.counted(1)
    links = []
    with k.nc.Block() as block:
        @block.scalar
        def _(act):
            for n, (h, d) in enumerate(units):
                if n:
                    act.wait_ge(*taken(n))
                act.activation(pre, fpre[:, 2 * h + d, :], ACT.Sigmoid)
                act.activation(key, fpre[:, 2 * h + d, :], ACT.Sigmoid, scale=-1.0).then_inc(gated.sem, 1)
                act.wait_ge(*turned(n + 1))
                act.activation(flat(key_t[:, 0:4, :]), B[4][:, :], ACT.Copy)
                act.activation(flat(key_t[:, 4:6, :]), B[5][:, :256], ACT.Copy).then_inc(turn_copied.sem, 1)

        @block.tensor
        def _(pe):
            for n, (h, d) in enumerate(units):
                pe.wait_ge(*ready(9 * n + 1))
                for lev in range(levels + 1):
                    if lev:
                        pe.wait_ge(*ready(9 * n + lev + 1))
                    if 8 * n + lev >= 4:
                        pe.wait_ge(*merged(8 * n + lev - 3))
                    for c in range(4):
                        t = slice(c * CH, (c + 1) * CH)
                        kx = key[:, CTX + c * CH:CTX + (c + 1) * CH] if lev == 0 else both[:, lev % 2, t]
                        qx = qg[:, h, t] if lev == 0 else both[:, lev % 2, t]
                        mm = pe.matmul(B[lev % 4][:, t], kx, qx, start=True, stop=True)
                    mm.then_inc(scored.sem, 1)
                pe.wait_ge(*ready(9 * n + 9))
                if n:
                    pe.wait_ge(*taken(n))
                for c in range(NCH):
                    mm = pe.transpose(B[4 + c // 4][:, (c % 4) * P:(c % 4 + 1) * P], key[:, c * CH:(c + 1) * CH],
                                      k.ident[:, :])
                mm.then_inc(turned.sem, 1)
                pe.wait_ge(*turn_copied(n + 1))
                for c in range(NCH):
                    mm = pe.matmul(B[6 + c // 4][:, (c % 4) * P:(c % 4 + 1) * P], key_t[:, c, :],
                                   val[:, 0, c, h * P:(h + 1) * P], start=True, stop=True)
                mm.then_inc(kv_done.sem, 1)
                pe.wait_ge(*merged(8 * n + 8))
                pe.wait_ge(*states(n + 1))
                for i in range(2, NCH):
                    c = order[d][i]
                    t = slice((c - 2) * CH, (c - 1) * CH)
                    pe.matmul(B[4][:, t], val[:, 0, c, h * P:(h + 1) * P], score[:, d, t], start=True, stop=False)
                    mm = pe.matmul(B[4][:, t], state[:, i, :], both[:, 0, t], start=False, stop=True)
                mm.then_inc(summed.sem, 1)

        @block.vector
        def _(dve):
            d_ = k.dve_done

            def link(ins):
                links.append(1)
                ins.then_inc(d_.sem, 1)
                dve.wait_ge(*d_(len(links)))
            for n, (h, d) in enumerate(units):
                one = k.v("lb1", 4 * d + h)
                dve.wait_ge(*gated(n + 1))
                dve.tensor_scalar(pre, pre, one, k.v("lb0", 4 * d + h), ALU.mult, ALU.add)
                dve.memset(suf, 1.0)
                link(dve.tensor_scalar(key, key, one, None, ALU.mult))
                dve.sem_inc(ready.sem, 1)
                qh, kh = 1 - d, d

                def merge(lev):
                    dve.wait_ge(*scored(8 * n + lev + 1))
                    dve.copy_predicated(score[:, d, :].rearrange("p (c t) -> p c t", t=CH),
                                        k.masks[:, 8 * d + lev:8 * d + lev + 1, :].to_broadcast([P, 4, CH]),
                                        B[lev % 4][:, :].rearrange("p (c t) -> p c t", t=CH)).then_inc(merged.sem, 1)
                for lev in range(1, levels + 1):
                    m = 1 << (lev - 1)
                    edge = m - 1 if d == 0 else 0

                    def halves(ap):
                        return ap.rearrange("p (b s m) -> p b s m", s=2, m=m)
                    x = halves(both[:, lev % 2, :])
                    q4, p4, s4, k4 = halves(qg[:, h, :]), halves(pre), halves(suf), halves(key)
                    nctx = CTX // (2 * m)
                    if lev > 2:
                        dve.wait_ge(*scored(8 * n + lev - 1))
                    dve.tensor_tensor(x[:, :, qh, :], q4[:, :, qh, :], p4[:, nctx:, qh, :], ALU.mult)
                    link(dve.tensor_tensor(x[:, :, kh, :], k4[:, nctx:, kh, :], s4[:, nctx:, kh, :], ALU.mult))
                    dve.sem_inc(ready.sem, 1)
                    nb = TOK // (2 * m)
                    link(dve.tensor_tensor(s4[:, :, kh, :], s4[:, :, kh, :],
                                           p4[:, :, qh, edge:edge + 1].to_broadcast([P, nb, m]), ALU.mult))
                    link(dve.tensor_tensor(p4[:, :, qh, :], p4[:, :, qh, :],
                                           p4[:, :, kh, edge:edge + 1].to_broadcast([P, nb, m]), ALU.mult))
                    merge(lev - 1)
                dve.wait_ge(*scored(8 * n + levels))
                dve.tensor_tensor(both[:, 0, :], qg[:, h, :], pre[:, CTX:], ALU.mult)
                link(dve.tensor_tensor(key, key, suf, ALU.mult))
                dve.sem_inc(ready.sem, 1)
                merge(levels)
                dve.wait_ge(*kv_done(n + 1))
                for i in range(1, NCH):
                    c = order[d][i - 1]
                    kv = B[6 + c // 4][:, (c % 4) * P:(c % 4 + 1) * P]
                    at = c * CH + (CH - 1 if d == 0 else 0)
                    if i == 1:
                        link(dve.tensor_copy(state[:, i, :], kv))
                    else:
                        link(dve.scalar_tensor_tensor(state[:, i, :], state[:, i - 1, :], pre[:, at:at + 1], kv,
                                                      ALU.mult, ALU.add))
                dve.sem_inc(states.sem, 1)
                dve.wait_ge(*summed(n + 1))
                if d == 0:
                    link(dve.tensor_scalar(out[:, h, :], B[4][:, :], float(P ** -0.5), None, ALU.mult))
                else:
                    link(dve.scalar_tensor_tensor(out[:, h, :], B[4][:, :], float(P ** -0.5), out[:, h, :],
                                                  ALU.mult, ALU.add))
                dve.sem_inc(taken.sem, 1)
    n = len(units)
    for s, m in ((gated, n), (ready, 9 * n), (scored, 8 * n), (merged, 8 * n), (turned, n), (turn_copied, n),
                 (kv_done, n), (states, n), (summed, n), (taken, n), (k.dve_done, len(links))):
        s.counted(m)


def stage_head_norms(k, at, weight, gates):
    out = view(k, M2_OUT, 8, 512)
    for h in range(HEADS2):
        norm(k, lambda j, h=h: out[:, at + h, :], lambda j, h=h: out[:, at + h, :], 1, 0, 512, 2, RMS_EPS, False,
             lambda j, h=h: k.v(weight, h))
    with k.nc.Block() as block:
        @block.vector
        def _(dve):
            for h in range(HEADS2):
                dve.tensor_tensor(out[:, at + h, :], out[:, at + h, :], gates[:, h, :], ALU.mult)


def grid(ap):
    return ap.rearrange("p (r c) -> p r c", c=64)


def stage_mlstm_inputs(k):
    pads = k.arena[:, ML_QP:ML_QP + 4 * 660].rearrange("p (t r c) -> p t r c", t=4, c=66)
    kctx = view(k, ML_KC, 2, 258)
    mq, mk = view(k, ML_Q, 2, 512), view(k, ML_K, 2, TOK)
    osig = view(k, ML_O, 4, 512)
    raw = view(k, ML_RAW, 4, TOK)
    src = lambda kk, c: k.H[:, kk, slice(*chunks_both()[c])]
    with k.nc.Block() as block:
        @block.vector
        def _(dve):
            dve.memset(k.arena[:, ML_QP:ML_Q], 0.0)

    def act_evict(act, i, u):
        for g in range(2):
            ins = act.activation(pads[:, 2 * u + g, 1:9, 1:65], grid(k.bank[4 * u + 2 * g + 1][:, :]), ACT.Copy)
            if u == 1:
                ins = act.activation(kctx[:, g, 1:257], k.bank[4 * u + 2 * g][:, :CTX], ACT.Copy)
        ins.then_inc(k.evicted.sem, 1)
    linear(k, k.ap["w_mqk"], 2, DT, 256, src, chunks_both(), act_evict)

    def o_evict(act, i, u):
        for g in range(2):
            ins = act.activation(flat(osig[:, bass.ds(4 * i + (2 * u + g), 1), :]), k.bank[4 * u + g][:, :], ACT.Sigmoid)
        ins.then_inc(k.evicted.sem, 1)

    def conv(dve):
        outs = [grid(mq[:, 0, :]), grid(mq[:, 1, :]), grid(mk[:, 0, CTX:]), grid(mk[:, 1, CTX:])]
        d = k.dve_done
        for tap in range(9):
            dy, dx = divmod(tap, 3)
            for t in range(4):
                x = pads[:, t, dy:dy + 8, dx:dx + 64]
                if tap:
                    dve.wait_ge(*d(4 * (tap - 1) + t + 1))
                    dve.scalar_tensor_tensor(outs[t], x, k.v("mconv_w", 9 * t + tap), outs[t], ALU.mult, ALU.add
                                             ).then_inc(d.sem, 1)
                else:
                    dve.tensor_scalar(outs[t], x, k.v("mconv_w", 9 * t), k.v("mconv_b", t), ALU.mult, ALU.add
                                      ).then_inc(d.sem, 1)
        for dx in range(3):
            for t in range(2):
                y, x, w = mk[:, t, :CTX], kctx[:, t, dx:dx + CTX], k.v("mconv_w", 9 * (2 + t) + 3 + dx)
                if dx:
                    dve.wait_ge(*d(36 + 2 * (dx - 1) + t + 1))
                    dve.scalar_tensor_tensor(y, x, w, y, ALU.mult, ALU.add).then_inc(d.sem, 1)
                else:
                    dve.tensor_scalar(y, x, w, k.v("mconv_b", 2 + t), ALU.mult, ALU.add).then_inc(d.sem, 1)
    linear(k, k.ap["w_mo"], 2, DT, 256, lambda kk, c: k.H[:, kk, LAT:], [(0, 512)], o_evict, dve_other=conv,
           counts={k.dve_done: 42})
    with k.nc.Block() as block:
        @block.sync
        def _(sp):
            sp.dma_start(k.W[0][:, :DT * P], k.ap["w_gates"]).then_inc(k.weights_in[0].sem, 16)

        @block.tensor
        def _(pe):
            pe.wait_ge(*k.weights_in[0](16))
            for c, (a, b) in enumerate(chunks_both()):
                for kk in range(DT):
                    mm = pe.matmul(k.bank[c][:, :b - a], k.W[0][:, kk * P:(kk + 1) * P], k.H[:, kk, a:b],
                                   start=kk == 0, stop=kk == DT - 1)
            mm.then_inc(k.pe_done.sem, 1)

        @block.scalar
        def _(act):
            for t in range(2):
                act.activation(mq[:, t, :], mq[:, t, :], ACT.Silu)
                act.activation(mk[:, t, :], mk[:, t, :], ACT.Silu)
            act.wait_ge(*k.pe_done(1))
            for g in range(4):
                for c, (a, b) in enumerate(chunks_both()):
                    act.activation(raw[0:4, g, a:b], k.bank[c][32 * g:32 * g + 4, :b - a], ACT.Identity,
                                   bias=k.v("ml_gb")[32 * g:32 * g + 4])
    k.weights_in[0].counted(16)
    k.pe_done.counted(1)


def stage_mlstm(k):
    mq, mk = view(k, ML_Q, 2, 512), view(k, ML_K, 2, TOK)
    raw = view(k, ML_RAW, 4, TOK)
    val = k.arena[:, M2_V:M2_V + 2 * NCH * 512].rearrange("p (s t e) -> p s t e", s=2, t=NCH)
    out = view(k, M2_OUT, 8, 512)
    free = k.H[:, :, :].rearrange("p k t -> p (k t)")
    run = free[:, 0:2 * TOK].rearrange("p (d t) -> p d t", t=TOK)
    top = free[:, 2 * TOK:4 * TOK].rearrange("p (d t) -> p d t", t=TOK)
    ones = free[:, 4 * TOK:5 * TOK]
    soft = free[:, 5 * TOK:6 * TOK]
    a_t = free[:, 6 * TOK:6 * TOK + 48].rearrange("p (d c h) -> p d c h", d=2, h=4)
    negm = k.rstd
    wts = k.sq
    prob = k.stage[:, 0, :, :]
    absd = k.stage[:, 1, 0, :512]
    part = k.stage[:, 1, 1, :512]
    B = k.bank
    d_ = k.dve_done
    steps = []
    with k.nc.Block() as block:
        @block.scalar
        def _(act):
            a = 0
            for d in range(2):
                f = raw[0:4, 2 * d + 1, :]
                if d:
                    act.wait_ge(*d_(2))
                for n, (func, scale, bias, x) in enumerate(((ACT.Abs, 1.0, 0.0, f), (ACT.Exp, -1.0, 0.0, soft[0:4]),
                                                            (ACT.Ln, 1.0, 1.0, soft[0:4]))):
                    act.activation(soft[0:4], x, func, scale=scale, bias=bias).then_inc(k.act_done.sem, 1)
                    a += 1
                    act.wait_ge(*k.act_done(a))

        @block.vector
        def _(dve):
            def link(ins):
                steps.append(1)
                ins.then_inc(d_.sem, 1)
                dve.wait_ge(*d_(len(steps)))
            link(dve.memset(ones[0:4], 1.0))
            for d in range(2):
                dve.wait_ge(*k.act_done(3 * (d + 1)))
                f = raw[0:4, 2 * d + 1, :]
                link(dve.scalar_tensor_tensor(f, f, 0.0, soft[0:4], ALU.min, ALU.subtract))
            for d in range(2):
                i, f, b, m = raw[0:4, 2 * d, :], raw[0:4, 2 * d + 1, :], run[0:4, d, :], top[0:4, d, :]
                if d == 0:
                    link(dve.tensor_tensor_scan(b, ones[0:4], f, 0.0, ALU.mult, ALU.add))
                else:
                    link(dve.tensor_tensor_scan(b[:, CTX - 1::-1], ones[0:4, :CTX], f[:, CTX - 1::-1], 0.0,
                                                ALU.mult, ALU.add))
                    link(dve.tensor_tensor_scan(b[:, TOK - 1:CTX - 1:-1], ones[0:4, CTX:], f[:, TOK - 1:CTX - 1:-1],
                                                b[:, 0:1], ALU.mult, ALU.add))
                link(dve.tensor_tensor(i, i, b, ALU.subtract))
                if d == 0:
                    link(dve.tensor_tensor_scan(m, i, i, -3.0e38, ALU.max, ALU.max))
                else:
                    link(dve.tensor_tensor_scan(m[:, CTX - 1::-1], i[:, CTX - 1::-1], i[:, CTX - 1::-1], -3.0e38,
                                                ALU.max, ALU.max))
                    link(dve.tensor_tensor_scan(m[:, TOK - 1:CTX - 1:-1], i[:, TOK - 1:CTX - 1:-1],
                                                i[:, TOK - 1:CTX - 1:-1], m[:, 0:1], ALU.max, ALU.max))
                link(dve.tensor_tensor(b, b, m, ALU.add))
                link(dve.tensor_scalar(b, b, -80.0, None, ALU.max))
    k.act_done.counted(6)
    d_.counted(len(steps))
    with k.nc.Block() as block:
        @block.tensor
        def _(pe):
            for d in range(2):
                for c in range(NCH):
                    mm = pe.transpose(B[0][:, (d * NCH + c) * 4:(d * NCH + c + 1) * 4],
                                      raw[0:4, 2 * d, c * P:(c + 1) * P], k.ident[0:4, 0:4])
            mm.then_inc(k.pe_done.sem, 1)

        @block.scalar
        def _(act):
            for d in range(2):
                act.activation(run[0:4, d, :], run[0:4, d, :], ACT.Exp, scale=-1.0)

        @block.vector
        def _(dve):
            dve.wait_ge(*k.pe_done(1))
            dve.tensor_copy(a_t.rearrange("p d c h -> p (d c h)"), B[0][:, :48])
    k.pe_done.counted(1)

    units = [(h, d) for h in range(HEADS2) for d in range(2)]
    spread, negated, clipped, weighed, scored, probed, summed, absolute, finished = k.more[0:9]

    def span(j, d):
        if j < 2:
            return 0, 512, None
        t = j - 2
        return (t * P, 512, t * P) if d == 0 else (0, (t + 1) * P, t * P)
    with k.nc.Block() as block:
        @block.tensor
        def _(pe):
            def sums(pe, n, h, d, j):
                lo, hi, _ = span(j, d)
                pe.wait_ge(*probed(6 * n + j + 1))
                pe.matmul(B[4][:, lo:hi], val[:, 1, j, h * P:(h + 1) * P], prob[:, j % 2, lo:hi],
                          start=j == 0, stop=j == NCH - 1)
                pe.matmul(B[5][:, lo:hi], k.mean[:, 3, :], prob[:, j % 2, lo:hi],
                          start=j == 0, stop=j == NCH - 1).then_inc(summed.sem, 1)
            for n, (h, d) in enumerate(units):
                if n:
                    pe.wait_ge(*finished(n))
                pe.matmul(B[0][:, :], k.sel[0:4, h, :], top[0:4, d, CTX:], start=True, stop=True)
                pe.matmul(B[1][:, :], k.sel[0:4, h, :], run[0:4, d, CTX:], start=True, stop=True
                          ).then_inc(spread.sem, 1)
                r = slice(64 * (h % 2), 64 * (h % 2) + 64)
                for j in range(NCH):
                    lo, hi, _ = span(j, d)
                    if 6 * n + j >= 2:
                        pe.wait_ge(*probed(6 * n + j - 1))
                    pe.matmul(B[2 + j % 2][:, lo:hi], mk[r, h // 2, j * P:(j + 1) * P], mq[r, h // 2, lo:hi],
                              start=True, stop=True).then_inc(scored.sem, 1)
                    if j:
                        sums(pe, n, h, d, j - 1)
                sums(pe, n, h, d, NCH - 1)

        @block.scalar
        def _(act):
            for n, (h, d) in enumerate(units):
                act.wait_ge(*spread(n + 1))
                if n:
                    act.wait_ge(*weighed(6 * n))
                    act.wait_ge(*clipped(4 * n))
                act.activation(negm[:, :], B[0][:, :], ACT.Copy, scale=-1.0).then_inc(negated.sem, 1)
                act.wait_ge(*negated(n + 1))
                for j in range(NCH):
                    lo, hi, dg = span(j, d)
                    if 6 * n + j >= 2 and dg is None:
                        act.wait_ge(*probed(6 * n + j - 1))
                    bias = a_t[:, d, j, h:h + 1]
                    w = wts[:, j % 2, :]
                    if dg is None:
                        act.activation(w, negm[:, :], ACT.Exp, bias=bias).then_inc(weighed.sem, 1)
                        continue
                    act.wait_ge(*clipped(4 * n + j - 1))
                    rest = (dg + P, hi) if d == 0 else (lo, dg)
                    if rest[1] > rest[0]:
                        act.activation(w[:, rest[0]:rest[1]], negm[:, rest[0]:rest[1]], ACT.Exp, bias=bias)
                    act.activation(w[:, dg:dg + P], w[:, dg:dg + P], ACT.Exp).then_inc(weighed.sem, 1)
                act.wait_ge(*summed(6 * (n + 1)))
                if n:
                    act.wait_ge(*finished(n))
                act.activation(absd, B[5][:, :], ACT.Abs).then_inc(absolute.sem, 1)

        @block.vector
        def _(dve):
            chain = []

            def link(ins):
                chain.append(1)
                ins.then_inc(d_.sem, 1)
                dve.wait_ge(*d_(len(chain)))
            for n, (h, d) in enumerate(units):
                dve.wait_ge(*negated(n + 1))
                for j in range(NCH):
                    lo, hi, dg = span(j, d)
                    w, p = wts[:, j % 2, :], prob[:, j % 2, :]
                    if 6 * n + j >= 2:
                        dve.wait_ge(*probed(6 * n + j - 1))
                    if dg is not None:
                        dve.tensor_scalar(w[:, dg:dg + P], negm[:, dg:dg + P], a_t[:, d, j, h:h + 1], 0.0,
                                          ALU.add, ALU.min).then_inc(clipped.sem, 1)
                    dve.wait_ge(*scored(6 * n + j + 1))
                    dve.wait_ge(*weighed(6 * n + j + 1))
                    if 6 * n + j >= 2:
                        dve.wait_ge(*summed(6 * n + j - 1))
                    ins = dve.scalar_tensor_tensor(p[:, lo:hi], B[2 + j % 2][:, lo:hi], 0.125, w[:, lo:hi],
                                                   ALU.mult, ALU.mult)
                    if dg is not None:
                        link(ins)
                        ins = dve.tensor_tensor(p[:, dg:dg + P], p[:, dg:dg + P], k.tri[:, d, :], ALU.mult)
                    ins.then_inc(probed.sem, 1)
                dve.wait_ge(*absolute(n + 1))
                link(dve.tensor_tensor(absd, absd, B[1][:, :], ALU.max))
                link(dve.reciprocal(absd, absd))
                o = out[:, 4 + h, :]
                if d == 0:
                    dve.tensor_tensor(o, B[4][:, :], absd, ALU.mult).then_inc(finished.sem, 1)
                else:
                    link(dve.tensor_tensor(part, B[4][:, :], absd, ALU.mult))
                    dve.tensor_tensor(o, o, part, ALU.add).then_inc(finished.sem, 1)
            steps[:] = chain
    n = len(units)
    for s, m in ((spread, n), (negated, n), (clipped, 4 * n), (weighed, 6 * n), (scored, 6 * n), (probed, 6 * n),
                 (summed, 6 * n), (absolute, n), (finished, n), (d_, len(steps))):
        s.counted(m)


def stage_second_inputs(k):
    qg = view(k, M2_QG, 8, 512)
    fpre = view(k, M2_F, 8, TOK)
    val = k.arena[:, M2_V:M2_V + 2 * NCH * 512].rearrange("p (s t e) -> p s t e", s=2, t=NCH)

    def qg_evict(act, i, u):
        for g in range(2):
            ins = act.activation(flat(qg[:, bass.ds(4 * i + (2 * u + g), 1), :]), k.bank[4 * u + g][:, :], ACT.Silu)
        ins.then_inc(k.evicted.sem, 1)

    def f_evict(act, i, u):
        for g in range(2):
            for c, (a, b) in enumerate(chunks_both()):
                ins = act.activation(flat(fpre[:, bass.ds(4 * i + (2 * u + g), 1), a:b]),
                                     k.bank[4 * u + 2 * g + c][:, :b - a], ACT.Copy)
        ins.then_inc(k.evicted.sem, 1)
    linear(k, k.ap["w_qg2"], 4, DT, 256, lambda kk, c: k.H[:, kk, LAT:], [(0, 512)], qg_evict)
    linear(k, k.ap["w_f2"], 4, DT, 256, lambda kk, c: k.H[:, kk, slice(*chunks_both()[c])], chunks_both(), f_evict)
    stage_token_values(k, k.ap["w_v2"], 2, NCH, 0, lambda s, t: val[:, s, t, :])


def block_two(k):
    ap = k.ap
    both = chunks_both()

    def modulated(weight, m, parts):
        stage_gains(k, k.v(weight, 0, 8), [k.mod2[:, m + 8:m + 16, w] for w in parts])
        for w in parts:
            a, b = both[1 - w]
            norm(k, lambda j: k.X[:, j, a:b], lambda j: k.H[:, j, a:b], DT, a, b, 0, RMS_EPS, False,
                 lambda j: k.gain[:, w, j:j + 1], shift=lambda j: k.mod2[:, m + j:m + j + 1, w])
    stage_modulation(k, ap["w_mod"], 18, 2, lambda kk: k.v("cc2", 2 * kk, 2),
                     k.mod2[:, :, :].rearrange("p a b -> p (a b)"), "b_mod")
    modulated("norm1", 0, (0, 1))
    hidden = view(k, 0, FT, TOK)
    src = lambda kk, c: k.H[:, kk, slice(*both[c])]
    stage_swiglu(k, ap["ffn1_w1"], src, both, hidden)
    stage_half_gates(k, [k.mod2[:, 16:24, 1], k.mod2[:, 16:24, 0]])
    stage_residual(k, ap["ffn1_w2"], 8, FT, P, lambda kk, c: hidden[:, kk, slice(*both[c])], both,
                   lambda n, c: k.gain[:, c, bass.ds(n, 1)], 1.0)
    modulated("norm2", 24, (0, 1))
    stage_second_inputs(k)
    stage_hgrn(k)
    stage_head_norms(k, 0, "hg_norm", view(k, M2_QG + 4 * 512, 4, 512))
    stage_mlstm_inputs(k)
    stage_mlstm(k)
    stage_head_norms(k, 4, "ml_norm", view(k, ML_O, 4, 512))
    out = view(k, M2_OUT, 8, 512)
    stage_residual(k, ap["w_out2"], 4, DT, 256, lambda kk, c: out[:, kk, :], [(LAT, TOK)],
                   lambda n, c: k.mod2[:, bass.ds(40 + n, 1), 0], 1.0)
    modulated("norm3", 48, (0,))
    hidden = view(k, 0, FT, 512)
    stage_swiglu(k, ap["ffn2_w1"], lambda kk, c: k.H[:, kk, LAT:], [(0, 512)], hidden)
    stage_half_gates(k, [k.mod2[:, 64:72, 0]])
    stage_residual(k, ap["ffn2_w2"], 8, FT, P, lambda kk, c: hidden[:, kk, :], [(LAT, TOK)],
                   lambda n, c: k.gain[:, 0, bass.ds(n, 1)], 1.0)
    norm(k, x_lat(k), x_lat(k), DT, LAT, TOK, 0, RMS_EPS, False, lambda j: k.v("fnorm2", j))


T3 = META + SEQ
M0 = LAT - META
QB = 5
HEADS3, TOPK = 8, SEQ // 4
MASKED = -1.0e38
PICKED = -3.0e38
WIDTH = [min(P * (b + 1), T3) for b in range(QB)]
ROWS = [min(P, T3 - P * b) for b in range(QB)]
BIAS_AT = [sum(WIDTH[:b]) for b in range(QB)]
A3_R = 0
A3_V = A3_R + 16 * T3
A3_OUT = A3_V + QB * 512
A3_MISC = A3_OUT + 8 * T3
A3_BIAS = A3_MISC + T3
A3_S = A3_BIAS + sum(WIDTH)
A3_PT = A3_S + 2 * T3
A3_SC = A3_PT + 2 * QB * P
A3_RB = A3_SC + T3
A3_KM = A3_SC
CHUNKS3 = [(M0, M0 + T3 // 2), (M0 + T3 // 2, TOK)]


def banks_of(width):
    return [(0, min(width, 512))] + ([(512, width)] if width > 512 else [])


def stage_third_inputs(k):
    r = view(k, A3_R, 16, T3)
    misc = k.arena[:, A3_MISC:A3_MISC + T3]
    v = k.arena[:, A3_V:A3_V + QB * 512].rearrange("p (t e) -> p t e", e=512)

    def act_evict(act, i, u):
        for g in range(2):
            for c, (a, b) in enumerate(CHUNKS3):
                ins = act.activation(flat(r[:, bass.ds(4 * i + (2 * u + g), 1), a - M0:b - M0]),
                                     k.bank[4 * u + 2 * g + c][:, :b - a], ACT.Copy)
        ins.then_inc(k.evicted.sem, 1)
    linear(k, k.ap["w_r3"], 8, DT, 256, lambda kk, c: k.H[:, kk, slice(*CHUNKS3[c])], CHUNKS3, act_evict)
    stage_token_values(k, k.ap["w_vs"], 1, QB, M0, lambda s, t: v[:, t, :], ROWS[-1])
    with k.nc.Block() as block:
        @block.sync
        def _(sp):
            sp.dma_start(k.W[0][:, :DT * P], k.ap["w_misc"]).then_inc(k.weights_in[0].sem, 16)

        @block.tensor
        def _(pe):
            pe.wait_ge(*k.weights_in[0](16))
            for c, (a, b) in enumerate(CHUNKS3):
                for kk in range(DT):
                    mm = pe.matmul(k.bank[c][:, :b - a], k.W[0][:, kk * P:(kk + 1) * P], k.H[:, kk, a:b],
                                   start=kk == 0, stop=kk == DT - 1)
            mm.then_inc(k.pe_done.sem, 1)

        @block.scalar
        def _(act):
            act.wait_ge(*k.pe_done(1))
            for c, (a, b) in enumerate(CHUNKS3):
                act.activation(misc[:, a - M0:b - M0], k.bank[c][:, :b - a], ACT.Copy)
    k.weights_in[0].counted(16)
    k.pe_done.counted(1)


def stage_rope3(k, tiles, rows, rot, cos, sin):
    tmp = k.arena[:, A3_S:A3_S + 2 * T3].rearrange("p (a t) -> p a t", t=T3)
    half = T3 // 2
    n = len(tiles)
    turned, swapped = k.more[0:2]
    with k.nc.Block() as block:
        @block.tensor
        def _(pe):
            for j, x in enumerate(tiles):
                if j >= 2:
                    pe.wait_ge(*swapped(j - 1))
                for c in range(2):
                    mm = pe.matmul(k.bank[2 * (j % 2) + c][:rows, :half], rot, x[:, c * half:(c + 1) * half],
                                   start=True, stop=True)
                mm.then_inc(turned.sem, 1)

        @block.vector
        def _(dve):
            for j, x in enumerate(tiles):
                t = tmp[:rows, j % 2, :]
                dve.wait_ge(*turned(j + 1))
                if j >= 2:
                    dve.wait_ge(*k.dve_done(2 * (j - 1)))
                for c in range(2):
                    ins = dve.tensor_tensor(t[:, c * half:(c + 1) * half], k.bank[2 * (j % 2) + c][:rows, :half],
                                            sin[:, c * half:(c + 1) * half], ALU.mult)
                ins.then_inc(swapped.sem, 1)
                dve.tensor_tensor(x, x, cos, ALU.mult).then_inc(k.dve_done.sem, 1)
                dve.wait_ge(*swapped(j + 1))
                dve.wait_ge(*k.dve_done(2 * j + 1))
                dve.tensor_tensor(x, x, t, ALU.add).then_inc(k.dve_done.sem, 1)
    for s, m in ((turned, n), (swapped, n), (k.dve_done, 2 * n)):
        s.counted(m)


def stage_selection(k):
    r = view(k, A3_R, 16, T3)
    misc = k.arena[:, A3_MISC:A3_MISC + T3]
    bias = k.arena[:, A3_BIAS:A3_BIAS + sum(WIDTH)]
    score = k.arena[:, A3_SC:A3_SC + T3]
    relus = view(k, A3_RB, 2, T3)
    w_i = k.rstd[:, 0:QB * 8].rearrange("p (b h) -> p b h", h=8)
    top = k.rstd[:, 64:72]
    weighted, scored, rectified, added = k.more[0:4]
    B = k.bank
    units = [(b, h) for b in range(1, QB) for h in range(8)]
    with k.nc.Block() as block:
        @block.tensor
        def _(pe):
            for b in range(QB):
                mm = pe.transpose(B[7][:ROWS[b], 8 * b:8 * b + 8], misc[0:8, b * P:b * P + ROWS[b]], k.ident[0:8, 0:8])
            mm.then_inc(weighted.sem, 1)
            for n, (b, h) in enumerate(units):
                rows = slice(64 * (h % 2), 64 * (h % 2) + 64)
                if n >= 2:
                    pe.wait_ge(*rectified(n - 1))
                for c, (lo, hi) in enumerate(banks_of(WIDTH[b])):
                    mm = pe.matmul(B[2 * (n % 2) + c][:ROWS[b], :hi - lo], r[rows, 8 + h // 2, b * P:b * P + ROWS[b]],
                                   r[rows, 12, lo:hi], start=True, stop=True)
                mm.then_inc(scored.sem, 1)

        @block.scalar
        def _(act):
            for n, (b, h) in enumerate(units):
                act.wait_ge(*scored(n + 1))
                if n >= 2:
                    act.wait_ge(*added(n - 1))
                for c, (lo, hi) in enumerate(banks_of(WIDTH[b])):
                    ins = act.activation(relus[:ROWS[b], n % 2, lo:hi], B[2 * (n % 2) + c][:ROWS[b], :hi - lo],
                                         ACT.Relu, scale=0.125)
                ins.then_inc(rectified.sem, 1)

        @block.vector
        def _(dve):
            chain = []

            def link(ins):
                chain.append(1)
                ins.then_inc(k.dve_done.sem, 1)
                dve.wait_ge(*k.dve_done(len(chain)))
            dve.wait_ge(*weighted(1))
            for b in range(QB):
                link(dve.tensor_scalar(w_i[:ROWS[b], b, :], B[7][:ROWS[b], 8 * b:8 * b + 8], float(8 ** -0.5), None,
                                       ALU.mult))
            dve.tensor_copy(bias[:, 0:P], k.neg[:, :])
            for n, (b, h) in enumerate(units):
                s = score[:ROWS[b], :WIDTH[b]]
                x, w = relus[:ROWS[b], n % 2, :WIDTH[b]], w_i[:ROWS[b], b, h:h + 1]
                dve.wait_ge(*rectified(n + 1))
                if h == 0:
                    ins = dve.tensor_scalar(s, x, w, None, ALU.mult)
                else:
                    ins = dve.scalar_tensor_tensor(s, x, w, s, ALU.mult, ALU.add)
                ins.then_inc(added.sem, 1)
                dve.wait_ge(*added(n + 1))
                if h < 7:
                    continue
                q, diag = ROWS[b], slice(b * P, WIDTH[b])
                nd = WIDTH[b] - b * P
                link(dve.tensor_tensor(s[:, diag], s[:, diag], k.neg[:q, :nd], ALU.add))
                for _round in range(TOPK // 8):
                    link(dve.max(top[:q], s))
                    link(dve.match_replace(s, top[:q], s, PICKED))
                out = bias[:q, BIAS_AT[b]:BIAS_AT[b] + WIDTH[b]]
                link(dve.tensor_scalar(out, s, 2.0 * MASKED, -1.0e30, ALU.is_gt, ALU.mult))
                link(dve.tensor_tensor(out[:, diag], out[:, diag], k.neg[:q, :nd], ALU.add))
            weighted.chain = len(chain)
    n = len(units)
    for s, m in ((weighted, 1), (scored, n), (rectified, n), (added, n), (k.dve_done, weighted.chain)):
        s.counted(m)


def stage_attention(k, query, keyf, value, bias, scale, first_tile):
    out = view(k, A3_OUT, 8, T3)
    s_buf = view(k, A3_S, 2, T3)
    p_t = k.arena[:, A3_PT:A3_PT + 2 * QB * P].rearrange("p (a t q) -> p a t q", a=2, q=P)
    top, total = k.rstd[:, 0:4], k.rstd[:, 8:12]
    scored, biased, exped, normed, turned, moved, summed, kept = k.more[0:8]
    B = k.bank
    units = [(b, h) for b in range(QB) for h in range(HEADS3)]
    N = len(units)
    with k.nc.Block() as block:
        @block.tensor
        def _(pe):
            for i in range(N + 2):
                if i < N:
                    n, (b, h) = i, units[i]
                    if n >= 2:
                        pe.wait_ge(*biased(n - 1))
                    for c, (lo, hi) in enumerate(banks_of(WIDTH[b])):
                        mm = pe.matmul(B[2 * (n % 2) + c][:ROWS[b], :hi - lo], query(h, b * P, b * P + ROWS[b]),
                                       keyf(h, lo, hi), start=True, stop=True)
                    mm.then_inc(scored.sem, 1)
                if 1 <= i <= N:
                    n, (b, h) = i - 1, units[i - 1]
                    pe.wait_ge(*normed(n + 1))
                    if n:
                        pe.wait_ge(*moved(n))
                    for t in range(b + 1):
                        kr = ROWS[t]
                        mm = pe.transpose(B[4 + t // 4][:kr, (t % 4) * P:(t % 4) * P + ROWS[b]],
                                          s_buf[:ROWS[b], n % 2, t * P:t * P + kr], k.ident[:ROWS[b], :ROWS[b]])
                    mm.then_inc(turned.sem, 1)
                if i >= 2:
                    n, (b, h) = i - 2, units[i - 2]
                    pe.wait_ge(*moved(n + 1))
                    if n >= 2:
                        pe.wait_ge(*kept(n - 1))
                    r = slice(64 * (h % 2), 64 * (h % 2) + 64)
                    for t in range(b + 1):
                        mm = pe.matmul(B[6 + n % 2][r, :ROWS[b]], value(h, t)[:ROWS[t]],
                                       p_t[:ROWS[t], n % 2, t, :ROWS[b]], start=t == 0, stop=t == b)
                    mm.then_inc(summed.sem, 1)

        @block.scalar
        def _(act):
            for i in range(N + 2):
                if i < N:
                    n, (b, h) = i, units[i]
                    s = s_buf[:ROWS[b], n % 2, :WIDTH[b]]
                    act.wait_ge(*biased(n + 1))
                    act.activation(s, s, ACT.Exp, bias=top[:ROWS[b], n % 4:n % 4 + 1],
                                   accum_out=total[:ROWS[b], n % 4:n % 4 + 1]).then_inc(exped.sem, 1)
                if 1 <= i <= N:
                    n, (b, h) = i - 1, units[i - 1]
                    act.wait_ge(*turned(n + 1))
                    if n >= 2:
                        act.wait_ge(*summed(n - 1))
                    full = min(b + 1, 4)
                    ins = act.activation(p_t[:, n % 2, :full, :ROWS[b]],
                                         B[4][:, :full * P].rearrange("p (t q) -> p t q", q=P)[:, :, :ROWS[b]], ACT.Copy)
                    if b == 4:
                        ins = act.activation(p_t[:ROWS[4], n % 2, 4, :ROWS[b]], B[5][:ROWS[4], :ROWS[b]], ACT.Copy)
                    ins.then_inc(moved.sem, 1)
                if i >= 2:
                    n, (b, h) = i - 2, units[i - 2]
                    act.wait_ge(*summed(n + 1))
                    r = slice(64 * (h % 2), 64 * (h % 2) + 64)
                    act.activation(out[r, first_tile + h // 2, b * P:b * P + ROWS[b]], B[6 + n % 2][r, :ROWS[b]],
                                   ACT.Copy).then_inc(kept.sem, 1)

        @block.vector
        def _(dve):
            d = k.dve_done
            for i in range(N + 1):
                if i < N:
                    n, (b, h) = i, units[i]
                    s = s_buf[:ROWS[b], n % 2, :WIDTH[b]]
                    dve.wait_ge(*scored(n + 1))
                    if n >= 2:
                        dve.wait_ge(*turned(n - 1))
                    for c, (lo, hi) in enumerate(banks_of(WIDTH[b])):
                        ins = dve.scalar_tensor_tensor(s[:, lo:hi], B[2 * (n % 2) + c][:ROWS[b], :hi - lo], scale,
                                                       bias(b)[:ROWS[b], lo:hi], ALU.mult, ALU.add)
                    ins.then_inc(d.sem, 1)
                    dve.wait_ge(*d(max(2 * n, 1)))
                    dve.tensor_reduce(top[:ROWS[b], n % 4:n % 4 + 1], s, AX.X, ALU.max, negate=True
                                      ).then_inc(biased.sem, 1)
                if i >= 1:
                    n, (b, h) = i - 1, units[i - 1]
                    s, one = s_buf[:ROWS[b], n % 2, :WIDTH[b]], total[:ROWS[b], n % 4:n % 4 + 1]
                    dve.wait_ge(*exped(n + 1))
                    dve.reciprocal(one, one).then_inc(d.sem, 1)
                    dve.wait_ge(*d(2 * i + 1 if i < N else 2 * N))
                    dve.tensor_scalar(s, s, one, None, ALU.mult).then_inc(normed.sem, 1)
    for s in (scored, biased, exped, normed, turned, moved, summed, kept):
        s.counted(N)
    k.dve_done.counted(2 * N)


def stage_latent_projections(k, tables):
    r = view(k, A3_R, 16, T3)
    qm, km = view(k, A3_R, 8, T3), view(k, A3_KM, 8, T3)
    v = k.arena[:, A3_V:A3_V + QB * 512].rearrange("p (t e) -> p t e", e=512)
    misc = k.arena[:, A3_MISC:A3_MISC + T3]
    half = T3 // 2
    w_uq = k.W[0][:, 0:2 * 768].rearrange("p (k n) -> p k n", n=768)
    w_k, w_v = k.W[1][:, 0:512], k.W[1][:, 512:1024]
    outs = []
    for h in range(HEADS3):
        for c in range(2):
            outs.append(("q", h, c))
    for h in range(HEADS3):
        for c in range(2):
            outs.append(("k", h, c))
    for t in range(QB):
        outs.append(("v", t, 0))
    with k.nc.Block() as block:
        @block.sync
        def _(sp):
            sp.dma_start(k.W[0][:, 0:1536], k.ap["w_uq"]).then_inc(k.weights_in[0].sem, 16)
            sp.dma_start(k.W[1][:, 0:1024], k.ap["w_ukv"]).then_inc(k.weights_in[1].sem, 16)

        @block.tensor
        def _(pe):
            pe.wait_ge(*k.weights_in[0](16))
            pe.wait_ge(*k.weights_in[1](16))
            for n, (kind, h, c) in enumerate(outs):
                if n >= 8:
                    pe.wait_ge(*k.act_done(n - 7))
                cols = slice(c * half, (c + 1) * half)
                if kind == "q":
                    pe.matmul(k.bank[n % 8][:96, :half], w_uq[:, 0, 96 * h:96 * h + 96], r[:, 13, cols], start=True,
                              stop=False)
                    mm = pe.matmul(k.bank[n % 8][:96, :half], w_uq[:, 1, 96 * h:96 * h + 96], r[:, 14, cols],
                                   start=False, stop=True)
                elif kind == "k":
                    mm = pe.matmul(k.bank[n % 8][:64, :half], w_k[:, 64 * h:64 * h + 64], r[:, 15, cols],
                                   start=True, stop=True)
                else:
                    mm = pe.matmul(k.bank[n % 8][:ROWS[h], :], r[:, 15, h * P:h * P + ROWS[h]], w_v,
                                   start=True, stop=True)
                mm.then_inc(k.pe_done.sem, 1)

        @block.scalar
        def _(act):
            act.activation(km[64:96, 0, :], misc[64:96, :], ACT.Copy)
            for n, (kind, h, c) in enumerate(outs):
                act.wait_ge(*k.pe_done(n + 1))
                cols = slice(c * half, (c + 1) * half)
                if kind == "q":
                    dst, src = qm[:96, h, cols], k.bank[n % 8][:96, :half]
                elif kind == "k":
                    dst, src = km[:64, h, cols], k.bank[n % 8][:64, :half]
                else:
                    dst, src = v[:ROWS[h], h, :], k.bank[n % 8][:ROWS[h], :]
                act.activation(dst, src, ACT.Copy).then_inc(k.act_done.sem, 1)
    for u in range(2):
        k.weights_in[u].counted(16)
    k.pe_done.counted(len(outs))
    k.act_done.counted(len(outs))
    cos, sin = tables
    stage_rope3(k, [qm[:96, h, :] for h in range(8)] + [km[:96, 0, :]], 96, k.rot96[:96, :96], cos[:96], sin[:96])
    with k.nc.Block() as block:
        @block.scalar
        def _(act):
            for h in range(1, HEADS3):
                act.activation(km[64:96, h, :], km[64:96, 0, :], ACT.Copy)


def block_three(k):
    ap = k.ap
    tables = k.H[:, :, :].rearrange("p k t -> p (k t)")[:, :4 * T3].rearrange("p (a t) -> p a t", t=T3)
    r = view(k, A3_R, 16, T3)
    with k.nc.Block() as block:
        @block.sync
        def _(sp):
            sp.dma_start(k.X[:, :, M0:LAT], ap["meta_t"].rearrange("(k p) t -> p k t", p=P)).then_inc(k.loaded.sem, 16)
            sp.wait_ge(*k.loaded(16))
    k.loaded.counted(16)
    for a, b in CHUNKS3:
        norm(k, lambda j: k.X[:, j, a:b], lambda j: k.H[:, j, a:b], DT, a, b, 0, RMS_EPS, False,
             lambda j: k.v("attn_norm", j))
    stage_third_inputs(k)
    with k.nc.Block() as block:
        @block.sync
        def _(sp):
            sp.dma_start(tables, ap["rope3"]).then_inc(k.loaded.sem, 16)
            sp.dma_start(k.rot32, ap["rot32"]).then_inc(k.loaded.sem, 16)
            sp.dma_start(k.rot96, ap["rot96"]).then_inc(k.loaded.sem, 16)
            sp.wait_ge(*k.loaded(48))
    k.loaded.counted(48)
    stage_rope3(k, [r[:, j, :] for j in range(13)], P, k.rot32, tables[:, 0, :], tables[:, 1, :])
    stage_selection(k)
    v = k.arena[:, A3_V:A3_V + QB * 512].rearrange("p (t e) -> p t e", e=512)

    def pair(h):
        return slice(64 * (h % 2), 64 * (h % 2) + 64)
    stage_attention(k, lambda h, a, b: r[pair(h), h // 2, a:b], lambda h, a, b: r[pair(h), 4 + h // 2, a:b],
                    lambda h, t: v[:, t, h * 64:(h + 1) * 64],
                    lambda b: k.arena[:, A3_BIAS + BIAS_AT[b]:A3_BIAS + BIAS_AT[b] + WIDTH[b]], 0.125, 4)
    for c in range(2):
        cols = slice(c * (T3 // 2), (c + 1) * (T3 // 2))
        norm(k, lambda j: r[:, 13 + j, cols], lambda j: r[:, 13 + j, cols], 2, 0, T3 // 2, 1, RMS_EPS, False,
             lambda j: k.v("q_norm", j))
        norm(k, lambda j: r[:, 15, cols], lambda j: r[:, 15, cols], 1, 0, T3 // 2, 2, RMS_EPS, False,
             lambda j: k.v("kv_norm", j))
    stage_latent_projections(k, (tables[:, 2, :], tables[:, 3, :]))
    qm, km = view(k, A3_R, 8, T3), view(k, A3_KM, 8, T3)
    causal = k.arena[:, A3_BIAS:A3_BIAS + QB * P]
    with k.nc.Block() as block:
        @block.vector
        def _(dve):
            dve.memset(causal[:, :4 * P], 0.0)
            dve.tensor_copy(causal[:, 4 * P:], k.neg[:, :])
    stage_attention(k, lambda h, a, b: qm[:96, h, a:b], lambda h, a, b: km[:96, h, a:b],
                    lambda h, t: v[:, t, h * 64:(h + 1) * 64],
                    lambda b: causal[:, (4 - b) * P:(4 - b) * P + WIDTH[b]], float(96 ** -0.5), 0)
    out = view(k, A3_OUT, 8, T3)
    stage_residual(k, ap["w_o3"], 4, DT, 256, lambda kk, c: out[:, kk, META:], [(LAT, TOK)], None, 1.0)
    norm(k, x_lat(k), lambda j: k.H[:, j, LAT:], DT, LAT, TOK, 0, RMS_EPS, False, lambda j: k.v("ffn_norm", j))
    hidden = view(k, 0, FT, 512)
    stage_swiglu(k, ap["w_gu3"], lambda kk, c: k.H[:, kk, LAT:], [(0, 512)], hidden)
    stage_residual(k, ap["w_down3"], 8, FT, P, lambda kk, c: hidden[:, kk, :], [(LAT, TOK)], None, 1.0)
    norm(k, x_lat(k), x_lat(k), DT, LAT, TOK, 0, RMS_EPS, False, lambda j: k.v("fnorm3", j))


def build(nc, ap, out):
    with ExitStack() as ctx:
        k = Core(nc, ctx, ap)
        stage_load(k)
        block_one(k)
        block_two(k)
        block_three(k)
        with nc.Block() as block:
            @block.sync
            def _(sp):
                sp.dma_start(out.rearrange("(k p) t -> p k t", p=P), k.X[:, :, LAT:]).then_inc(k.stored.sem, 16)
                sp.wait_ge(*k.stored(16))


def _columns(a, tiles):
    return a.reshape(tiles, 128).T


def _pack(w, groups, cols, order=None):
    kt = w.shape[0] // 128
    t = w.reshape(kt, 128, -1, 128)
    if order is not None:
        t = t[:, :, order, :]
    t = t.reshape(kt, 128, groups, cols).transpose(2, 1, 0, 3)
    return np.ascontiguousarray(t).reshape(groups, 128, kt * cols)


def _constants():
    c = {}
    c["ident"] = np.eye(128, dtype=np.float32)
    rot = np.zeros((128, 128), np.float32)
    for m in range(64):
        rot[m + 64, m] = -1.0
        rot[m, m + 64] = 1.0
    c["rot64"] = rot
    gamma = np.log(1.0 - 2.0 ** (-5.0 - np.arange(8)))
    rel = np.arange(512)[None, :] - np.arange(128)[:, None]
    c["decay"] = np.where(rel[None] >= 0, np.exp(gamma[:, None, None] * np.maximum(rel, 0)[None]), 0.0).astype(np.float32)
    s, t = np.arange(128)[:, None], np.arange(128)[None, :]
    masks = [s == t]
    for lev in range(7):
        m = 1 << lev
        same = s // (2 * m) == t // (2 * m)
        masks.append(same & ((s // m) % 2 == 0) & ((t // m) % 2 == 1))
    c["masks"] = np.stack(masks + [x.T for x in masks], 1).astype(np.int32).reshape(128, 2048)
    c["tri"] = np.stack([s <= t, s >= t], 1).astype(np.float32)
    sel = np.zeros((4, 4, 128), np.float32)
    for h in range(4):
        sel[h, h] = 1.0
    c["sel"] = sel
    c["neg"] = np.where(t > s, np.float32(-1.0e38), np.float32(0.0)).astype(np.float32)

    def swap(starts, half):
        r = np.zeros((128, 128), np.float32)
        for a in starts:
            for m in range(half):
                r[a + m + half, a + m] = -1.0
                r[a + m, a + m + half] = 1.0
        return r
    c["rot32"], c["rot96"] = swap((0, 64), 32), swap((64,), 16)
    tables = np.zeros((128, 4, 528), np.float32)
    pos = np.arange(528, dtype=np.float32)

    def angles(half):
        inv = np.power(np.float32(10000.0), -np.arange(half, dtype=np.float32) / np.float32(half)).astype(np.float32)
        return inv[:, None] * pos[None, :]
    for a in range(0, 128, 32):
        tables[a:a + 32, 0], tables[a:a + 32, 1] = np.cos(angles(32)), np.sin(angles(32))
    tables[:64, 2] = 1.0
    for a in (64, 80):
        tables[a:a + 16, 2], tables[a:a + 16, 3] = np.cos(angles(16)), np.sin(angles(16))
    c["rope3"] = tables
    return c
def _inputs_one(a):
    out = {}
    out["x_t"] = np.ascontiguousarray(a["x"][0].T)
    out["ctx_t"] = np.ascontiguousarray(a["ctx_2"][0].T)
    out["positions_b"] = np.ascontiguousarray(np.broadcast_to(a["positions"], (128, 512)))
    out["w_ada"] = _pack(a["w_ada"][0], 12, 512)
    w = a["w_in"][0]
    b = a["b_in"][0]
    at = np.cumsum([0, 1024, 1024, 2048, 2048, 1024, 1024, 1024, 1024])
    parts = [w[:, at[j]:at[j + 1]] for j in range(8)]
    bias = [b[at[j]:at[j + 1]] for j in range(8)]
    pairs = [t for j in range(8) for t in (j, 8 + j)]
    out["w_cpair"] = _pack(np.concatenate([parts[4], parts[5]], 1), 8, 256, pairs)
    out["w_qk"] = _pack(np.concatenate([parts[0], parts[1]], 1), 8, 256, pairs)
    out["w_v"] = _pack(parts[2], 4, 512)
    out["b_v"] = np.ascontiguousarray(bias[2][None])
    out["w_g"] = _pack(parts[3], 8, 256)
    out["w_ga"] = _pack(parts[6], 4, 256)
    out["w_gb"] = _pack(parts[7], 4, 256)
    out["w_conv_out"] = _pack(a["w_conv_out"][0], 4, 256)
    out["w_ret_out"] = _pack(a["w_ret_out"][0], 4, 256)
    out["w_out"] = _pack(a["w_out"][0], 4, 256)
    ffp = [t for j in range(22) for t in (j, 22 + j)]
    out["w_up"] = _pack(a["w_up"][0], 22, 256, ffp)
    out["w_down"] = _pack(a["w_down"][0], 8, 128)
    v = {}
    v["c"] = _columns(a["c"][0], 8)
    v["b_ada"] = _columns(a["b_ada"][0], 48)
    v["b_cval"], v["b_cgate"] = _columns(bias[4], 8), _columns(bias[5], 8)
    v["b_qk"] = _columns(np.concatenate([bias[0], bias[1]]), 16)[:, pairs]
    v["b_g"], v["b_ga"], v["b_gb"] = _columns(bias[3], 16), _columns(bias[6], 8), _columns(bias[7], 8)
    v["conv_w"] = a["conv_dw_w"][0].reshape(31, 8, 128).transpose(2, 1, 0).reshape(128, 248)
    v["conv_b"] = _columns(a["conv_dw_b"][0], 8)
    v["cln_g"], v["cln_b"] = _columns(a["conv_ln_g"][0], 8), _columns(a["conv_ln_b"][0], 8)
    v["gn_g"], v["gn_b"] = _columns(a["ret_gn_g"][0], 16), _columns(a["ret_gn_b"][0], 16)
    v["ln1_g"], v["ln1_b"] = _columns(a["ln1_g"][0], 8), _columns(a["ln1_b"][0], 8)
    v["ffn_w"] = a["ffn_dw_w"][0].reshape(3, 44, 128).transpose(2, 1, 0)[:, ffp, :].reshape(128, 132)
    v["ffn_b"] = _columns(a["ffn_dw_b"][0], 44)[:, ffp]
    v["ln2_g"], v["ln2_b"] = _columns(a["ln2_g"][0], 8), _columns(a["ln2_b"][0], 8)
    half = np.arange(64, dtype=np.float32)
    freq = np.float32(10000.0) ** (-half / np.float32(64))
    v["inv_freq"] = np.concatenate([freq, freq])[:, None].astype(np.float32)
    return out, v


def _inputs_two(a):
    out, v = {}, {}
    out["w_mod"] = _pack(a["w_mod_2"][0], 18, 512)
    pairs = [t for j in range(22) for t in (j, 22 + j)]
    for n in ("ffn1", "ffn2"):
        out[n + "_w1"] = _pack(a[n + "_w1_2"][0], 22, 256, pairs)
        out[n + "_w2"] = _pack(a[n + "_w2_2"][0], 8, 128)
    w = a["w_in_2"][0]
    out["w_qg2"] = _pack(np.concatenate([w[:, 0:512], w[:, 1024:1536]], 1), 4, 256)
    out["w_f2"] = _pack(w[:, 1536:2560], 4, 256, [0, 4, 1, 5, 2, 6, 3, 7])
    out["w_v2"] = _pack(np.concatenate([w[:, 512:1024], w[:, 3072:3584]], 1), 2, 512)
    out["w_mqk"] = _pack(w[:, 2560:3072], 2, 256)
    out["w_mo"] = _pack(w[:, 3584:4096], 2, 256)
    gates = np.zeros((1024, 128), np.float32)
    gb = np.zeros((128, 1), np.float32)
    for g in range(4):
        gates[:, 32 * g:32 * g + 4] = w[:, 4096 + 4 * g:4100 + 4 * g]
        gb[32 * g:32 * g + 4, 0] = a["ml_gate_b_2"][0, 4 * g:4 * g + 4]
    out["w_gates"] = _pack(gates, 1, 128)[0]
    out["w_out2"] = _pack(a["w_out_2"][0], 4, 256)
    v["ml_gb"] = gb
    v["cc2"] = np.stack([_columns(a["c_2"][0], 8), _columns(a["c_ctx_2"], 8)], 2).reshape(128, 16)
    b = _columns(a["b_mod_2"][0], 72)
    v["b_mod"] = np.stack([b, b], 2).reshape(128, 144)
    for n in ("norm1", "norm2", "norm3"):
        v[n] = _columns(a[n + "_w_2"][0], 8)
    v["fnorm2"] = _columns(a["final_norm_w_2"], 8)
    v["mconv_w"] = a["ml_conv_w_2"][0].reshape(9, 4, 128).transpose(2, 1, 0).reshape(128, 36)
    v["mconv_b"] = _columns(a["ml_conv_b_2"][0], 4)
    lb = a["hg_lb_logits_2"]
    v["lb0"], v["lb1"] = _columns(lb[0].reshape(-1), 8), _columns(lb[1].reshape(-1), 8)
    v["hg_norm"], v["ml_norm"] = _columns(a["hg_norm_w_2"][0], 4), _columns(a["ml_norm_w_2"][0], 4)
    return out, v


def _inputs_three(a):
    out, v = {}, {}
    out["meta_t"] = np.ascontiguousarray(a["meta_tokens_3"].T)
    w = a["w_in_3"][0]
    cq, ckv, kr = w[:, 0:256], w[:, 256:384], w[:, 384:416]
    qs, ks, vs, qi, ki, wi = (w[:, 416:928], w[:, 928:1440], w[:, 1440:1952], w[:, 1952:2464], w[:, 2464:2528],
                              w[:, 2528:2536])
    out["w_r3"] = _pack(np.concatenate([qs, ks, qi, ki, ki, cq, ckv], 1), 8, 256)
    out["w_vs"] = _pack(vs, 1, 512)
    misc = np.zeros((1024, 128), np.float32)
    misc[:, 0:8] = wi
    misc[:, 64:96] = kr
    out["w_misc"] = _pack(misc, 1, 128)[0]
    out["w_uq"] = np.ascontiguousarray(a["w_uq_3"][0].reshape(2, 128, 768).transpose(1, 0, 2)).reshape(128, 1536)
    out["w_ukv"] = np.ascontiguousarray(
        a["w_ukv_3"][0].reshape(128, 8, 2, 64).transpose(0, 2, 1, 3)).reshape(128, 1024)
    out["w_o3"] = _pack(a["w_o_3"][0], 4, 256)
    pairs = [t for j in range(22) for t in (j, 22 + j)]
    out["w_gu3"] = _pack(np.concatenate([a["w_gate_3"][0], a["w_up_3"][0]], 1), 22, 256, pairs)
    out["w_down3"] = _pack(a["w_down_3"][0], 8, 128)
    v["attn_norm"], v["ffn_norm"] = _columns(a["attn_norm_g_3"][0], 8), _columns(a["ffn_norm_g_3"][0], 8)
    v["q_norm"], v["kv_norm"] = _columns(a["mla_q_norm_g_3"][0], 2), _columns(a["mla_kv_norm_g_3"][0], 1)
    v["fnorm3"] = _columns(a["final_norm_g_3"], 8)
    return out, v


def _arrays(inputs):
    a = {n: np.asarray(x) for n, x in inputs.items()}
    arrays, vecs = _constants(), {}
    for part in (_inputs_one, _inputs_two, _inputs_three):
        out, v = part(a)
        arrays.update(out)
        vecs.update(v)
    arrays["vecs"] = np.ascontiguousarray(np.concatenate([vecs[n] for n in VEC_SIZES], 1))
    return arrays


def kernel(**inputs):
    import concourse.bacc as bacc
    from concourse.bass_utils import run_bass_kernel_spmd

    nc = bacc.Bacc("TRN2", target_bir_lowering=False, num_devices=1)
    arrays = _arrays(inputs)
    ap = {n: nc.dram_tensor("in_" + n, x.shape, mybir.dt.from_np(x.dtype), kind="ExternalInput").ap()
          for n, x in arrays.items()}
    out = nc.dram_tensor("out_t", (D, SEQ), F32, kind="ExternalOutput").ap()
    build(nc, ap, out)
    r = run_bass_kernel_spmd(nc, [{"in_" + n: x for n, x in arrays.items()}], core_ids=[0])
    return np.ascontiguousarray(r.results[0]["out_t"].T)[None]
```

```python
from contextlib import ExitStack

import numpy as np

import concourse.bass as bass
from concourse import mybir

F32 = mybir.dt.float32
F32R = mybir.dt.float32r
U8 = mybir.dt.uint8
I32 = mybir.dt.int32
ALU = mybir.AluOpType
ACT = mybir.ActivationFunctionType
AX = mybir.AxisListType

P = 128
D = 1024
DT = D // P
SEQ, CTX, META = 512, 256, 16
TOK = CTX + SEQ
LAT = CTX
FF = 2816
FT = FF // P
CONV_K = 31
RET_HEADS = 8
ALPHA = float(2.0 ** 0.25)
LN_EPS, RMS_EPS = 1e-5, 1e-6
SLOT = 4096
PART = SLOT // 2

VEC_SIZES = dict(
    c=8, b_ada=48, b_cval=8, b_cgate=8, b_qk=16, b_g=16, b_ga=8, b_gb=8, conv_w=8 * CONV_K, conv_b=8,
    cln_g=8, cln_b=8, gn_g=16, gn_b=16, ln1_g=8, ln1_b=8, ffn_w=2 * FT * 3, ffn_b=2 * FT, ln2_g=8, ln2_b=8,
    inv_freq=1,
    cc2=16, b_mod=144, norm1=8, norm2=8, norm3=8, fnorm2=8, mconv_w=36, mconv_b=4, lb0=8, lb1=8,
    hg_norm=4, ml_norm=4, ml_gb=1,
    attn_norm=8, q_norm=2, kv_norm=1, ffn_norm=8, fnorm3=8,
)
VEC_AT = {}
_at = 0
for _name, _n in VEC_SIZES.items():
    VEC_AT[_name] = _at
    _at += _n
NVEC = _at


PLAIN = dict(w_ada=(12, DT, 512), w_cpair=(8, DT, 256), w_qk=(8, DT, 256), w_v=(4, DT, 512), w_ga=(4, DT, 256),
             w_conv_out=(4, DT, 256), w_g=(8, DT, 256), w_gb=(4, DT, 256), w_ret_out=(4, 16, 256), w_out=(4, DT, 256),
             w_mod=(18, DT, 512), w_qg2=(4, DT, 256), w_f2=(4, DT, 256), w_v2=(2, DT, 512), w_mqk=(2, DT, 256),
             w_mo=(2, DT, 256), w_out2=(4, DT, 256), w_r3=(8, DT, 256), w_o3=(4, DT, 256))


class Signal:

    def __init__(self, handle):
        self.sem, self.base = handle, 0

    def __call__(self, n):
        return self.sem, n + self.base

    def counted(self, n):
        self.base += n


class Core:

    def __init__(self, nc, ctx, ap):
        self.nc, self.ap = nc, ap

        def sb(name, shape, dt=F32):
            return ctx.enter_context(nc.sbuf_tensor(name, shape, dt))

        def sig(name):
            self.signals.append(Signal(ctx.enter_context(nc.semaphore(name))))
            return self.signals[-1]
        self.signals = []

        self.X = sb("X", [P, DT, TOK])
        def place(name, size):
            self.offset[name] = nc.sbuf_base
            return sb(name, [P, size])

        def also(name, where, at, size):
            return nc.alloc_sbuf_tensor_at(name, [P, size], F32R, offset=self.offset[where] + 4 * at)
        self.offset = {}
        h = place("H", DT * TOK)
        self.H = h[:, :].rearrange("p (k t) -> p k t", t=TOK)
        self.W = [place(f"W{u}", SLOT) for u in range(2)]
        self.arena = place("arena", ARENA)
        self.h_high = also("h_high", "H", 0, DT * TOK)[:, :].rearrange("p (k t) -> p k t", t=TOK)
        self.h_low = also("h_low", "arena", A_HLOW, DT * TOK)
        self.w_high = [also(f"w_high{u}", f"W{u}", PART, PART) for u in range(2)]
        self.w_low = [also(f"w_low{u}", "arena", A_WLOW + u * PART, PART) for u in range(2)]
        self.hidden_parts = also("hidden_parts", "arena", A_HIDDEN, A_TAPS - A_HIDDEN)
        self.vec = sb("vec", [P, NVEC])
        self.mod1 = sb("mod1", [P, 48])
        self.mod2 = sb("mod2", [P, 72, 2])
        self.gain = sb("gain", [P, 2, DT])
        self.ident = sb("ident", [P, P])
        self.rot = sb("rot", [P, P])
        self.masks = sb("masks", [P, 16, P], U8)
        self.tri = sb("tri", [P, 2, P])
        self.rot32, self.rot96 = self.tri[:, 0, :], self.tri[:, 1, :]
        self.neg = sb("neg", [P, P])
        self.sel = sb("sel", [4, 4, P])
        self.mean = sb("mean", [P, 4, P])
        self.sq = sb("sq", [P, 3, 512])
        self.rstd = sb("rstd", [P, 512])
        self.stage = sb("stage", [P, 2, 2, 516])
        self.bank = [ctx.enter_context(nc.psum_tensor(f"bank{i}", [P, 512], F32)) for i in range(8)]

        self.loaded = sig("loaded")
        self.weights_in = [sig(f"weights_in{u}") for u in range(2)]
        self.high_made = sig("high_made")
        self.split_done = sig("split_done")
        self.fetched = None
        self.group_done = sig("group_done")
        self.evicted = sig("evicted")
        self.act_turn = sig("act_turn")
        self.dve_turn = sig("dve_turn")
        self.act_done = sig("act_done")
        self.dve_done = sig("dve_done")
        self.pe_done = sig("pe_done")
        self.pool_done = sig("pool_done")
        self.stored = sig("stored")
        self.more = [sig(f"more{i}") for i in range(13)]
        self.streams = {name: Stream(ap[name], *shape) for name, shape in PLAIN.items()}
        for up, down, tokens in (("w_up", "w_down", SEQ), ("ffn1_w1", "ffn1_w2", TOK), ("ffn2_w1", "ffn2_w2", SEQ),
                                 ("w_gu3", "w_down3", SEQ)):
            for n, (first, tiles) in enumerate(PIECES[tokens]):
                self.streams[up, n] = Stream(ap[up], tiles, DT, 2 * P, first, True)
                cols = P if tokens == SEQ else 2 * P
                self.streams[down, n] = Stream(ap[f"{down}_{n}"], D // cols, tiles, cols, 0, True)

    def v(self, name, j=0, n=1):
        at = VEC_AT[name]
        return self.vec[:, bass.ds(at + j, n)] if not isinstance(j, int) else self.vec[:, at + j:at + j + n]


    def hidden(self, tiles, width):
        def tiled(ap):
            return ap.rearrange("p (a b) -> p a b", b=width)
        n = tiles * width
        return (tiled(self.arena[:, A_HIDDEN + n:A_HIDDEN + 2 * n]), tiled(self.hidden_parts[:, :n]),
                tiled(self.hidden_parts[:, n:2 * n]))

    def low_tiles(self, width):
        n = DT * width
        return [ap.rearrange("p (a b) -> p a b", b=width)
                for ap in (self.h_low[:, :n], self.arena[:, A_HLOW:A_HLOW + n])]

    def weight_parts(self, u, size):
        return self.w_high[u][:, :size], self.w_low[u][:, :size]


class Stream:

    def __init__(self, w, groups, kt, cols, first=0, split=False):
        self.w, self.groups, self.kt, self.cols, self.first, self.split = w, groups, kt, cols, first, split
        self.size = kt * cols
        assert groups % 2 == 0 and self.size <= (PART if split else SLOT)

    def fetch(self, k, sp, i, u):
        sp.dma_start(k.W[u][:, :self.size],
                     self.w[bass.ds(self.first + 2 * i + u, 1)].rearrange("a p n -> (a p) n")
                     ).then_inc(k.weights_in[u].sem, 16)

    def high(self, k, act, u):
        act.activation(k.weight_parts(u, self.size)[0], k.W[u][:, :self.size], ACT.Copy).then_inc(k.high_made.sem, 1)

    def low(self, k, pool, u):
        hi, lo = k.weight_parts(u, self.size)
        pool.tensor_tensor(lo, k.W[u][:, :self.size], hi, ALU.subtract).then_inc(k.split_done.sem, 1)


def flat(ap):
    return ap.rearrange("p a t -> p (a t)")


def start_stream(k, stream):
    def sync(sp):
        for u in range(2):
            stream.fetch(k, sp, 0, u)

    def scalar(act):
        for u in range(2):
            act.wait_ge(*k.weights_in[u](16))
            stream.high(k, act, u)

    def pool(gp):
        for u in range(2):
            gp.wait_ge(*k.high_made(u + 1))
            stream.low(k, gp, u)
    return sync, scalar if stream.split else None, pool if stream.split else None


class Linear:

    def __init__(self, k, stream, src, chunks, act_evict=None, dve_evict=None, products=None, dve_other=None,
                 counts=None, then=None, ready=None):
        self.k, self.stream, self.src, self.chunks, self.then = k, stream, src, chunks, then
        self.act_evict, self.dve_evict, self.products, self.dve_other = act_evict, dve_evict, products, dve_other
        self.counts, self.ready = counts or {}, ready
        self.half = stream.groups // 2

    def sync(self, sp):
        k, stream, then, half = self.k, self.stream, self.then, self.half

        def refill(i, last):
            for u in range(2):
                if stream.split and not (last and not then.split):
                    sp.wait_ge(*k.split_done(2 * i + (u + 1)))
                else:
                    sp.wait_ge(*k.group_done(2 * i + (u + 1)))
                if last:
                    then.fetch(k, sp, 0, u)
                else:
                    stream.fetch(k, sp, i + 1, u)
        if half > 1:
            with sp.Fori(0, half - 1) as i:
                refill(i, False)
        if then:
            refill(half - 1, True)

    def tensor(self, pe):
        k, stream, chunks, src, ready = self.k, self.stream, self.chunks, self.src, self.ready
        cols, kt, split = stream.cols, stream.kt, stream.split

        def pair(i, first):
            for u in range(2):
                if split:
                    pe.wait_ge(*k.split_done(2 * i + (u + 1)))
                    weights = k.weight_parts(u, stream.size)
                else:
                    pe.wait_ge(*k.weights_in[u](16 * i + 16))
                    weights = k.W[u]
                pe.wait_ge(*k.evicted(2 * i + (u - 1)))
                if self.products:
                    self.products(pe, i, u).then_inc(k.group_done.sem, 1)
                    continue
                for g in range(cols // P):
                    for c, (a, b) in enumerate(chunks):
                        bank = k.bank[4 * u + len(chunks) * g + c][:, :b - a]
                        for kk in range(kt):
                            at = slice(kk * cols + g * P, kk * cols + (g + 1) * P)
                            if first and (u, g, c) == (0, 0, 0):
                                ready(pe, kk)
                            if not split:
                                mm = pe.matmul(bank, weights[:, at], src(kk, c), start=kk == 0, stop=kk == kt - 1)
                                continue
                            hi, lo = src(kk, c)
                            pe.matmul(bank, weights[0][:, at], hi, start=kk == 0, stop=False)
                            pe.matmul(bank, weights[0][:, at], lo, start=False, stop=False)
                            mm = pe.matmul(bank, weights[1][:, at], hi, start=False, stop=kk == kt - 1)
                mm.then_inc(k.group_done.sem, 1)
        if ready:
            pair(0, True)
        if self.half > (1 if ready else 0):
            with pe.Fori(1 if ready else 0, self.half) as i:
                pair(i, False)

    def scalar(self, act):
        k, stream, then, half = self.k, self.stream, self.then, self.half
        splits = stream.split or (then and then.split)

        def pair(i, last):
            for u in range(2):
                act.wait_ge(*k.group_done(2 * i + (u + 1)))
                follows = then if last else stream
                if follows and follows.split and splits:
                    act.wait_ge(*k.weights_in[u](16 * i + 32))
                    follows.high(k, act, u)
                if self.act_evict:
                    act.sem_inc(k.act_turn.sem, 1)
                    self.act_evict(act, i, u)
        if not (self.act_evict or splits):
            return
        if half > 1 or not splits:
            with act.Fori(0, half - 1 if splits else half) as i:
                pair(i, False)
        if splits:
            pair(half - 1, True)

    def gpsimd(self, gp):
        k, stream, then, half = self.k, self.stream, self.then, self.half

        def lows(i, last):
            for u in range(2):
                before = 2 * i + 2 if stream.split else 0
                gp.wait_ge(*k.high_made(before + (u + 1)))
                (then if last else stream).low(k, gp, u)
        if stream.split and half > 1:
            with gp.Fori(0, half - 1) as i:
                lows(i, False)
        if then and then.split:
            lows(half - 1, True)

    def vector(self, dve):
        k = self.k
        if self.dve_other:
            self.dve_other(dve)
        if self.dve_evict:
            with dve.Fori(0, self.half) as i:
                for u in range(2):
                    dve.wait_ge(*k.group_done(2 * i + (u + 1)))
                    dve.sem_inc(k.dve_turn.sem, 1)
                    self.dve_evict(dve, i, u)

    def counted(self):
        k, groups = self.k, self.stream.groups
        for u in range(2):
            k.weights_in[u].counted(8 * groups)
        k.group_done.counted(groups)
        k.evicted.counted(groups)
        if self.stream.split:
            k.high_made.counted(groups)
            k.split_done.counted(groups)
        for s, n in self.counts.items():
            s.counted(n)


def run(k, linears):
    marks = [s.base for s in k.signals]
    for p, q in zip(linears, linears[1:]):
        assert p.then is q.stream
    start = (None,) * 3 if k.fetched is linears[0].stream else start_stream(k, linears[0].stream)
    assert k.fetched in (None, linears[0].stream)

    def in_turn():
        for s, base in zip(k.signals, marks):
            s.base = base
        for p in linears:
            yield p
            p.counted()
    with k.nc.Block() as block:
        @block.sync
        def _(sp):
            if start[0]:
                start[0](sp)
            for p in in_turn():
                p.sync(sp)

        @block.tensor
        def _(pe):
            for p in in_turn():
                p.tensor(pe)

        @block.scalar
        def _(act):
            if start[1]:
                start[1](act)
            for p in in_turn():
                p.scalar(act)

        @block.gpsimd
        def _(gp):
            if start[2]:
                start[2](gp)
            for p in in_turn():
                p.gpsimd(gp)

        @block.vector
        def _(dve):
            for p in in_turn():
                p.vector(dve)
    for p in in_turn():
        pass
    k.fetched = linears[-1].then


def linear(k, *args, **rest):
    run(k, [Linear(k, *args, **rest)])


def norm(k, src, dst, nt, a, b, mean, eps, center, gain=None, post=None, shift=None, parts=None, then=None):
    nc, n = k.nc, b - a
    pe_done, act_done, dve_done = k.pe_done, k.act_done, k.dve_done
    steps = nt if center else 0
    start = start_stream(k, then) if then else (None,) * 3
    with nc.Block() as block:
        @block.sync
        def _(sp):
            if start[0]:
                start[0](sp)

        @block.gpsimd
        def _(gp):
            if start[2]:
                start[2](gp)

        @block.tensor
        def _(pe):
            if center:
                for j in range(nt):
                    mm = pe.matmul(k.bank[0][:, :n], k.mean[:, mean, :], src(j), start=j == 0, stop=j == nt - 1)
                mm.then_inc(pe_done.sem, 1)
            for j in range(nt):
                pe.wait_ge(*act_done(j + 1))
                pe.matmul(k.bank[1][:, :n], k.mean[:, mean, :], k.sq[:, j % 3, :n],
                          start=j == 0, stop=j == nt - 1).then_inc(pe_done.sem, 1)

        @block.scalar
        def _(act):
            for j in range(nt):
                if center:
                    act.wait_ge(*dve_done(j + 1))
                if j >= 3:
                    act.wait_ge(*pe_done((1 if center else 0) + j - 2))
                act.activation(k.sq[:, j % 3, :n], dst(j) if center else src(j), ACT.Square
                               ).then_inc(act_done.sem, 1)
            if start[1]:
                start[1](act)
            act.wait_ge(*dve_done(steps + 2))
            act.activation(k.rstd[:, :n], k.rstd[:, :n], ACT.Sqrt).then_inc(act_done.sem, 1)
            if post or shift or parts:
                for j in range(nt):
                    act.wait_ge(*dve_done(steps + 3 + j))
                    act.activation(parts(j)[0] if parts else dst(j), dst(j), post or ACT.Identity,
                                   bias=shift(j) if shift else 0.0).then_inc(act_done.sem, 1)

        @block.vector
        def _(dve):
            if center:
                dve.wait_ge(*pe_done(1))
                for j in range(nt):
                    dve.tensor_tensor(dst(j), src(j), k.bank[0][:, :n], ALU.subtract).then_inc(dve_done.sem, 1)
            dve.wait_ge(*pe_done((1 if center else 0) + nt))
            dve.tensor_scalar(k.rstd[:, :n], k.bank[1][:, :n], eps, None, ALU.add).then_inc(dve_done.sem, 1)
            dve.wait_ge(*dve_done(steps + 1))
            dve.reciprocal(k.rstd[:, :n], k.rstd[:, :n]).then_inc(dve_done.sem, 1)
            dve.wait_ge(*act_done(nt + 1))
            for j in range(nt):
                x = dst(j) if center else src(j)
                if gain:
                    dve.scalar_tensor_tensor(dst(j), x, gain(j), k.rstd[:, :n], ALU.mult, ALU.mult
                                             ).then_inc(dve_done.sem, 1)
                else:
                    dve.tensor_tensor(dst(j), x, k.rstd[:, :n], ALU.mult).then_inc(dve_done.sem, 1)
            if parts:
                for j in range(nt):
                    hi, lo = parts(j)
                    dve.wait_ge(*act_done(nt + 2 + j))
                    if shift:
                        dve.scalar_tensor_tensor(lo, dst(j), shift(j), hi, ALU.add, ALU.subtract)
                    else:
                        dve.tensor_tensor(lo, dst(j), hi, ALU.subtract)
    pe_done.counted((1 if center else 0) + nt)
    act_done.counted(nt * (2 if post or shift or parts else 1) + 1)
    dve_done.counted(steps + 2 + nt)
    k.fetched = then or k.fetched


A_QK = 0
A_V = A_QK + 16 * 512
A_PAD = A_V + 4 * 2048
A_CONV = A_PAD + 8 * 542
A_COS = A_CONV
A_SIN = A_COS + 512
A_TMP = A_SIN + 512
A_DECAY = A_TMP + 2 * 512
A_P = A_DECAY + 2 * 512
ARENA = A_P + 1280
A_HLOW = 0
A_WLOW = A_HLOW + DT * TOK
A_HIDDEN = A_WLOW + 2 * PART
PIECES = {SEQ: ((0, 12), (12, 10)), TOK: ((0, 8), (8, 8), (16, 6))}
A_TAPS = A_HIDDEN + 2 * 12 * SEQ


def view(k, at, a, b):
    return k.arena[:, at:at + a * b].rearrange("p (a b) -> p a b", b=b)


def stage_load(k):
    nc, ap = k.nc, k.ap
    wide = k.arena[:, :16 * P].bitcast(I32)
    with nc.Block() as block:
        @block.sync
        def _(sp):
            sp.dma_start(k.vec[:, :], ap["vecs"]).then_inc(k.loaded.sem, 16)
            sp.dma_start(k.X[:, :, LAT:], ap["x_t"].rearrange("(k p) t -> p k t", p=P)).then_inc(k.loaded.sem, 16)
            sp.dma_start(k.X[:, :, :CTX], ap["ctx_t"].rearrange("(k p) t -> p k t", p=P)).then_inc(k.loaded.sem, 16)
            sp.dma_start(k.ident[:, :], ap["ident"]).then_inc(k.loaded.sem, 16)
            sp.dma_start(k.rot[:, :], ap["rot64"]).then_inc(k.loaded.sem, 16)
            sp.dma_start(wide, ap["masks"]).then_inc(k.loaded.sem, 16)
            sp.dma_start(k.tri[:, :, :], ap["tri"]).then_inc(k.loaded.sem, 16)
            sp.dma_start(k.sel[:, :, :], ap["sel"]).then_inc(k.loaded.sem, 16)
            sp.dma_start(k.neg[:, :], ap["neg"]).then_inc(k.loaded.sem, 16)
            sp.wait_ge(*k.loaded(144))

        @block.scalar
        def _(act):
            act.sem_inc(k.evicted.sem, 2)
            act.sem_inc(k.group_done.sem, 2)

        @block.vector
        def _(dve):
            for j, n in enumerate((1024, 256, 128, 1)):
                dve.memset(k.mean[:, j, :], 1.0 / n)
    k.loaded.counted(144)
    k.evicted.counted(2)
    k.group_done.counted(2)
    with nc.Block() as block:
        @block.vector
        def _(dve):
            dve.tensor_copy(k.masks[:, :, :].rearrange("p a b -> p (a b)"), wide)

        @block.scalar
        def _(act):
            act.activation(k.v("c", 0, 8), k.v("c", 0, 8), ACT.Silu)
            act.activation(k.v("cc2", 0, 16), k.v("cc2", 0, 16), ACT.Silu)


def stage_modulation(k, stream, n, src, then):
    width = P // n
    per = 512 // width
    repeated = view(k, 0, DT, P)
    diagonal = view(k, DT * P, 1, width)
    kept = k.arena[:, DT * P + P:DT * P + P + per * stream.groups]
    with k.nc.Block() as block:
        @block.vector
        def _(dve):
            for kk in range(DT):
                for c in range(n):
                    at = slice(c * width, (c + 1) * width)
                    dve.tensor_scalar(repeated[:, kk, at], k.mean[:, 3, at], src(kk, c), None, ALU.mult)
            if n == 1:
                dve.tensor_copy(diagonal[:, 0, :], k.ident[:, :])
            else:
                dve.tensor_tensor(diagonal[:, 0, :], k.ident[:, :width], k.ident[:, width:], ALU.add)

    def products(pe, i, u):
        for kk in range(DT):
            mm = pe.matmul(k.bank[4 * u][:, :], repeated[:, kk, :], k.W[u][:, kk * 512:(kk + 1) * 512],
                           start=kk == 0, stop=kk == DT - 1)
        return mm

    def evict(dve, i, u):
        own = k.stage[:, u, 0, :512].rearrange("p (a b) -> p a b", b=width)
        dve.tensor_tensor(own, k.bank[4 * u][:, :].rearrange("p (a b) -> p a b", b=width),
                          diagonal.to_broadcast([P, per, width]), ALU.mult).then_inc(k.dve_done.sem, 1)
        dve.wait_ge(*k.dve_done(2 * i + (u + 1)))
        dve.sem_inc(k.dve_turn.sem, 1)
        dve.tensor_reduce(kept[:, bass.ds((2 * i + u) * per, per)], own, AX.X, ALU.add).then_inc(k.evicted.sem, 1)
    linear(k, stream, None, None, dve_evict=evict, products=products, counts={k.dve_done: stream.groups}, then=then)
    return kept


def stage_gains(k, weight, scale):
    nc = k.nc
    n = len(scale)
    with nc.Block() as block:
        @block.vector
        def _(dve):
            for c, s in enumerate(scale):
                ins = dve.tensor_scalar(k.gain[:, c, :], s, 1.0, None, ALU.add)
                ins.then_inc(k.dve_done.sem, 1)
            if weight is not None:
                for c in range(n):
                    dve.wait_ge(*k.dve_done(c + 1))
                    dve.tensor_tensor(k.gain[:, c, :], k.gain[:, c, :], weight, ALU.mult).then_inc(k.dve_done.sem, 1)
    k.dve_done.counted(n * (2 if weight is not None else 1))


def stage_conv_input(k):
    pad = view(k, A_PAD, DT, 542)

    def act_evict(act, i, u):
        n = 2 * i + u
        act.wait_ge(*k.evicted(2 * i + (u - 1)))
        act.activation(k.stage[:, u, 0, :512], k.bank[4 * u + 1][:, :], ACT.Sigmoid,
                       bias=k.v("b_cgate", n)).then_inc(k.act_done.sem, 1)

    def dve_evict(dve, i, u):
        n = 2 * i + u
        dve.wait_ge(*k.act_done(2 * i + (u + 1)))
        dve.scalar_tensor_tensor(pad[:, bass.ds(n, 1), 30:542].rearrange("p a t -> p (a t)"), k.bank[4 * u][:, :],
                                 k.v("b_cval", n), k.stage[:, u, 0, :512], ALU.add, ALU.mult
                                 ).then_inc(k.evicted.sem, 1)

    def zeros(dve):
        dve.memset(pad[:, :, 0:30], 0.0)
    linear(k, k.streams["w_cpair"], lambda kk, c: k.H[:, kk, LAT:], [(0, 512)],
           act_evict, dve_evict, dve_other=zeros, counts={k.act_done: 8}, then=k.streams["w_qk"])


def causal_conv(k, first, tiles):
    pad = view(k, A_PAD, DT, 542)
    conv = view(k, A_CONV, DT, 512)

    def program(dve):
        with dve.Fori(0, tiles // 2) as i:
            for tap in range(CONV_K):
                for h in range(2):
                    j = 2 * i + (first + h)
                    y, x = flat(conv[:, bass.ds(j, 1), :]), flat(pad[:, bass.ds(j, 1), tap:tap + 512])
                    wt = k.v("conv_w", j * CONV_K + tap)
                    if tap:
                        dve.wait_ge(*k.dve_done(2 * CONV_K * i + (2 * tap + h - 1)))
                        dve.sem_inc(k.dve_turn.sem, 1)
                        dve.scalar_tensor_tensor(y, x, wt, y, ALU.mult, ALU.add).then_inc(k.dve_done.sem, 1)
                    else:
                        dve.tensor_scalar(y, x, wt, k.v("conv_b", j), ALU.mult, ALU.add).then_inc(k.dve_done.sem, 1)
    return program


def stage_queries_and_conv(k):
    qk = view(k, A_QK, 16, 512)

    def act_evict(act, i, u):
        for g in range(2):
            n = 4 * i + (2 * u + g)
            ins = act.activation(flat(qk[:, bass.ds(n, 1), :]), k.bank[4 * u + g][:, :], ACT.Identity,
                                 bias=k.v("b_qk", n))
        ins.then_inc(k.evicted.sem, 1)

    linear(k, k.streams["w_qk"], lambda kk, c: k.H[:, kk, LAT:], [(0, 512)], act_evict,
           dve_other=causal_conv(k, 0, 4), counts={k.dve_done: 4 * CONV_K}, then=k.streams["w_v"])


def stage_values(k):
    v = view(k, A_V, 4, 2048)
    bias = k.stage[0:1, :, :, :].rearrange("p a b c -> p (a b c)")[:, :2048]
    with k.nc.Block() as block:
        @block.sync
        def _(sp):
            sp.dma_start(bias, k.ap["b_v"]).then_inc(k.loaded.sem, 16)
            sp.wait_ge(*k.loaded(16))
    k.loaded.counted(16)

    def products(pe, i, u):
        for t in range(4):
            for kk in range(DT):
                pe.matmul(k.bank[4 * u + t][:, :], k.H[:, kk, LAT + t * P:LAT + (t + 1) * P],
                          k.W[u][:, kk * 512:(kk + 1) * 512], start=kk == 0, stop=False)
            mm = pe.matmul(k.bank[4 * u + t][:, :], k.mean[0:1, 3, :], bias[:, bass.ds((2 * i + u) * 512, 512)],
                           start=False, stop=True)
        return mm

    def act_evict(act, i, u):
        for t in range(4):
            ins = act.activation(v[:, t, bass.ds((2 * i + u) * 512, 512)], k.bank[4 * u + t][:, :], ACT.Copy)
        ins.then_inc(k.evicted.sem, 1)
    linear(k, k.streams["w_v"], None, None, act_evict, products=products,
           dve_other=causal_conv(k, 4, 4), counts={k.dve_done: 4 * CONV_K}, then=k.streams["w_ga"])


def stage_rope_tables(k):
    pos = k.arena[:, A_P:A_P + 512]
    posi = k.arena[:, A_P + 512:A_P + 1024].bitcast(I32)
    ang, turns = k.arena[:, A_TMP:A_TMP + 512], k.arena[:, A_TMP + 512:A_TMP + 1024]
    cos, sin = k.arena[:, A_COS:A_COS + 512], k.arena[:, A_SIN:A_SIN + 512]
    TWO_PI = 2 * np.pi
    c1 = 6.28125
    c2 = 0.0019350051879882812
    c3 = float(TWO_PI - c1 - c2)
    magic = float(1.5 * 2 ** 23)
    pi_in = float(np.nextafter(np.float32(np.pi), np.float32(0)))
    d = k.dve_done
    with k.nc.Block() as block:
        @block.sync
        def _(sp):
            sp.dma_start(posi, k.ap["positions_b"]).then_inc(k.loaded.sem, 16)

        @block.vector
        def _(dve):
            def step(ins, n):
                ins.then_inc(d.sem, 1)
                dve.wait_ge(*d(n))
            dve.wait_ge(*k.loaded(16))
            step(dve.tensor_copy(pos, posi), 1)
            step(dve.tensor_scalar(ang, pos, k.v("inv_freq"), None, ALU.mult), 2)
            step(dve.tensor_scalar(turns, ang, float(1 / TWO_PI), None, ALU.mult), 3)
            step(dve.tensor_scalar(turns, turns, magic, None, ALU.add), 4)
            step(dve.tensor_scalar(turns, turns, -magic, None, ALU.add), 5)
            step(dve.scalar_tensor_tensor(ang, turns, -c1, ang, ALU.mult, ALU.add), 6)
            step(dve.scalar_tensor_tensor(ang, turns, -c2, ang, ALU.mult, ALU.add), 7)
            step(dve.scalar_tensor_tensor(ang, turns, -c3, ang, ALU.mult, ALU.add), 8)
            step(dve.tensor_scalar(sin, ang, pi_in, -pi_in, ALU.min, ALU.max), 9)
            step(dve.tensor_scalar(ang, ang, float(np.pi / 2), None, ALU.add), 10)
            step(dve.tensor_scalar(turns, ang, float(np.pi), -float(TWO_PI), ALU.is_gt, ALU.mult), 11)
            step(dve.tensor_tensor(ang, ang, turns, ALU.add), 12)
            step(dve.tensor_scalar(cos, ang, pi_in, -pi_in, ALU.min, ALU.max), 13)

        @block.scalar
        def _(act):
            act.wait_ge(*d(13))
            act.activation(sin, sin, ACT.Sin)
            act.activation(cos, cos, ACT.Sin)
    k.loaded.counted(16)
    d.counted(13)


def stage_retention(k):
    qk = view(k, A_QK, 16, 512)
    v = view(k, A_V, 4, 2048)
    cos, sin = k.arena[:, A_COS:A_COS + 512], k.arena[:, A_SIN:A_SIN + 512]
    tmp = view(k, A_TMP, 2, 512)
    decay = view(k, A_DECAY, 2, 512)
    probs = k.arena[:, A_P:A_P + 1280]
    at = [0, 512, 896, 1152]
    scale = float(P ** -0.5)
    rotated, scored, summed, mean_in, variance_in = k.more[0:5]
    roped, weighted, centred, normed, inverted = k.more[5:10]
    copied, squared, tabled = k.more[10:13]
    B = k.bank
    where = [(2, 0), (3, 0), (4, 0), (3, 384)]
    with k.nc.Block() as block:
        @block.sync
        def _(sp):
            for h in range(RET_HEADS):
                if h >= 2:
                    sp.wait_ge(*weighted(4 * (h - 1)))
                sp.dma_start(decay[:, h % 2, :], k.ap["decay"][h]).then_inc(tabled.sem, 16)
                sp.wait_ge(*tabled(16 * (h + 1)))

        @block.tensor
        def _(pe):
            def rotate(h):
                for s in range(2):
                    mm = pe.matmul(B[s][:, :], k.rot[:, :], qk[:, 2 * h + s, :], start=True, stop=True)
                mm.then_inc(rotated.sem, 1)
            rotate(0)
            for h in range(RET_HEADS + 1):
                if h < RET_HEADS:
                    pe.wait_ge(*roped(2 * (h + 1)))
                    if h:
                        pe.wait_ge(*weighted(4 * h))
                    for j in range(4):
                        bank, col = where[j]
                        pe.matmul(B[bank][:, col:col + 512 - j * P], qk[:, 2 * h + 1, j * P:(j + 1) * P],
                                  qk[:, 2 * h, j * P:], start=True, stop=True).then_inc(scored.sem, 1)
                if h:
                    pe.wait_ge(*centred(2 * h))
                    for e in range(2):
                        pe.wait_ge(*squared(2 * (h - 1) + e + 1))
                        mm = pe.matmul(B[5][:, :], k.mean[:, 1, :], k.sq[:, e, :], start=e == 0, stop=e == 1)
                    mm.then_inc(variance_in.sem, 1)
                if h + 1 < RET_HEADS:
                    rotate(h + 1)
                if h == RET_HEADS:
                    break
                if h:
                    pe.wait_ge(*copied(2 * h))
                for j in range(4):
                    pe.wait_ge(*weighted(4 * h + j + 1))
                    for e in range(2):
                        mm = pe.matmul(B[6 + e][:, j * P:], v[:, j, h * 256 + e * P:h * 256 + (e + 1) * P],
                                       probs[:, at[j]:at[j] + 512 - j * P], start=j == 0, stop=j == 3)
                mm.then_inc(summed.sem, 1)
                pe.wait_ge(*copied(2 * h + 2))
                if h:
                    pe.wait_ge(*inverted(2 * h))
                for e in range(2):
                    mm = pe.matmul(B[5][:, :], k.mean[:, 1, :], qk[:, 2 * h + e, :], start=e == 0, stop=e == 1)
                mm.then_inc(mean_in.sem, 1)

        @block.scalar
        def _(act):
            for h in range(RET_HEADS + 1):
                if h:
                    p = h - 1
                    for e in range(2):
                        act.wait_ge(*centred(2 * p + e + 1))
                        if p:
                            act.wait_ge(*variance_in(p))
                        act.activation(k.sq[:, e, :], qk[:, 2 * p + e, :], ACT.Square).then_inc(squared.sem, 1)
                    act.wait_ge(*inverted(2 * p + 2))
                    act.activation(k.rstd[:, :], k.rstd[:, :], ACT.Sqrt).then_inc(k.act_done.sem, 1)
                if h < RET_HEADS:
                    act.wait_ge(*summed(h + 1))
                    for e in range(2):
                        act.activation(qk[:, 2 * h + e, :], B[6 + e][:, :], ACT.Copy).then_inc(copied.sem, 1)
                if h:
                    act.wait_ge(*normed(p + 1))
                    for e in range(2):
                        act.activation(qk[:, 2 * p + e, :], qk[:, 2 * p + e, :], ACT.Identity,
                                       bias=k.v("gn_b", 2 * p + e), scale=k.v("gn_g", 2 * p + e))

        @block.vector
        def _(dve):
            def rope(h):
                dve.wait_ge(*rotated(h + 1))
                for s in range(2):
                    x = qk[:, 2 * h + s, :]
                    if h:
                        dve.wait_ge(*roped(2 * h))
                    dve.tensor_tensor(tmp[:, s, :], B[s][:, :], sin, ALU.mult).then_inc(k.dve_done.sem, 1)
                    dve.tensor_tensor(x, x, cos, ALU.mult).then_inc(k.dve_done.sem, 1)
                for s in range(2):
                    x = qk[:, 2 * h + s, :]
                    dve.wait_ge(*k.dve_done(4 * h + 2 * s + 2))
                    dve.tensor_tensor(x, x, tmp[:, s, :], ALU.add).then_inc(roped.sem, 1)
            rope(0)
            for h in range(RET_HEADS + 1):
                if h < RET_HEADS:
                    if h:
                        dve.wait_ge(*summed(h))
                    dve.wait_ge(*tabled(16 * (h + 1)))
                    for j in range(4):
                        bank, col = where[j]
                        dve.wait_ge(*scored(4 * h + (j + 1 if j != 1 else 4)))
                        dve.scalar_tensor_tensor(probs[:, at[j]:at[j] + 512 - j * P], B[bank][:, col:col + 512 - j * P],
                                                 scale, decay[:, h % 2, :512 - j * P], ALU.mult, ALU.mult
                                                 ).then_inc(weighted.sem, 1)
                if h + 1 < RET_HEADS:
                    rope(h + 1)
                if h:
                    p = h - 1
                    dve.wait_ge(*variance_in(h))
                    dve.tensor_scalar(k.rstd[:, :], B[5][:, :], LN_EPS, None, ALU.add).then_inc(inverted.sem, 1)
                    dve.wait_ge(*inverted(2 * p + 1))
                    dve.reciprocal(k.rstd[:, :], k.rstd[:, :]).then_inc(inverted.sem, 1)
                    dve.wait_ge(*k.act_done(h))
                    for e in range(2):
                        x = qk[:, 2 * p + e, :]
                        ins = dve.tensor_tensor(x, x, k.rstd[:, :], ALU.mult)
                    ins.then_inc(normed.sem, 1)
                if h < RET_HEADS:
                    dve.wait_ge(*mean_in(h + 1))
                    for e in range(2):
                        x = qk[:, 2 * h + e, :]
                        dve.tensor_tensor(x, x, B[5][:, :], ALU.subtract).then_inc(centred.sem, 1)
    n = RET_HEADS
    for s, m in ((k.act_done, n), (rotated, n), (scored, 4 * n), (summed, n), (mean_in, n), (variance_in, n),
                 (roped, 2 * n), (weighted, 4 * n), (centred, 2 * n), (normed, n), (inverted, 2 * n),
                 (copied, 2 * n), (squared, 2 * n), (tabled, 16 * n), (k.dve_done, 4 * n)):
        s.counted(m)


def stage_gate(k, stream, func, bias, dst_at, times, then):
    dst = view(k, dst_at, 2 * stream.groups, 512)

    def act_evict(act, i, u):
        act.wait_ge(*k.evicted(2 * i + (u - 1)))
        for g in range(2):
            n = 4 * i + (2 * u + g)
            out = k.stage[:, u, g, :512] if times else flat(dst[:, bass.ds(n, 1), :])
            ins = act.activation(out, k.bank[4 * u + g][:, :], func, bias=k.v(bias, n))
        ins.then_inc((k.act_done if times else k.evicted).sem, 1)

    def dve_evict(dve, i, u):
        dve.wait_ge(*k.act_done(2 * i + (u + 1)))
        for g in range(2):
            x = flat(dst[:, bass.ds(4 * i + (2 * u + g), 1), :])
            ins = dve.tensor_tensor(x, x, k.stage[:, u, g, :512], ALU.mult)
        ins.then_inc(k.evicted.sem, 1)
    linear(k, stream, lambda kk, c: k.H[:, kk, LAT:], [(0, 512)], act_evict,
           dve_evict if times else None, counts={k.act_done: stream.groups} if times else None, then=then)


def stage_conv_out(k):
    m, conv = view(k, A_PAD, DT, 512), view(k, A_CONV, DT, 512)

    def dve_evict(dve, i, u):
        for g in range(2):
            x = flat(m[:, bass.ds(4 * i + (2 * u + g), 1), :])
            ins = dve.tensor_tensor(x, x, k.bank[4 * u + g][:, :], ALU.mult)
        ins.then_inc(k.evicted.sem, 1)
    linear(k, k.streams["w_conv_out"], lambda kk, c: conv[:, kk, :], [(0, 512)], dve_evict=dve_evict,
           then=k.streams["w_g"])


def stage_retention_out(k):
    m, gate, r = view(k, A_PAD, DT, 512), view(k, A_CONV, DT, 512), view(k, A_QK, 16, 512)

    def dve_evict(dve, i, u):
        for g in range(2):
            n = 4 * i + (2 * u + g)
            x = flat(gate[:, bass.ds(n, 1), :])
            dve.tensor_tensor(x, x, k.bank[4 * u + g][:, :], ALU.mult).then_inc(k.dve_done.sem, 1)
        for g in range(2):
            n = 4 * i + (2 * u + g)
            dve.wait_ge(*k.dve_done(4 * i + (2 * u + g + 1)))
            dve.sem_inc(k.dve_turn.sem, 1)
            ins = dve.tensor_tensor(flat(m[:, bass.ds(n, 1), :]), flat(m[:, bass.ds(n, 1), :]),
                                    flat(gate[:, bass.ds(n, 1), :]), ALU.add)
        ins.then_inc(k.evicted.sem, 1)
    linear(k, k.streams["w_ret_out"], lambda kk, c: r[:, kk, :], [(0, 512)], dve_evict=dve_evict,
           counts={k.dve_done: 8}, then=k.streams["w_out"])


def residual(k, stream, src, chunks, gate, alpha, then=None, ready=None):
    tiles = stream.cols // P
    nch = len(chunks)

    def tile(n, c):
        a, b = chunks[c]
        return k.X[:, bass.ds(n, 1), a:b].rearrange("p a t -> p (a t)")

    def act_evict(act, i, u):
        for g in range(tiles):
            for c in range(nch):
                n = tiles * (2 * i + u) + g
                ins = act.activation(tile(n, c), tile(n, c), ACT.Copy, scale=alpha)
        ins.then_inc(k.act_done.sem, 1)

    def dve_evict(dve, i, u):
        if alpha != 1.0:
            dve.wait_ge(*k.act_done(2 * i + (u + 1)))
            dve.sem_inc(k.dve_turn.sem, 1)
        for g in range(tiles):
            for c in range(nch):
                n = tiles * (2 * i + u) + g
                a, b = chunks[c]
                ins = dve.scalar_tensor_tensor(tile(n, c), k.bank[4 * u + nch * g + c][:, :b - a],
                                               gate(n, c) if gate else 1.0,
                                               tile(n, c), ALU.mult, ALU.add)
        ins.then_inc(k.evicted.sem, 1)
    return Linear(k, stream, src, chunks, act_evict if alpha != 1.0 else None, dve_evict,
                  counts={k.act_done: stream.groups} if alpha != 1.0 else None, then=then, ready=ready)


def split_tile(k, dve, done, parts, n):
    whole, hi, lo = (flat(p[:, bass.ds(n, 1), :]) for p in parts)
    dve.wait_ge(*k.dve_done(done))
    dve.sem_inc(k.dve_turn.sem, 1)
    dve.tensor_copy(hi, whole).then_inc(k.dve_done.sem, 1)
    dve.wait_ge(*k.dve_done(done + 1))
    dve.sem_inc(k.dve_turn.sem, 1)
    return dve.tensor_tensor(lo, whole, hi, ALU.subtract)


def ffn1_up(k, stream, parts, then):
    hidden = parts[0]
    taps = view(k, A_TAPS, 4, 512)

    def act_evict(act, i, u):
        act.wait_ge(*k.evicted(2 * i + (u - 1)))
        for g in range(2):
            act.activation(k.stage[:, u, g, 2:514], k.bank[4 * u + g][:, :], ACT.Copy).then_inc(k.act_done.sem, 1)
        act.wait_ge(*k.dve_done(16 * i + (8 * u + 6)))
        act.sem_inc(k.act_turn.sem, 1)
        act.activation(k.stage[:, u, 1, 2:514], taps[:, 2 * u + 1, :], ACT.Silu).then_inc(k.act_done.sem, 1)

    def dve_evict(dve, i, u):
        n = 2 * i + u
        d = 16 * i + 8 * u
        dve.wait_ge(*k.act_done(6 * i + (3 * u + 2)))
        dve.sem_inc(k.dve_turn.sem, 1)
        for tap in range(3):
            for g in range(2):
                y, x = taps[:, 2 * u + g, :], k.stage[:, u, g, tap:tap + 512]
                wt = k.v("ffn_w", n * 6 + (6 * stream.first + 3 * g + tap))
                if tap:
                    dve.wait_ge(*k.dve_done(d + (2 * tap + g - 1)))
                    dve.sem_inc(k.dve_turn.sem, 1)
                    dve.scalar_tensor_tensor(y, x, wt, y, ALU.mult, ALU.add).then_inc(k.dve_done.sem, 1)
                else:
                    dve.tensor_scalar(y, x, wt, k.v("ffn_b", n * 2 + (2 * stream.first + g)), ALU.mult, ALU.add
                                      ).then_inc(k.dve_done.sem, 1)
        dve.wait_ge(*k.act_done(6 * i + (3 * u + 3)))
        dve.sem_inc(k.dve_turn.sem, 1)
        dve.tensor_tensor(flat(hidden[:, bass.ds(n, 1), :]), taps[:, 2 * u, :], k.stage[:, u, 1, 2:514], ALU.mult
                          ).then_inc(k.dve_done.sem, 1)
        split_tile(k, dve, d + 7, parts, n).then_inc(k.evicted.sem, 1)
    return Linear(
        k, stream, h_parts(k, [(LAT, TOK)], LAT), [(0, 512)], act_evict, dve_evict, counts={k.act_done: 3 * stream.groups, k.dve_done: 8 * stream.groups}, then=then)


def h_parts(k, chunks, first):
    hi, lo = k.h_high, k.low_tiles(TOK - first)[0]
    return lambda kk, c: (hi[:, kk, slice(*chunks[c])], lo[:, kk, chunks[c][0] - first:chunks[c][1] - first])


def norm_parts(k, a, b, first):
    hi, (lo, whole) = k.h_high, k.low_tiles(TOK - first)
    return (lambda j: whole[:, j, a - first:b - first],
            lambda j: (hi[:, j, a:b], lo[:, j, a - first:b - first]))


def stage_ffn(k, up, down, chunks, make_up, gate, alpha, then):
    pieces = PIECES[sum(b - a for a, b in chunks)]
    first = chunks[0][0]
    linears = []
    for n, (_, tiles) in enumerate(pieces):
        parts = k.hidden(tiles, TOK - first)
        linears.append(make_up(k, k.streams[up, n], parts, k.streams[down, n]))

        def tile_there(pe, kk, tiles=tiles):
            pe.wait_ge(*k.evicted(kk + 1 - tiles))
        linears.append(residual(
            k, k.streams[down, n],
            lambda kk, c, parts=parts: tuple(p[:, kk, chunks[c][0] - first:chunks[c][1] - first] for p in parts[1:]),
            chunks, gate, alpha if n == 0 else 1.0, k.streams[up, n + 1] if n + 1 < len(pieces) else then, tile_there))
    run(k, linears)


def x_lat(k):
    return lambda j: k.X[:, j, LAT:]


def block_one(k):
    st = k.streams
    h = lambda j: k.H[:, j, LAT:]
    whole, parts = norm_parts(k, LAT, TOK, LAT)
    kept = stage_modulation(k, st["w_ada"], 1, lambda kk, which: k.v("c", kk), st["w_cpair"])
    with k.nc.Block() as block:
        @block.vector
        def _(dve):
            dve.tensor_tensor(k.mod1[:, :], kept, k.v("b_ada", 0, 48), ALU.add)
    stage_gains(k, None, [k.mod1[:, 8:16]])
    norm(k, x_lat(k), h, DT, LAT, TOK, 0, LN_EPS, True, lambda j: k.gain[:, 0, j:j + 1],
         shift=lambda j: k.mod1[:, j:j + 1])
    stage_conv_input(k)
    stage_queries_and_conv(k)
    stage_values(k)
    conv = view(k, A_CONV, DT, 512)
    norm(k, lambda j: conv[:, j, :], lambda j: conv[:, j, :], DT, 0, 512, 0, LN_EPS, True,
         lambda j: k.v("cln_g", j), post=ACT.Silu, shift=lambda j: k.v("cln_b", j))
    stage_gate(k, st["w_ga"], ACT.Sigmoid, "b_ga", A_PAD, False, st["w_conv_out"])
    stage_conv_out(k)
    stage_rope_tables(k)
    stage_retention(k)
    stage_gate(k, st["w_g"], ACT.Silu, "b_g", A_QK, True, st["w_gb"])
    stage_gate(k, st["w_gb"], ACT.Sigmoid, "b_gb", A_CONV, False, st["w_ret_out"])
    stage_retention_out(k)
    m = view(k, A_PAD, DT, 512)
    run(k, [residual(k, st["w_out"], lambda kk, c: m[:, kk, :], [(LAT, TOK)],
                     lambda n, c: k.mod1[:, bass.ds(16 + n, 1)], ALPHA, st["w_up", 0])])
    norm(k, x_lat(k), x_lat(k), DT, LAT, TOK, 0, LN_EPS, True, lambda j: k.v("ln1_g", j),
         shift=lambda j: k.v("ln1_b", j))
    stage_gains(k, None, [k.mod1[:, 32:40]])
    norm(k, x_lat(k), whole, DT, LAT, TOK, 0, LN_EPS, True, lambda j: k.gain[:, 0, j:j + 1],
         shift=lambda j: k.mod1[:, 24 + j:25 + j], parts=parts)
    with k.nc.Block() as block:
        @block.vector
        def _(dve):
            for u in range(2):
                dve.memset(k.stage[:, u, :, 0:2], 0.0)
    stage_ffn(k, "w_up", "w_down", [(LAT, TOK)], ffn1_up, lambda n, c: k.mod1[:, bass.ds(40 + n, 1)], ALPHA,
              st["w_mod"])
    norm(k, x_lat(k), x_lat(k), DT, LAT, TOK, 0, LN_EPS, True, lambda j: k.v("ln2_g", j),
         shift=lambda j: k.v("ln2_b", j))


HEADS2 = 4
CH = 2 * 64
NCH = TOK // CH
M2_QG = 0
M2_F = M2_QG + 8 * 512
M2_V = M2_F + 8 * TOK
M2_OUT = M2_V + 2 * NCH * 512
M2_WORK = M2_OUT + 8 * 512
ML_QP = 0
ML_KC = ML_QP + 4 * 660
ML_Q = ML_KC + 2 * 258
ML_K = ML_Q + 2 * 512
ML_O = ML_K + 2 * TOK
ML_RAW = M2_WORK
ML_ROWS = ML_O + 4 * 512


def chunks_both():
    return [(0, CTX), (LAT, TOK)]


def swiglu(chunks):
    widths = [b - a for a, b in chunks]
    at = [0, widths[0]]
    nch = len(chunks)

    def make(k, stream, parts, then):
        def act_evict(act, i, u):
            act.wait_ge(*k.evicted(2 * i + (u - 1)))
            s = flat(k.stage[:, u, :, :])
            for c in range(nch):
                ins = act.activation(s[:, at[c]:at[c] + widths[c]], k.bank[4 * u + c][:, :widths[c]], ACT.Silu)
            ins.then_inc(k.act_done.sem, 1)

        def dve_evict(dve, i, u):
            n = 2 * i + u
            dve.wait_ge(*k.act_done(2 * i + (u + 1)))
            dve.sem_inc(k.dve_turn.sem, 1)
            s = flat(k.stage[:, u, :, :])
            for c in range(nch):
                h = flat(parts[0][:, bass.ds(n, 1), at[c]:at[c] + widths[c]])
                ins = dve.tensor_tensor(h, s[:, at[c]:at[c] + widths[c]], k.bank[4 * u + nch + c][:, :widths[c]],
                                        ALU.mult)
            ins.then_inc(k.dve_done.sem, 1)
            split_tile(k, dve, 4 * i + (2 * u + 1), parts, n).then_inc(k.evicted.sem, 1)
        return Linear(k, stream, h_parts(k, chunks, chunks[0][0]), chunks, act_evict, dve_evict,
                      counts={k.act_done: stream.groups, k.dve_done: 2 * stream.groups}, then=then)
    return make


def stage_half_gates(k, gates):
    with k.nc.Block() as block:
        @block.vector
        def _(dve):
            for c, g in enumerate(gates):
                dve.tensor_scalar(k.gain[:, c, :], g, 0.5, None, ALU.mult)


def stage_token_values(k, stream, w, sets, tiles, first, dst, last_rows=P):
    nc = k.nc
    n = sets * tiles
    fetched = k.fetched is not None
    assert not fetched or k.fetched is stream
    k.fetched = None
    with nc.Block() as block:
        @block.sync
        def _(sp):
            for s in range(0 if fetched else sets):
                sp.dma_start(k.W[s][:, :SLOT], w[s]).then_inc(k.weights_in[s].sem, 16)

        @block.tensor
        def _(pe):
            for m in range(n):
                s, t = divmod(m, tiles)
                rows = last_rows if t == tiles - 1 else P
                if t == 0:
                    pe.wait_ge(*k.weights_in[s](16))
                if m >= 8:
                    pe.wait_ge(*k.act_done(m - 7))
                for kk in range(DT):
                    mm = pe.matmul(k.bank[m % 8][:rows, :], k.H[:, kk, first + t * P:first + t * P + rows],
                                   k.W[s][:, kk * 512:(kk + 1) * 512], start=kk == 0, stop=kk == DT - 1)
                mm.then_inc(k.pe_done.sem, 1)

        @block.scalar
        def _(act):
            for m in range(n):
                s, t = divmod(m, tiles)
                rows = last_rows if t == tiles - 1 else P
                act.wait_ge(*k.pe_done(m + 1))
                act.activation(dst(s, t)[:rows], k.bank[m % 8][:rows, :], ACT.Copy).then_inc(k.act_done.sem, 1)
    for s in range(sets):
        k.weights_in[s].counted(16)
    k.pe_done.counted(n)
    k.act_done.counted(n)


def stage_hgrn(k):
    qg = view(k, M2_QG, 8, 512)
    fpre = view(k, M2_F, 8, TOK)
    val = k.arena[:, M2_V:M2_V + 2 * NCH * 512].rearrange("p (s t e) -> p s t e", s=2, t=NCH)
    out = view(k, M2_OUT, 8, 512)
    pres = [k.arena[:, M2_WORK:M2_WORK + TOK], k.W[1][:, 0:TOK]]
    keys = [k.arena[:, M2_WORK + TOK:M2_WORK + 2 * TOK], k.W[1][:, TOK:2 * TOK]]
    suf = k.arena[:, M2_WORK + 2 * TOK:M2_WORK + 3 * TOK]
    both = view(k, M2_WORK + 3 * TOK, 2, 512)
    decayed = k.arena[:, M2_WORK + 3 * TOK + 1024:M2_WORK + 3 * TOK + 1536]
    score = k.sq
    spare = k.stage[:, :, :, :].rearrange("p a b c -> p (a b c)")
    key_t = spare[:, 0:TOK].rearrange("p (c d) -> p c d", d=P)
    state = spare[:, TOK:2 * TOK].rearrange("p (c d) -> p c d", d=P)
    gated, ready, scored, merged, turned, turn_copied, kv_done, states, summed, taken = k.more[0:10]
    B = k.bank
    units = [(h, d) for h in range(HEADS2) for d in range(2)]
    order = [[0, 1, 2, 3, 4, 5], [1, 0, 5, 4, 3, 2]]
    levels = 7
    with k.nc.Block() as block:
        @block.vector
        def _(dve):
            for d in range(2):
                dve.memset(score[:, d, :], 0.0)
            dve.tensor_tensor(k.v("lb1", 0, 8), k.v("lb0", 0, 8), k.v("lb1", 0, 8), ALU.subtract
                              ).then_inc(k.dve_done.sem, 1)
            dve.wait_ge(*k.act_done(1))
            dve.tensor_scalar(k.v("lb1", 0, 8), k.v("lb0", 0, 8), -1.0, 1.0, ALU.mult, ALU.add)

        @block.scalar
        def _(act):
            act.wait_ge(*k.dve_done(1))
            act.activation(k.v("lb0", 0, 8), k.v("lb1", 0, 8), ACT.Sigmoid).then_inc(k.act_done.sem, 1)
    k.dve_done.counted(1)
    k.act_done.counted(1)
    links = []
    with k.nc.Block() as block:
        @block.scalar
        def _(act):
            def gates(n):
                h, d = units[n]
                act.activation(pres[n % 2], fpre[:, 2 * h + d, :], ACT.Sigmoid)
                act.activation(keys[n % 2], fpre[:, 2 * h + d, :], ACT.Sigmoid, scale=-1.0).then_inc(gated.sem, 1)
            gates(0)
            for n in range(len(units)):
                if n + 1 < len(units):
                    if n:
                        act.wait_ge(*taken(n))
                    gates(n + 1)
                act.wait_ge(*turned(n + 1))
                act.activation(flat(key_t[:, 0:4, :]), B[4][:, :], ACT.Copy)
                act.activation(flat(key_t[:, 4:6, :]), B[5][:, :256], ACT.Copy).then_inc(turn_copied.sem, 1)

        @block.tensor
        def _(pe):
            def sums(n):
                h, d = units[n]
                pe.wait_ge(*merged(8 * n + 8))
                pe.wait_ge(*states(n + 1))
                for i in range(2, NCH):
                    c = order[d][i]
                    t = slice((c - 2) * CH, (c - 1) * CH)
                    pe.matmul(B[4][:, t], val[:, 0, c, h * P:(h + 1) * P], score[:, d, t], start=True, stop=False)
                    mm = pe.matmul(B[4][:, t], state[:, i, :], decayed[:, t], start=False, stop=True)
                mm.then_inc(summed.sem, 1)

            for n, (h, d) in enumerate(units):
                key = keys[n % 2]
                for lev in range(levels + 1):
                    pe.wait_ge(*ready(9 * n + lev + 1))
                    if 8 * n + lev >= 4:
                        pe.wait_ge(*merged(8 * n + lev - 3))
                    for c in range(4):
                        t = slice(c * CH, (c + 1) * CH)
                        kx = key[:, CTX + c * CH:CTX + (c + 1) * CH] if lev == 0 else both[:, lev % 2, t]
                        qx = qg[:, h, t] if lev == 0 else both[:, lev % 2, t]
                        mm = pe.matmul(B[lev % 4][:, t], kx, qx, start=True, stop=True)
                    mm.then_inc(scored.sem, 1)
                    if n and lev == 1:
                        sums(n - 1)
                pe.wait_ge(*ready(9 * n + 9))
                if n:
                    pe.wait_ge(*taken(n))
                for c in range(NCH):
                    mm = pe.transpose(B[4 + c // 4][:, (c % 4) * P:(c % 4 + 1) * P], key[:, c * CH:(c + 1) * CH],
                                      k.ident[:, :])
                mm.then_inc(turned.sem, 1)
                pe.wait_ge(*turn_copied(n + 1))
                for c in range(NCH):
                    mm = pe.matmul(B[6 + c // 4][:, (c % 4) * P:(c % 4 + 1) * P], key_t[:, c, :],
                                   val[:, 0, c, h * P:(h + 1) * P], start=True, stop=True)
                mm.then_inc(kv_done.sem, 1)
            sums(len(units) - 1)

        @block.vector
        def _(dve):
            d_ = k.dve_done

            def link(ins):
                links.append(1)
                ins.then_inc(d_.sem, 1)
                dve.wait_ge(*d_(len(links)))

            def merge(n, lev):
                h, d = units[n]
                dve.wait_ge(*scored(8 * n + lev + 1))
                dve.copy_predicated(score[:, d, :].rearrange("p (c t) -> p c t", t=CH),
                                    k.masks[:, 8 * d + lev:8 * d + lev + 1, :].to_broadcast([P, 4, CH]),
                                    B[lev % 4][:, :].rearrange("p (c t) -> p c t", t=CH)).then_inc(merged.sem, 1)

            def carry(n):
                h, d = units[n]
                pre = pres[n % 2]
                merge(n, levels)
                dve.wait_ge(*kv_done(n + 1))
                for i in range(1, NCH):
                    c = order[d][i - 1]
                    kv = B[6 + c // 4][:, (c % 4) * P:(c % 4 + 1) * P]
                    at = c * CH + (CH - 1 if d == 0 else 0)
                    if i == 1:
                        link(dve.tensor_copy(state[:, i, :], kv))
                    else:
                        link(dve.scalar_tensor_tensor(state[:, i, :], state[:, i - 1, :], pre[:, at:at + 1], kv,
                                                      ALU.mult, ALU.add))
                dve.sem_inc(states.sem, 1)

            def take(n):
                h, d = units[n]
                dve.wait_ge(*summed(n + 1))
                if d == 0:
                    link(dve.tensor_scalar(out[:, h, :], B[4][:, :], float(P ** -0.5), None, ALU.mult))
                else:
                    link(dve.scalar_tensor_tensor(out[:, h, :], B[4][:, :], float(P ** -0.5), out[:, h, :],
                                                  ALU.mult, ALU.add))
                dve.sem_inc(taken.sem, 1)

            for n, (h, d) in enumerate(units):
                pre, key = pres[n % 2], keys[n % 2]
                one = k.v("lb1", 4 * d + h)
                dve.wait_ge(*gated(n + 1))
                dve.tensor_scalar(pre, pre, one, k.v("lb0", 4 * d + h), ALU.mult, ALU.add)
                dve.memset(suf, 1.0)
                link(dve.tensor_scalar(key, key, one, None, ALU.mult))
                dve.sem_inc(ready.sem, 1)
                qh, kh = 1 - d, d
                for lev in range(1, levels + 1):
                    m = 1 << (lev - 1)
                    edge = m - 1 if d == 0 else 0

                    def halves(ap):
                        return ap.rearrange("p (b s m) -> p b s m", s=2, m=m)
                    x = halves(both[:, lev % 2, :])
                    q4, p4, s4, k4 = halves(qg[:, h, :]), halves(pre), halves(suf), halves(key)
                    nctx = CTX // (2 * m)
                    if lev > 2:
                        dve.wait_ge(*scored(8 * n + lev - 1))
                    elif n:
                        dve.wait_ge(*scored(8 * n))
                    dve.tensor_tensor(x[:, :, qh, :], q4[:, :, qh, :], p4[:, nctx:, qh, :], ALU.mult)
                    link(dve.tensor_tensor(x[:, :, kh, :], k4[:, nctx:, kh, :], s4[:, nctx:, kh, :], ALU.mult))
                    dve.sem_inc(ready.sem, 1)
                    nb = TOK // (2 * m)
                    link(dve.tensor_tensor(s4[:, :, kh, :], s4[:, :, kh, :],
                                           p4[:, :, qh, edge:edge + 1].to_broadcast([P, nb, m]), ALU.mult))
                    link(dve.tensor_tensor(p4[:, :, qh, :], p4[:, :, qh, :],
                                           p4[:, :, kh, edge:edge + 1].to_broadcast([P, nb, m]), ALU.mult))
                    if n and lev == 1:
                        carry(n - 1)
                    merge(n, lev - 1)
                    if n and lev == 3:
                        take(n - 1)
                dve.tensor_tensor(decayed, qg[:, h, :], pre[:, CTX:], ALU.mult)
                link(dve.tensor_tensor(key, key, suf, ALU.mult))
                dve.sem_inc(ready.sem, 1)
            carry(len(units) - 1)
            take(len(units) - 1)
    n = len(units)
    for s, m in ((gated, n), (ready, 9 * n), (scored, 8 * n), (merged, 8 * n), (turned, n), (turn_copied, n),
                 (kv_done, n), (states, n), (summed, n), (taken, n), (k.dve_done, len(links))):
        s.counted(m)


def stage_head_norms(k, at, weight, gates):
    out = view(k, M2_OUT, 8, 512)
    for h in range(HEADS2):
        norm(k, lambda j, h=h: out[:, at + h, :], lambda j, h=h: out[:, at + h, :], 1, 0, 512, 2, RMS_EPS, False,
             lambda j, h=h: k.v(weight, h))
    with k.nc.Block() as block:
        @block.vector
        def _(dve):
            for h in range(HEADS2):
                dve.tensor_tensor(out[:, at + h, :], out[:, at + h, :], gates[:, h, :], ALU.mult)


def grid(ap):
    return ap.rearrange("p (r c) -> p r c", c=64)


def stage_mlstm_inputs(k):
    pads = k.arena[:, ML_QP:ML_QP + 4 * 660].rearrange("p (t r c) -> p t r c", t=4, c=66)
    kctx = view(k, ML_KC, 2, 258)
    mq, mk = view(k, ML_Q, 2, 512), view(k, ML_K, 2, TOK)
    osig = view(k, ML_O, 4, 512)
    raw = view(k, ML_RAW, 4, TOK)
    src = lambda kk, c: k.H[:, kk, slice(*chunks_both()[c])]
    with k.nc.Block() as block:
        @block.vector
        def _(dve):
            dve.memset(k.arena[:, ML_QP:ML_Q], 0.0)

    def act_evict(act, i, u):
        for g in range(2):
            ins = act.activation(pads[:, 2 * u + g, 1:9, 1:65], grid(k.bank[4 * u + 2 * g + 1][:, :]), ACT.Copy)
            if u == 1:
                ins = act.activation(kctx[:, g, 1:257], k.bank[4 * u + 2 * g][:, :CTX], ACT.Copy)
        ins.then_inc(k.evicted.sem, 1)
    linear(k, k.streams["w_mqk"], src, chunks_both(), act_evict, then=k.streams["w_mo"])

    def o_evict(act, i, u):
        for g in range(2):
            ins = act.activation(flat(osig[:, bass.ds(4 * i + (2 * u + g), 1), :]), k.bank[4 * u + g][:, :], ACT.Sigmoid)
        ins.then_inc(k.evicted.sem, 1)

    def conv(dve):
        outs = [grid(mq[:, 0, :]), grid(mq[:, 1, :]), grid(mk[:, 0, CTX:]), grid(mk[:, 1, CTX:])]
        d = k.dve_done
        for tap in range(9):
            dy, dx = divmod(tap, 3)
            for t in range(4):
                x = pads[:, t, dy:dy + 8, dx:dx + 64]
                if tap:
                    dve.wait_ge(*d(4 * (tap - 1) + t + 1))
                    dve.scalar_tensor_tensor(outs[t], x, k.v("mconv_w", 9 * t + tap), outs[t], ALU.mult, ALU.add
                                             ).then_inc(d.sem, 1)
                else:
                    dve.tensor_scalar(outs[t], x, k.v("mconv_w", 9 * t), k.v("mconv_b", t), ALU.mult, ALU.add
                                      ).then_inc(d.sem, 1)
        for dx in range(3):
            for t in range(2):
                y, x, w = mk[:, t, :CTX], kctx[:, t, dx:dx + CTX], k.v("mconv_w", 9 * (2 + t) + 3 + dx)
                if dx:
                    dve.wait_ge(*d(36 + 2 * (dx - 1) + t + 1))
                    dve.scalar_tensor_tensor(y, x, w, y, ALU.mult, ALU.add).then_inc(d.sem, 1)
                else:
                    dve.tensor_scalar(y, x, w, k.v("mconv_b", 2 + t), ALU.mult, ALU.add).then_inc(d.sem, 1)
    linear(k, k.streams["w_mo"], lambda kk, c: k.H[:, kk, LAT:], [(0, 512)], o_evict, dve_other=conv,
           counts={k.dve_done: 42})
    with k.nc.Block() as block:
        @block.sync
        def _(sp):
            sp.dma_start(k.W[0][:, :DT * P], k.ap["w_gates"]).then_inc(k.weights_in[0].sem, 16)

        @block.tensor
        def _(pe):
            pe.wait_ge(*k.weights_in[0](16))
            for c, (a, b) in enumerate(chunks_both()):
                for kk in range(DT):
                    mm = pe.matmul(k.bank[c][:, :b - a], k.W[0][:, kk * P:(kk + 1) * P], k.H[:, kk, a:b],
                                   start=kk == 0, stop=kk == DT - 1)
            mm.then_inc(k.pe_done.sem, 1)

        @block.scalar
        def _(act):
            for t in range(2):
                act.activation(mq[:, t, :], mq[:, t, :], ACT.Silu)
                act.activation(mk[:, t, :], mk[:, t, :], ACT.Silu)
            act.wait_ge(*k.pe_done(1))
            for g in range(4):
                for c, (a, b) in enumerate(chunks_both()):
                    act.activation(raw[0:4, g, a:b], k.bank[c][32 * g:32 * g + 4, :b - a], ACT.Identity,
                                   bias=k.v("ml_gb")[32 * g:32 * g + 4])
    k.weights_in[0].counted(16)
    k.pe_done.counted(1)


def stage_mlstm(k):
    mq, mk = view(k, ML_Q, 2, 512), view(k, ML_K, 2, TOK)
    raw = view(k, ML_RAW, 4, TOK)
    val = k.arena[:, M2_V:M2_V + 2 * NCH * 512].rearrange("p (s t e) -> p s t e", s=2, t=NCH)
    out = view(k, M2_OUT, 8, 512)
    free = k.H[:, :, :].rearrange("p k t -> p (k t)")
    run = free[:, 0:2 * TOK].rearrange("p (d t) -> p d t", t=TOK)
    top = free[:, 2 * TOK:4 * TOK].rearrange("p (d t) -> p d t", t=TOK)
    ones = free[:, 4 * TOK:5 * TOK]
    soft = free[:, 5 * TOK:6 * TOK]
    a_t = free[:, 6 * TOK:6 * TOK + 48].rearrange("p (d c h) -> p d c h", d=2, h=4)
    negm = k.rstd
    wts = k.sq
    prob = k.stage[:, 0, :, :]
    absd = k.stage[:, 1, 0, :512]
    part = k.stage[:, 1, 1, :512]
    B = k.bank
    d_ = k.dve_done
    steps = []
    with k.nc.Block() as block:
        @block.scalar
        def _(act):
            a = 0
            for d in range(2):
                f = raw[0:4, 2 * d + 1, :]
                if d:
                    act.wait_ge(*d_(2))
                for n, (func, scale, bias, x) in enumerate(((ACT.Abs, 1.0, 0.0, f), (ACT.Exp, -1.0, 0.0, soft[0:4]),
                                                            (ACT.Ln, 1.0, 1.0, soft[0:4]))):
                    act.activation(soft[0:4], x, func, scale=scale, bias=bias).then_inc(k.act_done.sem, 1)
                    a += 1
                    act.wait_ge(*k.act_done(a))

        @block.vector
        def _(dve):
            def link(ins):
                steps.append(1)
                ins.then_inc(d_.sem, 1)
                dve.wait_ge(*d_(len(steps)))
            link(dve.memset(ones[0:4], 1.0))
            for d in range(2):
                dve.wait_ge(*k.act_done(3 * (d + 1)))
                f = raw[0:4, 2 * d + 1, :]
                link(dve.scalar_tensor_tensor(f, f, 0.0, soft[0:4], ALU.min, ALU.subtract))
            for d in range(2):
                i, f, b, m = raw[0:4, 2 * d, :], raw[0:4, 2 * d + 1, :], run[0:4, d, :], top[0:4, d, :]
                if d == 0:
                    link(dve.tensor_tensor_scan(b, ones[0:4], f, 0.0, ALU.mult, ALU.add))
                else:
                    link(dve.tensor_tensor_scan(b[:, CTX - 1::-1], ones[0:4, :CTX], f[:, CTX - 1::-1], 0.0,
                                                ALU.mult, ALU.add))
                    link(dve.tensor_tensor_scan(b[:, TOK - 1:CTX - 1:-1], ones[0:4, CTX:], f[:, TOK - 1:CTX - 1:-1],
                                                b[:, 0:1], ALU.mult, ALU.add))
                link(dve.tensor_tensor(i, i, b, ALU.subtract))
                if d == 0:
                    link(dve.tensor_tensor_scan(m, i, i, -3.0e38, ALU.max, ALU.max))
                else:
                    link(dve.tensor_tensor_scan(m[:, CTX - 1::-1], i[:, CTX - 1::-1], i[:, CTX - 1::-1], -3.0e38,
                                                ALU.max, ALU.max))
                    link(dve.tensor_tensor_scan(m[:, TOK - 1:CTX - 1:-1], i[:, TOK - 1:CTX - 1:-1],
                                                i[:, TOK - 1:CTX - 1:-1], m[:, 0:1], ALU.max, ALU.max))
                link(dve.tensor_tensor(b, b, m, ALU.add))
                link(dve.tensor_scalar(b, b, -80.0, None, ALU.max))
    k.act_done.counted(6)
    d_.counted(len(steps))
    with k.nc.Block() as block:
        @block.tensor
        def _(pe):
            for d in range(2):
                for c in range(NCH):
                    mm = pe.transpose(B[0][:, (d * NCH + c) * 4:(d * NCH + c + 1) * 4],
                                      raw[0:4, 2 * d, c * P:(c + 1) * P], k.ident[0:4, 0:4])
            mm.then_inc(k.pe_done.sem, 1)

        @block.scalar
        def _(act):
            for d in range(2):
                act.activation(run[0:4, d, :], run[0:4, d, :], ACT.Exp, scale=-1.0)

        @block.vector
        def _(dve):
            dve.wait_ge(*k.pe_done(1))
            dve.tensor_copy(a_t.rearrange("p d c h -> p (d c h)"), B[0][:, :48])
    k.pe_done.counted(1)

    units = [(h, d) for h in range(HEADS2) for d in range(2)]
    spread, negated, clipped, weighed, scored, probed, summed, absolute, finished = k.more[0:9]

    def span(j, d):
        if j < 2:
            return 0, 512, None
        t = j - 2
        return (t * P, 512, t * P) if d == 0 else (0, (t + 1) * P, t * P)
    with k.nc.Block() as block:
        @block.tensor
        def _(pe):
            def sums(pe, n, h, d, j):
                lo, hi, _ = span(j, d)
                pe.wait_ge(*probed(6 * n + j + 1))
                pe.matmul(B[4][:, lo:hi], val[:, 1, j, h * P:(h + 1) * P], prob[:, j % 2, lo:hi],
                          start=j == 0, stop=j == NCH - 1)
                pe.matmul(B[5][:, lo:hi], k.mean[:, 3, :], prob[:, j % 2, lo:hi],
                          start=j == 0, stop=j == NCH - 1).then_inc(summed.sem, 1)
            for n, (h, d) in enumerate(units):
                if n:
                    pe.wait_ge(*finished(n))
                pe.matmul(B[0][:, :], k.sel[0:4, h, :], top[0:4, d, CTX:], start=True, stop=True)
                pe.matmul(B[1][:, :], k.sel[0:4, h, :], run[0:4, d, CTX:], start=True, stop=True
                          ).then_inc(spread.sem, 1)
                r = slice(64 * (h % 2), 64 * (h % 2) + 64)
                for j in range(NCH):
                    lo, hi, _ = span(j, d)
                    if 6 * n + j >= 2:
                        pe.wait_ge(*probed(6 * n + j - 1))
                    pe.matmul(B[2 + j % 2][:, lo:hi], mk[r, h // 2, j * P:(j + 1) * P], mq[r, h // 2, lo:hi],
                              start=True, stop=True).then_inc(scored.sem, 1)
                    if j:
                        sums(pe, n, h, d, j - 1)
                sums(pe, n, h, d, NCH - 1)

        @block.scalar
        def _(act):
            for n, (h, d) in enumerate(units):
                act.wait_ge(*spread(n + 1))
                if n:
                    act.wait_ge(*weighed(6 * n))
                    act.wait_ge(*clipped(4 * n))
                act.activation(negm[:, :], B[0][:, :], ACT.Copy, scale=-1.0).then_inc(negated.sem, 1)
                act.wait_ge(*negated(n + 1))
                for j in range(NCH):
                    lo, hi, dg = span(j, d)
                    if 6 * n + j >= 2 and dg is None:
                        act.wait_ge(*probed(6 * n + j - 1))
                    bias = a_t[:, d, j, h:h + 1]
                    w = wts[:, j % 2, :]
                    if dg is None:
                        act.activation(w, negm[:, :], ACT.Exp, bias=bias).then_inc(weighed.sem, 1)
                        continue
                    act.wait_ge(*clipped(4 * n + j - 1))
                    rest = (dg + P, hi) if d == 0 else (lo, dg)
                    if rest[1] > rest[0]:
                        act.activation(w[:, rest[0]:rest[1]], negm[:, rest[0]:rest[1]], ACT.Exp, bias=bias)
                    act.activation(w[:, dg:dg + P], w[:, dg:dg + P], ACT.Exp).then_inc(weighed.sem, 1)
                act.wait_ge(*summed(6 * (n + 1)))
                if n:
                    act.wait_ge(*finished(n))
                act.activation(absd, B[5][:, :], ACT.Abs).then_inc(absolute.sem, 1)

        @block.vector
        def _(dve):
            chain = []

            def link(ins):
                chain.append(1)
                ins.then_inc(d_.sem, 1)
                dve.wait_ge(*d_(len(chain)))
            for n, (h, d) in enumerate(units):
                dve.wait_ge(*negated(n + 1))
                for j in range(NCH):
                    lo, hi, dg = span(j, d)
                    w, p = wts[:, j % 2, :], prob[:, j % 2, :]
                    if 6 * n + j >= 2:
                        dve.wait_ge(*probed(6 * n + j - 1))
                    if dg is not None:
                        dve.tensor_scalar(w[:, dg:dg + P], negm[:, dg:dg + P], a_t[:, d, j, h:h + 1], 0.0,
                                          ALU.add, ALU.min).then_inc(clipped.sem, 1)
                    dve.wait_ge(*scored(6 * n + j + 1))
                    dve.wait_ge(*weighed(6 * n + j + 1))
                    if 6 * n + j >= 2:
                        dve.wait_ge(*summed(6 * n + j - 1))
                    ins = dve.scalar_tensor_tensor(p[:, lo:hi], B[2 + j % 2][:, lo:hi], 0.125, w[:, lo:hi],
                                                   ALU.mult, ALU.mult)
                    if dg is not None:
                        link(ins)
                        ins = dve.tensor_tensor(p[:, dg:dg + P], p[:, dg:dg + P], k.tri[:, d, :], ALU.mult)
                    ins.then_inc(probed.sem, 1)
                dve.wait_ge(*absolute(n + 1))
                link(dve.tensor_tensor(absd, absd, B[1][:, :], ALU.max))
                link(dve.reciprocal(absd, absd))
                o = out[:, 4 + h, :]
                if d == 0:
                    dve.tensor_tensor(o, B[4][:, :], absd, ALU.mult).then_inc(finished.sem, 1)
                else:
                    link(dve.tensor_tensor(part, B[4][:, :], absd, ALU.mult))
                    dve.tensor_tensor(o, o, part, ALU.add).then_inc(finished.sem, 1)
            steps[:] = chain
    n = len(units)
    for s, m in ((spread, n), (negated, n), (clipped, 4 * n), (weighed, 6 * n), (scored, 6 * n), (probed, 6 * n),
                 (summed, 6 * n), (absolute, n), (finished, n), (d_, len(steps))):
        s.counted(m)


def stage_second_inputs(k):
    qg = view(k, M2_QG, 8, 512)
    fpre = view(k, M2_F, 8, TOK)
    val = k.arena[:, M2_V:M2_V + 2 * NCH * 512].rearrange("p (s t e) -> p s t e", s=2, t=NCH)

    def qg_evict(act, i, u):
        for g in range(2):
            ins = act.activation(flat(qg[:, bass.ds(4 * i + (2 * u + g), 1), :]), k.bank[4 * u + g][:, :], ACT.Silu)
        ins.then_inc(k.evicted.sem, 1)

    def f_evict(act, i, u):
        for g in range(2):
            for c, (a, b) in enumerate(chunks_both()):
                ins = act.activation(flat(fpre[:, bass.ds(4 * i + (2 * u + g), 1), a:b]),
                                     k.bank[4 * u + 2 * g + c][:, :b - a], ACT.Copy)
        ins.then_inc(k.evicted.sem, 1)
    linear(k, k.streams["w_qg2"], lambda kk, c: k.H[:, kk, LAT:], [(0, 512)], qg_evict, then=k.streams["w_f2"])
    linear(k, k.streams["w_f2"], lambda kk, c: k.H[:, kk, slice(*chunks_both()[c])], chunks_both(), f_evict,
           then=k.streams["w_v2"])
    stage_token_values(k, k.streams["w_v2"], k.ap["w_v2"], 2, NCH, 0, lambda s, t: val[:, s, t, :])


def block_two(k):
    ap, st = k.ap, k.streams
    both = chunks_both()

    def modulated(weight, m, which, first=None):
        stage_gains(k, k.v(weight, 0, 8), [k.mod2[:, m + 8:m + 16, w] for w in which])
        for w in which:
            a, b = both[1 - w]
            whole, parts = ((lambda j: k.H[:, j, a:b]), None) if first is None else norm_parts(k, a, b, first)
            norm(k, lambda j: k.X[:, j, a:b], whole, DT, a, b, 0, RMS_EPS, False,
                 lambda j: k.gain[:, w, j:j + 1], shift=lambda j: k.mod2[:, m + j:m + j + 1, w], parts=parts)
    kept = stage_modulation(k, st["w_mod"], 2, lambda kk, which: k.v("cc2", 2 * kk + which), st["ffn1_w1", 0])
    halves = kept.rearrange("p (t h) -> p t h", h=2)
    with k.nc.Block() as block:
        @block.tensor
        def _(pe):
            for w in range(2):
                own = slice(64 * w, 64 * w + 64)
                for h in range(2):
                    pe.matmul(k.bank[w][64 * h:64 * h + 64, :72], k.ident[own, own], halves[own, :, h],
                              start=True, stop=True).then_inc(k.pe_done.sem, 1)

        @block.vector
        def _(dve):
            for w in range(2):
                dve.wait_ge(*k.pe_done(2 * w + 2))
                dve.tensor_tensor(k.mod2[:, :, w], k.bank[w][:, :72],
                                  k.v("b_mod", 0, 144).rearrange("p (t w) -> p t w", w=2)[:, :, w], ALU.add)
    k.pe_done.counted(4)
    modulated("norm1", 0, (0, 1), 0)
    stage_half_gates(k, [k.mod2[:, 16:24, 1], k.mod2[:, 16:24, 0]])
    stage_ffn(k, "ffn1_w1", "ffn1_w2", both, swiglu(both), lambda n, c: k.gain[:, c, bass.ds(n, 1)], 1.0,
              st["w_qg2"])
    modulated("norm2", 24, (0, 1))
    stage_second_inputs(k)
    stage_hgrn(k)
    stage_head_norms(k, 0, "hg_norm", view(k, M2_QG + 4 * 512, 4, 512))
    stage_mlstm_inputs(k)
    stage_mlstm(k)
    stage_head_norms(k, 4, "ml_norm", view(k, ML_O, 4, 512))
    out = view(k, M2_OUT, 8, 512)
    run(k, [residual(k, st["w_out2"], lambda kk, c: out[:, kk, :], [(LAT, TOK)],
                     lambda n, c: k.mod2[:, bass.ds(40 + n, 1), 0], 1.0, st["ffn2_w1", 0])])
    modulated("norm3", 48, (0,), LAT)
    stage_half_gates(k, [k.mod2[:, 64:72, 0]])
    stage_ffn(k, "ffn2_w1", "ffn2_w2", [(LAT, TOK)], swiglu([(LAT, TOK)]),
              lambda n, c: k.gain[:, 0, bass.ds(n, 1)], 1.0, st["w_r3"])
    norm(k, x_lat(k), x_lat(k), DT, LAT, TOK, 0, RMS_EPS, False, lambda j: k.v("fnorm2", j))


T3 = META + SEQ
M0 = LAT - META
QB = 5
HEADS3, TOPK = 8, SEQ // 4
MASKED = -1.0e38
PICKED = -3.0e38
WIDTH = [min(P * (b + 1), T3) for b in range(QB)]
ROWS = [min(P, T3 - P * b) for b in range(QB)]
BIAS_AT = [sum(WIDTH[:b]) for b in range(QB)]
A3_R = 0
A3_V = A3_R + 16 * T3
A3_OUT = A3_V + QB * 512
A3_MISC = A3_OUT + 8 * T3
A3_BIAS = A3_MISC + T3
A3_S = A3_BIAS + sum(WIDTH)
A3_PT = A3_S + 3 * T3
A3_SC = A3_PT + 2 * QB * P
A3_RB = A3_SC + T3
A3_KM = A3_SC
CHUNKS3 = [(M0, M0 + T3 // 2), (M0 + T3 // 2, TOK)]


def banks_of(width):
    return [(0, min(width, 512))] + ([(512, width)] if width > 512 else [])


def stage_third_inputs(k):
    r = view(k, A3_R, 16, T3)
    misc = k.arena[:, A3_MISC:A3_MISC + T3]
    v = k.arena[:, A3_V:A3_V + QB * 512].rearrange("p (t e) -> p t e", e=512)

    def act_evict(act, i, u):
        for g in range(2):
            for c, (a, b) in enumerate(CHUNKS3):
                ins = act.activation(flat(r[:, bass.ds(4 * i + (2 * u + g), 1), a - M0:b - M0]),
                                     k.bank[4 * u + 2 * g + c][:, :b - a], ACT.Copy)
        ins.then_inc(k.evicted.sem, 1)
    linear(k, k.streams["w_r3"], lambda kk, c: k.H[:, kk, slice(*CHUNKS3[c])], CHUNKS3, act_evict)
    stage_token_values(k, None, k.ap["w_vs"], 1, QB, M0, lambda s, t: v[:, t, :], ROWS[-1])
    with k.nc.Block() as block:
        @block.sync
        def _(sp):
            sp.dma_start(k.W[0][:, :DT * P], k.ap["w_misc"]).then_inc(k.weights_in[0].sem, 16)

        @block.tensor
        def _(pe):
            pe.wait_ge(*k.weights_in[0](16))
            for c, (a, b) in enumerate(CHUNKS3):
                for kk in range(DT):
                    mm = pe.matmul(k.bank[c][:, :b - a], k.W[0][:, kk * P:(kk + 1) * P], k.H[:, kk, a:b],
                                   start=kk == 0, stop=kk == DT - 1)
            mm.then_inc(k.pe_done.sem, 1)

        @block.scalar
        def _(act):
            act.wait_ge(*k.pe_done(1))
            for c, (a, b) in enumerate(CHUNKS3):
                act.activation(misc[:, a - M0:b - M0], k.bank[c][:, :b - a], ACT.Copy)
    k.weights_in[0].counted(16)
    k.pe_done.counted(1)


def stage_rope3(k, tiles, rows, rot, cos, sin):
    tmp = k.arena[:, A3_S:A3_S + 2 * T3].rearrange("p (a t) -> p a t", t=T3)
    half = T3 // 2
    n = len(tiles)
    turned, swapped = k.more[0:2]
    with k.nc.Block() as block:
        @block.tensor
        def _(pe):
            for j, x in enumerate(tiles):
                if j >= 2:
                    pe.wait_ge(*swapped(j - 1))
                for c in range(2):
                    mm = pe.matmul(k.bank[2 * (j % 2) + c][:rows, :half], rot, x[:, c * half:(c + 1) * half],
                                   start=True, stop=True)
                mm.then_inc(turned.sem, 1)

        @block.vector
        def _(dve):
            for j, x in enumerate(tiles):
                t = tmp[:rows, j % 2, :]
                dve.wait_ge(*turned(j + 1))
                if j >= 2:
                    dve.wait_ge(*k.dve_done(2 * (j - 1)))
                for c in range(2):
                    ins = dve.tensor_tensor(t[:, c * half:(c + 1) * half], k.bank[2 * (j % 2) + c][:rows, :half],
                                            sin[:, c * half:(c + 1) * half], ALU.mult)
                ins.then_inc(swapped.sem, 1)
                dve.tensor_tensor(x, x, cos, ALU.mult).then_inc(k.dve_done.sem, 1)
                dve.wait_ge(*swapped(j + 1))
                dve.wait_ge(*k.dve_done(2 * j + 1))
                dve.tensor_tensor(x, x, t, ALU.add).then_inc(k.dve_done.sem, 1)
    for s, m in ((turned, n), (swapped, n), (k.dve_done, 2 * n)):
        s.counted(m)


def stage_selection(k):
    r = view(k, A3_R, 16, T3)
    misc = k.arena[:, A3_MISC:A3_MISC + T3]
    bias = k.arena[:, A3_BIAS:A3_BIAS + sum(WIDTH)]
    score = k.arena[:, A3_SC:A3_SC + T3]
    relus = view(k, A3_RB, 2, T3)
    w_i = k.rstd[:, 0:QB * 8].rearrange("p (b h) -> p b h", h=8)
    top = k.rstd[:, 64:72]
    weighted, scored, rectified, added = k.more[0:4]
    B = k.bank
    units = [(b, h) for b in range(1, QB) for h in range(8)]
    with k.nc.Block() as block:
        @block.tensor
        def _(pe):
            for b in range(QB):
                mm = pe.transpose(B[7][:ROWS[b], 8 * b:8 * b + 8], misc[0:8, b * P:b * P + ROWS[b]], k.ident[0:8, 0:8])
            mm.then_inc(weighted.sem, 1)
            for n, (b, h) in enumerate(units):
                rows = slice(64 * (h % 2), 64 * (h % 2) + 64)
                if n >= 2:
                    pe.wait_ge(*rectified(n - 1))
                for c, (lo, hi) in enumerate(banks_of(WIDTH[b])):
                    mm = pe.matmul(B[2 * (n % 2) + c][:ROWS[b], :hi - lo], r[rows, 8 + h // 2, b * P:b * P + ROWS[b]],
                                   r[rows, 12, lo:hi], start=True, stop=True)
                mm.then_inc(scored.sem, 1)

        @block.scalar
        def _(act):
            for n, (b, h) in enumerate(units):
                act.wait_ge(*scored(n + 1))
                if n >= 2:
                    act.wait_ge(*added(n - 1))
                for c, (lo, hi) in enumerate(banks_of(WIDTH[b])):
                    ins = act.activation(relus[:ROWS[b], n % 2, lo:hi], B[2 * (n % 2) + c][:ROWS[b], :hi - lo],
                                         ACT.Relu, scale=0.125)
                ins.then_inc(rectified.sem, 1)

        @block.vector
        def _(dve):
            chain = []

            def link(ins):
                chain.append(1)
                ins.then_inc(k.dve_done.sem, 1)
                dve.wait_ge(*k.dve_done(len(chain)))
            dve.wait_ge(*weighted(1))
            for b in range(QB):
                link(dve.tensor_scalar(w_i[:ROWS[b], b, :], B[7][:ROWS[b], 8 * b:8 * b + 8], float(8 ** -0.5), None,
                                       ALU.mult))
            dve.tensor_copy(bias[:, 0:P], k.neg[:, :])
            for n, (b, h) in enumerate(units):
                s = score[:ROWS[b], :WIDTH[b]]
                x, w = relus[:ROWS[b], n % 2, :WIDTH[b]], w_i[:ROWS[b], b, h:h + 1]
                dve.wait_ge(*rectified(n + 1))
                if h == 0:
                    ins = dve.tensor_scalar(s, x, w, None, ALU.mult)
                else:
                    ins = dve.scalar_tensor_tensor(s, x, w, s, ALU.mult, ALU.add)
                ins.then_inc(added.sem, 1)
                dve.wait_ge(*added(n + 1))
                if h < 7:
                    continue
                q, diag = ROWS[b], slice(b * P, WIDTH[b])
                nd = WIDTH[b] - b * P
                link(dve.tensor_tensor(s[:, diag], s[:, diag], k.neg[:q, :nd], ALU.add))
                for _round in range(TOPK // 8):
                    link(dve.max(top[:q], s))
                    link(dve.match_replace(s, top[:q], s, PICKED))
                out = bias[:q, BIAS_AT[b]:BIAS_AT[b] + WIDTH[b]]
                link(dve.tensor_scalar(out, s, 2.0 * MASKED, -1.0e30, ALU.is_gt, ALU.mult))
                link(dve.tensor_tensor(out[:, diag], out[:, diag], k.neg[:q, :nd], ALU.add))
            weighted.chain = len(chain)
    n = len(units)
    for s, m in ((weighted, 1), (scored, n), (rectified, n), (added, n), (k.dve_done, weighted.chain)):
        s.counted(m)


def stage_attention(k, query, keyf, value, bias, scale, first_tile):
    out = view(k, A3_OUT, 8, T3)
    s_buf = view(k, A3_S, 3, T3)
    p_t = k.arena[:, A3_PT:A3_PT + 2 * QB * P].rearrange("p (a t q) -> p a t q", a=2, q=P)
    top, total = k.rstd[:, 0:4], k.rstd[:, 8:12]
    scored, biased, exped, normed, turned, moved, summed, kept = k.more[0:8]
    B = k.bank
    units = [(b, h) for b in range(QB) for h in range(HEADS3)]
    N = len(units)
    with k.nc.Block() as block:
        @block.tensor
        def _(pe):
            for i in range(N + 3):
                if i < N:
                    n, (b, h) = i, units[i]
                    if n >= 2:
                        pe.wait_ge(*biased(n - 1))
                    for c, (lo, hi) in enumerate(banks_of(WIDTH[b])):
                        mm = pe.matmul(B[2 * (n % 2) + c][:ROWS[b], :hi - lo], query(h, b * P, b * P + ROWS[b]),
                                       keyf(h, lo, hi), start=True, stop=True)
                    mm.then_inc(scored.sem, 1)
                if 2 <= i < N + 2:
                    n, (b, h) = i - 2, units[i - 2]
                    pe.wait_ge(*normed(n + 1))
                    if n:
                        pe.wait_ge(*moved(n))
                    for t in range(b + 1):
                        kr = ROWS[t]
                        mm = pe.transpose(B[4 + t // 4][:kr, (t % 4) * P:(t % 4) * P + ROWS[b]],
                                          s_buf[:ROWS[b], n % 3, t * P:t * P + kr], k.ident[:ROWS[b], :ROWS[b]])
                    mm.then_inc(turned.sem, 1)
                if i >= 3:
                    n, (b, h) = i - 3, units[i - 3]
                    pe.wait_ge(*moved(n + 1))
                    if n >= 2:
                        pe.wait_ge(*kept(n - 1))
                    r = slice(64 * (h % 2), 64 * (h % 2) + 64)
                    for t in range(b + 1):
                        mm = pe.matmul(B[6 + n % 2][r, :ROWS[b]], value(h, t)[:ROWS[t]],
                                       p_t[:ROWS[t], n % 2, t, :ROWS[b]], start=t == 0, stop=t == b)
                    mm.then_inc(summed.sem, 1)

        @block.scalar
        def _(act):
            for i in range(N + 3):
                if 2 <= i < N + 2:
                    n, (b, h) = i - 2, units[i - 2]
                    act.wait_ge(*turned(n + 1))
                    if n >= 2:
                        act.wait_ge(*summed(n - 1))
                    full = min(b + 1, 4)
                    ins = act.activation(p_t[:, n % 2, :full, :ROWS[b]],
                                         B[4][:, :full * P].rearrange("p (t q) -> p t q", q=P)[:, :, :ROWS[b]], ACT.Copy)
                    if b == 4:
                        ins = act.activation(p_t[:ROWS[4], n % 2, 4, :ROWS[b]], B[5][:ROWS[4], :ROWS[b]], ACT.Copy)
                    ins.then_inc(moved.sem, 1)
                if i < N:
                    n, (b, h) = i, units[i]
                    s = s_buf[:ROWS[b], n % 3, :WIDTH[b]]
                    act.wait_ge(*biased(n + 1))
                    act.activation(s, s, ACT.Exp, bias=top[:ROWS[b], n % 4:n % 4 + 1],
                                   accum_out=total[:ROWS[b], n % 4:n % 4 + 1]).then_inc(exped.sem, 1)
                if i >= 3:
                    n, (b, h) = i - 3, units[i - 3]
                    act.wait_ge(*summed(n + 1))
                    r = slice(64 * (h % 2), 64 * (h % 2) + 64)
                    act.activation(out[r, first_tile + h // 2, b * P:b * P + ROWS[b]], B[6 + n % 2][r, :ROWS[b]],
                                   ACT.Copy).then_inc(kept.sem, 1)

        @block.vector
        def _(dve):
            d = k.dve_done
            for i in range(N + 1):
                if i < N:
                    n, (b, h) = i, units[i]
                    s = s_buf[:ROWS[b], n % 3, :WIDTH[b]]
                    dve.wait_ge(*scored(n + 1))
                    if n >= 3:
                        dve.wait_ge(*turned(n - 2))
                    for c, (lo, hi) in enumerate(banks_of(WIDTH[b])):
                        ins = dve.scalar_tensor_tensor(s[:, lo:hi], B[2 * (n % 2) + c][:ROWS[b], :hi - lo], scale,
                                                       bias(b)[:ROWS[b], lo:hi], ALU.mult, ALU.add)
                    ins.then_inc(d.sem, 1)
                    dve.wait_ge(*d(max(2 * n, 1)))
                    dve.tensor_reduce(top[:ROWS[b], n % 4:n % 4 + 1], s, AX.X, ALU.max, negate=True
                                      ).then_inc(biased.sem, 1)
                if i >= 1:
                    n, (b, h) = i - 1, units[i - 1]
                    s, one = s_buf[:ROWS[b], n % 3, :WIDTH[b]], total[:ROWS[b], n % 4:n % 4 + 1]
                    dve.wait_ge(*exped(n + 1))
                    dve.reciprocal(one, one).then_inc(d.sem, 1)
                    dve.wait_ge(*d(2 * i + 1 if i < N else 2 * N))
                    dve.tensor_scalar(s, s, one, None, ALU.mult).then_inc(normed.sem, 1)
    for s in (scored, biased, exped, normed, turned, moved, summed, kept):
        s.counted(N)
    k.dve_done.counted(2 * N)


def stage_latent_projections(k, tables):
    r = view(k, A3_R, 16, T3)
    qm, km = view(k, A3_R, 8, T3), view(k, A3_KM, 8, T3)
    v = k.arena[:, A3_V:A3_V + QB * 512].rearrange("p (t e) -> p t e", e=512)
    misc = k.arena[:, A3_MISC:A3_MISC + T3]
    half = T3 // 2
    w_uq = k.W[0][:, 0:2 * 768].rearrange("p (k n) -> p k n", n=768)
    w_k, w_v = k.W[1][:, 0:512], k.W[1][:, 512:1024]
    outs = []
    for h in range(HEADS3):
        for c in range(2):
            outs.append(("q", h, c))
    for h in range(HEADS3):
        for c in range(2):
            outs.append(("k", h, c))
    for t in range(QB):
        outs.append(("v", t, 0))
    with k.nc.Block() as block:
        @block.sync
        def _(sp):
            sp.dma_start(k.W[0][:, 0:1536], k.ap["w_uq"]).then_inc(k.weights_in[0].sem, 16)
            sp.dma_start(k.W[1][:, 0:1024], k.ap["w_ukv"]).then_inc(k.weights_in[1].sem, 16)

        @block.tensor
        def _(pe):
            pe.wait_ge(*k.weights_in[0](16))
            pe.wait_ge(*k.weights_in[1](16))
            for n, (kind, h, c) in enumerate(outs):
                if n >= 8:
                    pe.wait_ge(*k.act_done(n - 7))
                cols = slice(c * half, (c + 1) * half)
                if kind == "q":
                    pe.matmul(k.bank[n % 8][:96, :half], w_uq[:, 0, 96 * h:96 * h + 96], r[:, 13, cols], start=True,
                              stop=False)
                    mm = pe.matmul(k.bank[n % 8][:96, :half], w_uq[:, 1, 96 * h:96 * h + 96], r[:, 14, cols],
                                   start=False, stop=True)
                elif kind == "k":
                    mm = pe.matmul(k.bank[n % 8][:64, :half], w_k[:, 64 * h:64 * h + 64], r[:, 15, cols],
                                   start=True, stop=True)
                else:
                    mm = pe.matmul(k.bank[n % 8][:ROWS[h], :], r[:, 15, h * P:h * P + ROWS[h]], w_v,
                                   start=True, stop=True)
                mm.then_inc(k.pe_done.sem, 1)

        @block.scalar
        def _(act):
            act.activation(km[64:96, 0, :], misc[64:96, :], ACT.Copy)
            for n, (kind, h, c) in enumerate(outs):
                act.wait_ge(*k.pe_done(n + 1))
                cols = slice(c * half, (c + 1) * half)
                if kind == "q":
                    dst, src = qm[:96, h, cols], k.bank[n % 8][:96, :half]
                elif kind == "k":
                    dst, src = km[:64, h, cols], k.bank[n % 8][:64, :half]
                else:
                    dst, src = v[:ROWS[h], h, :], k.bank[n % 8][:ROWS[h], :]
                act.activation(dst, src, ACT.Copy).then_inc(k.act_done.sem, 1)
    for u in range(2):
        k.weights_in[u].counted(16)
    k.pe_done.counted(len(outs))
    k.act_done.counted(len(outs))
    cos, sin = tables
    stage_rope3(k, [qm[:96, h, :] for h in range(8)] + [km[:96, 0, :]], 96, k.rot96[:96, :96], cos[:96], sin[:96])
    with k.nc.Block() as block:
        @block.scalar
        def _(act):
            for h in range(1, HEADS3):
                act.activation(km[64:96, h, :], km[64:96, 0, :], ACT.Copy)


def block_three(k):
    ap = k.ap
    tables = k.H[:, :, :].rearrange("p k t -> p (k t)")[:, :4 * T3].rearrange("p (a t) -> p a t", t=T3)
    r = view(k, A3_R, 16, T3)
    with k.nc.Block() as block:
        @block.sync
        def _(sp):
            sp.dma_start(k.X[:, :, M0:LAT], ap["meta_t"].rearrange("(k p) t -> p k t", p=P)).then_inc(k.loaded.sem, 16)
            sp.wait_ge(*k.loaded(16))
    k.loaded.counted(16)
    for a, b in CHUNKS3:
        norm(k, lambda j: k.X[:, j, a:b], lambda j: k.H[:, j, a:b], DT, a, b, 0, RMS_EPS, False,
             lambda j: k.v("attn_norm", j))
    stage_third_inputs(k)
    with k.nc.Block() as block:
        @block.sync
        def _(sp):
            sp.dma_start(tables, ap["rope3"]).then_inc(k.loaded.sem, 16)
            sp.dma_start(k.rot32, ap["rot32"]).then_inc(k.loaded.sem, 16)
            sp.dma_start(k.rot96, ap["rot96"]).then_inc(k.loaded.sem, 16)
            sp.wait_ge(*k.loaded(48))
    k.loaded.counted(48)
    stage_rope3(k, [r[:, j, :] for j in range(13)], P, k.rot32, tables[:, 0, :], tables[:, 1, :])
    stage_selection(k)
    v = k.arena[:, A3_V:A3_V + QB * 512].rearrange("p (t e) -> p t e", e=512)

    def pair(h):
        return slice(64 * (h % 2), 64 * (h % 2) + 64)
    stage_attention(k, lambda h, a, b: r[pair(h), h // 2, a:b], lambda h, a, b: r[pair(h), 4 + h // 2, a:b],
                    lambda h, t: v[:, t, h * 64:(h + 1) * 64],
                    lambda b: k.arena[:, A3_BIAS + BIAS_AT[b]:A3_BIAS + BIAS_AT[b] + WIDTH[b]], 0.125, 4)
    for c in range(2):
        cols = slice(c * (T3 // 2), (c + 1) * (T3 // 2))
        norm(k, lambda j: r[:, 13 + j, cols], lambda j: r[:, 13 + j, cols], 2, 0, T3 // 2, 1, RMS_EPS, False,
             lambda j: k.v("q_norm", j))
        norm(k, lambda j: r[:, 15, cols], lambda j: r[:, 15, cols], 1, 0, T3 // 2, 2, RMS_EPS, False,
             lambda j: k.v("kv_norm", j))
    stage_latent_projections(k, (tables[:, 2, :], tables[:, 3, :]))
    qm, km = view(k, A3_R, 8, T3), view(k, A3_KM, 8, T3)
    causal = k.arena[:, A3_BIAS:A3_BIAS + QB * P]
    with k.nc.Block() as block:
        @block.vector
        def _(dve):
            dve.memset(causal[:, :4 * P], 0.0)
            dve.tensor_copy(causal[:, 4 * P:], k.neg[:, :])
    stage_attention(k, lambda h, a, b: qm[:96, h, a:b], lambda h, a, b: km[:96, h, a:b],
                    lambda h, t: v[:, t, h * 64:(h + 1) * 64],
                    lambda b: causal[:, (4 - b) * P:(4 - b) * P + WIDTH[b]], float(96 ** -0.5), 0)
    out = view(k, A3_OUT, 8, T3)
    run(k, [residual(k, k.streams["w_o3"], lambda kk, c: out[:, kk, META:], [(LAT, TOK)], None, 1.0,
                     k.streams["w_gu3", 0])])
    whole, parts = norm_parts(k, LAT, TOK, LAT)
    norm(k, x_lat(k), whole, DT, LAT, TOK, 0, RMS_EPS, False, lambda j: k.v("ffn_norm", j), parts=parts)
    stage_ffn(k, "w_gu3", "w_down3", [(LAT, TOK)], swiglu([(LAT, TOK)]), None, 1.0, None)
    norm(k, x_lat(k), x_lat(k), DT, LAT, TOK, 0, RMS_EPS, False, lambda j: k.v("fnorm3", j))


def build(nc, ap, out):
    with ExitStack() as ctx:
        k = Core(nc, ctx, ap)
        stage_load(k)
        block_one(k)
        block_two(k)
        block_three(k)
        with nc.Block() as block:
            @block.sync
            def _(sp):
                sp.dma_start(out.rearrange("(k p) t -> p k t", p=P), k.X[:, :, LAT:]).then_inc(k.stored.sem, 16)
                sp.wait_ge(*k.stored(16))


def _columns(a, tiles):
    return a.reshape(tiles, 128).T


def _pack(w, groups, cols, order=None):
    kt = w.shape[0] // 128
    t = w.reshape(kt, 128, -1, 128)
    if order is not None:
        t = t[:, :, order, :]
    t = t.reshape(kt, 128, groups, cols).transpose(2, 1, 0, 3)
    return np.ascontiguousarray(t).reshape(groups, 128, kt * cols)


def _pieces(out, name, w, sizes, cols):
    at = 0
    for n, tiles in enumerate(sizes):
        out[f"{name}_{n}"] = _pack(w[at:at + 128 * tiles], 1024 // cols, cols)
        at += 128 * tiles


def _constants():
    c = {}
    c["ident"] = np.eye(128, dtype=np.float32)
    rot = np.zeros((128, 128), np.float32)
    for m in range(64):
        rot[m + 64, m] = -1.0
        rot[m, m + 64] = 1.0
    c["rot64"] = rot
    gamma = np.log(1.0 - 2.0 ** (-5.0 - np.arange(8)))
    rel = np.arange(512)[None, :] - np.arange(128)[:, None]
    c["decay"] = np.where(rel[None] >= 0, np.exp(gamma[:, None, None] * np.maximum(rel, 0)[None]), 0.0).astype(np.float32)
    s, t = np.arange(128)[:, None], np.arange(128)[None, :]
    masks = [s == t]
    for lev in range(7):
        m = 1 << lev
        same = s // (2 * m) == t // (2 * m)
        masks.append(same & ((s // m) % 2 == 0) & ((t // m) % 2 == 1))
    c["masks"] = np.stack(masks + [x.T for x in masks], 1).astype(np.int32).reshape(128, 2048)
    c["tri"] = np.stack([s <= t, s >= t], 1).astype(np.float32)
    sel = np.zeros((4, 4, 128), np.float32)
    for h in range(4):
        sel[h, h] = 1.0
    c["sel"] = sel
    c["neg"] = np.where(t > s, np.float32(-1.0e38), np.float32(0.0)).astype(np.float32)

    def swap(starts, half):
        r = np.zeros((128, 128), np.float32)
        for a in starts:
            for m in range(half):
                r[a + m + half, a + m] = -1.0
                r[a + m, a + m + half] = 1.0
        return r
    c["rot32"], c["rot96"] = swap((0, 64), 32), swap((64,), 16)
    tables = np.zeros((128, 4, 528), np.float32)
    pos = np.arange(528, dtype=np.float32)

    def angles(half):
        inv = np.power(np.float32(10000.0), -np.arange(half, dtype=np.float32) / np.float32(half)).astype(np.float32)
        return inv[:, None] * pos[None, :]
    for a in range(0, 128, 32):
        tables[a:a + 32, 0], tables[a:a + 32, 1] = np.cos(angles(32)), np.sin(angles(32))
    tables[:64, 2] = 1.0
    for a in (64, 80):
        tables[a:a + 16, 2], tables[a:a + 16, 3] = np.cos(angles(16)), np.sin(angles(16))
    c["rope3"] = tables
    return c
def _inputs_one(a):
    out = {}
    out["x_t"] = np.ascontiguousarray(a["x"][0].T)
    out["ctx_t"] = np.ascontiguousarray(a["ctx_2"][0].T)
    out["positions_b"] = np.ascontiguousarray(np.broadcast_to(a["positions"], (128, 512)))
    out["w_ada"] = _pack(a["w_ada"][0], 12, 512)
    w = a["w_in"][0]
    b = a["b_in"][0]
    at = np.cumsum([0, 1024, 1024, 2048, 2048, 1024, 1024, 1024, 1024])
    parts = [w[:, at[j]:at[j + 1]] for j in range(8)]
    bias = [b[at[j]:at[j + 1]] for j in range(8)]
    pairs = [t for j in range(8) for t in (j, 8 + j)]
    out["w_cpair"] = _pack(np.concatenate([parts[4], parts[5]], 1), 8, 256, pairs)
    out["w_qk"] = _pack(np.concatenate([parts[0], parts[1]], 1), 8, 256, pairs)
    out["w_v"] = _pack(parts[2], 4, 512)
    out["b_v"] = np.ascontiguousarray(bias[2][None])
    out["w_g"] = _pack(parts[3], 8, 256)
    out["w_ga"] = _pack(parts[6], 4, 256)
    out["w_gb"] = _pack(parts[7], 4, 256)
    out["w_conv_out"] = _pack(a["w_conv_out"][0], 4, 256)
    out["w_ret_out"] = _pack(a["w_ret_out"][0], 4, 256)
    out["w_out"] = _pack(a["w_out"][0], 4, 256)
    ffp = [t for j in range(22) for t in (j, 22 + j)]
    out["w_up"] = _pack(a["w_up"][0], 22, 256, ffp)
    _pieces(out, "w_down", a["w_down"][0], (12, 10), 128)
    v = {}
    v["c"] = _columns(a["c"][0], 8)
    v["b_ada"] = _columns(a["b_ada"][0], 48)
    v["b_cval"], v["b_cgate"] = _columns(bias[4], 8), _columns(bias[5], 8)
    v["b_qk"] = _columns(np.concatenate([bias[0], bias[1]]), 16)[:, pairs]
    v["b_g"], v["b_ga"], v["b_gb"] = _columns(bias[3], 16), _columns(bias[6], 8), _columns(bias[7], 8)
    v["conv_w"] = a["conv_dw_w"][0].reshape(31, 8, 128).transpose(2, 1, 0).reshape(128, 248)
    v["conv_b"] = _columns(a["conv_dw_b"][0], 8)
    v["cln_g"], v["cln_b"] = _columns(a["conv_ln_g"][0], 8), _columns(a["conv_ln_b"][0], 8)
    v["gn_g"], v["gn_b"] = _columns(a["ret_gn_g"][0], 16), _columns(a["ret_gn_b"][0], 16)
    v["ln1_g"], v["ln1_b"] = _columns(a["ln1_g"][0], 8), _columns(a["ln1_b"][0], 8)
    v["ffn_w"] = a["ffn_dw_w"][0].reshape(3, 44, 128).transpose(2, 1, 0)[:, ffp, :].reshape(128, 132)
    v["ffn_b"] = _columns(a["ffn_dw_b"][0], 44)[:, ffp]
    v["ln2_g"], v["ln2_b"] = _columns(a["ln2_g"][0], 8), _columns(a["ln2_b"][0], 8)
    half = np.arange(64, dtype=np.float32)
    freq = np.float32(10000.0) ** (-half / np.float32(64))
    v["inv_freq"] = np.concatenate([freq, freq])[:, None].astype(np.float32)
    return out, v


def _inputs_two(a):
    out, v = {}, {}
    out["w_mod"] = _pack(a["w_mod_2"][0], 18, 512)
    pairs = [t for j in range(22) for t in (j, 22 + j)]
    for n in ("ffn1", "ffn2"):
        out[n + "_w1"] = _pack(a[n + "_w1_2"][0], 22, 256, pairs)
    _pieces(out, "ffn1_w2", a["ffn1_w2_2"][0], (8, 8, 6), 256)
    _pieces(out, "ffn2_w2", a["ffn2_w2_2"][0], (12, 10), 128)
    w = a["w_in_2"][0]
    out["w_qg2"] = _pack(np.concatenate([w[:, 0:512], w[:, 1024:1536]], 1), 4, 256)
    out["w_f2"] = _pack(w[:, 1536:2560], 4, 256, [0, 4, 1, 5, 2, 6, 3, 7])
    out["w_v2"] = _pack(np.concatenate([w[:, 512:1024], w[:, 3072:3584]], 1), 2, 512)
    out["w_mqk"] = _pack(w[:, 2560:3072], 2, 256)
    out["w_mo"] = _pack(w[:, 3584:4096], 2, 256)
    gates = np.zeros((1024, 128), np.float32)
    gb = np.zeros((128, 1), np.float32)
    for g in range(4):
        gates[:, 32 * g:32 * g + 4] = w[:, 4096 + 4 * g:4100 + 4 * g]
        gb[32 * g:32 * g + 4, 0] = a["ml_gate_b_2"][0, 4 * g:4 * g + 4]
    out["w_gates"] = _pack(gates, 1, 128)[0]
    out["w_out2"] = _pack(a["w_out_2"][0], 4, 256)
    v["ml_gb"] = gb
    v["cc2"] = np.stack([_columns(a["c_2"][0], 8), _columns(a["c_ctx_2"], 8)], 2).reshape(128, 16)
    b = _columns(a["b_mod_2"][0], 72)
    v["b_mod"] = np.stack([b, b], 2).reshape(128, 144)
    for n in ("norm1", "norm2", "norm3"):
        v[n] = _columns(a[n + "_w_2"][0], 8)
    v["fnorm2"] = _columns(a["final_norm_w_2"], 8)
    v["mconv_w"] = a["ml_conv_w_2"][0].reshape(9, 4, 128).transpose(2, 1, 0).reshape(128, 36)
    v["mconv_b"] = _columns(a["ml_conv_b_2"][0], 4)
    lb = a["hg_lb_logits_2"]
    v["lb0"], v["lb1"] = _columns(lb[0].reshape(-1), 8), _columns(lb[1].reshape(-1), 8)
    v["hg_norm"], v["ml_norm"] = _columns(a["hg_norm_w_2"][0], 4), _columns(a["ml_norm_w_2"][0], 4)
    return out, v


def _inputs_three(a):
    out, v = {}, {}
    out["meta_t"] = np.ascontiguousarray(a["meta_tokens_3"].T)
    w = a["w_in_3"][0]
    cq, ckv, kr = w[:, 0:256], w[:, 256:384], w[:, 384:416]
    qs, ks, vs, qi, ki, wi = (w[:, 416:928], w[:, 928:1440], w[:, 1440:1952], w[:, 1952:2464], w[:, 2464:2528],
                              w[:, 2528:2536])
    out["w_r3"] = _pack(np.concatenate([qs, ks, qi, ki, ki, cq, ckv], 1), 8, 256)
    out["w_vs"] = _pack(vs, 1, 512)
    misc = np.zeros((1024, 128), np.float32)
    misc[:, 0:8] = wi
    misc[:, 64:96] = kr
    out["w_misc"] = _pack(misc, 1, 128)[0]
    out["w_uq"] = np.ascontiguousarray(a["w_uq_3"][0].reshape(2, 128, 768).transpose(1, 0, 2)).reshape(128, 1536)
    out["w_ukv"] = np.ascontiguousarray(
        a["w_ukv_3"][0].reshape(128, 8, 2, 64).transpose(0, 2, 1, 3)).reshape(128, 1024)
    out["w_o3"] = _pack(a["w_o_3"][0], 4, 256)
    pairs = [t for j in range(22) for t in (j, 22 + j)]
    out["w_gu3"] = _pack(np.concatenate([a["w_gate_3"][0], a["w_up_3"][0]], 1), 22, 256, pairs)
    _pieces(out, "w_down3", a["w_down_3"][0], (12, 10), 128)
    v["attn_norm"], v["ffn_norm"] = _columns(a["attn_norm_g_3"][0], 8), _columns(a["ffn_norm_g_3"][0], 8)
    v["q_norm"], v["kv_norm"] = _columns(a["mla_q_norm_g_3"][0], 2), _columns(a["mla_kv_norm_g_3"][0], 1)
    v["fnorm3"] = _columns(a["final_norm_g_3"], 8)
    return out, v


def _arrays(inputs):
    a = {n: np.asarray(x) for n, x in inputs.items()}
    arrays, vecs = _constants(), {}
    for part in (_inputs_one, _inputs_two, _inputs_three):
        out, v = part(a)
        arrays.update(out)
        vecs.update(v)
    arrays["vecs"] = np.ascontiguousarray(np.concatenate([vecs[n] for n in VEC_SIZES], 1))
    return arrays


def kernel(**inputs):
    import concourse.bacc as bacc
    from concourse.bass_utils import run_bass_kernel_spmd

    nc = bacc.Bacc("TRN2", target_bir_lowering=False, num_devices=1)
    arrays = _arrays(inputs)
    ap = {n: nc.dram_tensor("in_" + n, x.shape, mybir.dt.from_np(x.dtype), kind="ExternalInput").ap()
          for n, x in arrays.items()}
    out = nc.dram_tensor("out_t", (D, SEQ), F32, kind="ExternalOutput").ap()
    build(nc, ap, out)
    r = run_bass_kernel_spmd(nc, [{"in_" + n: x for n, x in arrays.items()}], core_ids=[0])
    return np.ascontiguousarray(r.results[0]["out_t"].T)[None]
```
